# Optimizing a Trainium2 kernel written in Bass

```python
import numpy as np
import jax
import jax.numpy as jnp
from jax import lax

D_MODEL = 1024
BATCH = 1
SEQ = 1024
DEPTH = 1
DEC_BATCH = 8
DEC_SEQ = 4
PAST_LEN = 512
PAGE_SIZE = 128

N_BRANCH = 4
BRANCH_W = D_MODEL // 4
H_A = 4
HD_A = BRANCH_W // H_A
Q_BLOCK = 128
SB_BIAS_INIT = -8.0
H_B = 4
DK_B = BRANCH_W // H_B
DV_B = BRANCH_W // H_B
CHUNK_B = 64
W_C = BRANCH_W
H_C = 4
CONV_C = 4
RG_C = 8.0
W_D = BRANCH_W
POOL_WINDOWS = (2, 4, 8, 16)
POOL_G = len(POOL_WINDOWS)
POOL_HIST = max(POOL_WINDOWS) - 1
D_FF = 2816
CONV_F = 3
D_PLE = 256
EPS = 1e-6
IN_SIZES = (BRANCH_W,) * 10 + (N_BRANCH * D_MODEL,)
F32 = jnp.float32

kernel_name = 'hybrid_sb_hgrn2_rglru_pool_decoder_step'

def rmsnorm(x, g):
    xf = x.astype(F32)
    y = xf * lax.rsqrt(jnp.mean(xf * xf, axis=-1, keepdims=True) + EPS)
    return (y * g.astype(F32)).astype(x.dtype)

def causal_dwconv(hist, x, w, b):
    width = w.shape[0]
    L = x.shape[1]
    ext = jnp.concatenate([hist.astype(x.dtype), x], axis=1)
    y = b + ext[:, 0:L] * w[0]
    for j in range(1, width):
        y = y + ext[:, j:j + L] * w[j]
    return y, ext[:, L:]

def sb_block(q, k, v, q_pos, k_pos, bias):
    z = jnp.einsum('bqhd,bkhd->bhqk', q, k) * (HD_A ** -0.5) + bias[None, :, None, None]
    mask = k_pos[None, :] < q_pos[:, None]
    log_keep = jnp.where(mask, jax.nn.log_sigmoid(-z), 0.0)
    later = lax.cumsum(log_keep, axis=3, reverse=True) - log_keep
    w = jnp.where(mask, jnp.exp(jax.nn.log_sigmoid(z) + later), 0.0)
    return jnp.einsum('bhqk,bkhd->bqhd', w, v)

def stick_breaking(q, k, v, pos0, bias):
    B, L, H, D = q.shape
    k_pos = jnp.arange(k.shape[1])
    q_pos = pos0 + jnp.arange(L)
    blk = Q_BLOCK if L % Q_BLOCK == 0 else L
    nb = L // blk
    kf, vf = k.astype(F32), v.astype(F32)
    bf = bias.astype(F32)
    qb = q.astype(F32).reshape(B, nb, blk, H, D).transpose(1, 0, 2, 3, 4)
    pb = q_pos.reshape(nb, blk)
    o = lax.map(lambda a: sb_block(a[0], kf, vf, a[1], k_pos, bf), (qb, pb))
    return o.transpose(1, 0, 2, 3, 4).reshape(B, L, H, D)

def gla_chunk_scan(q, k, v, log_f, S0, chunk):
    B, L, H, _ = q.shape
    DV = v.shape[-1]
    n = L // chunk

    def to_chunks(a):
        return a.reshape(B, n, chunk, H, a.shape[-1]).transpose(1, 0, 3, 2, 4)

    causal = jnp.tril(jnp.ones((chunk, chunk), dtype=bool))

    def step(S, inp):
        qc, kc, vc, lfc = inp
        b = jnp.cumsum(lfc, axis=2)
        diff = jnp.where(causal[None, None, :, :, None],
                         b[:, :, :, None, :] - b[:, :, None, :, :], -jnp.inf)
        att = jnp.einsum('bhtk,bhsk,bhtsk->bhts', qc, kc, jnp.exp(diff))
        o = jnp.einsum('bhts,bhsv->bhtv', att, vc) + jnp.einsum('bhtk,bhkv->bhtv', qc * jnp.exp(b), S)
        b_last = b[:, :, -1:, :]
        S_new = jnp.exp(b_last[:, :, 0, :])[..., None] * S + jnp.einsum(
            'bhsk,bhsv->bhkv', kc * jnp.exp(b_last - b), vc)
        return S_new, o

    S, o = lax.scan(step, S0, (to_chunks(q), to_chunks(k), to_chunks(v), to_chunks(log_f)))
    return o.transpose(1, 0, 3, 2, 4).reshape(B, L, H, DV), S

def hgrn2(qb, fb, ib, gb, S0, lp):
    B, L, _ = qb.shape
    lb = lp['lb']
    fr = fb.astype(F32)
    log_f = jnp.logaddexp(jnp.log(lb), jnp.log1p(-lb) + jax.nn.log_sigmoid(fr))
    kb = (1.0 - lb) * jax.nn.sigmoid(-fr)
    qh = jax.nn.silu(qb.astype(F32))
    to_h = lambda a: a.reshape(B, L, H_B, -1)
    chunk = CHUNK_B if L % CHUNK_B == 0 else L
    o, S = gla_chunk_scan(to_h(qh), to_h(kb), to_h(ib.astype(F32)), to_h(log_f), S0.astype(F32), chunk)
    o = rmsnorm(o, lp['hgrn_norm']).reshape(B, L, BRANCH_W) * jax.nn.silu(gb.astype(F32))
    return o, S

def rg_lru(xc, gc, conv_hist, h0, lp):
    xconv, conv_new = causal_dwconv(conv_hist, xc, lp['conv_c_w'], lp['conv_c_b'])
    xf = xconv.astype(F32)
    B, L, C = xf.shape
    xh = xf.reshape(B, L, H_C, C // H_C)
    r = jax.nn.sigmoid(jnp.einsum('blhi,hij->blhj', xh, lp['w_rg_a'].astype(F32)).reshape(B, L, C) + lp['b_rg_a'])
    ig = jax.nn.sigmoid(jnp.einsum('blhi,hij->blhj', xh, lp['w_rg_x'].astype(F32)).reshape(B, L, C) + lp['b_rg_x'])
    log_a = -RG_C * r * jax.nn.softplus(-lp['lam'].astype(F32))
    a = jnp.exp(log_a)
    u = jnp.sqrt(-jnp.expm1(2.0 * log_a)) * (ig * xf)

    def step(h, au):
        h = au[0] * h + au[1]
        return h, h

    hT, hs = lax.scan(step, h0.astype(F32), (a.transpose(1, 0, 2), u.transpose(1, 0, 2)))
    y = hs.transpose(1, 0, 2) * jax.nn.gelu(gc.astype(F32))
    return y, hT, conv_new

def pool_mixer(xd, hist, pos0, lp):
    B, L, C = xd.shape
    ext_raw = jnp.concatenate([hist.astype(xd.dtype), xd], axis=1)
    ext = ext_raw.astype(F32)
    cs = jnp.concatenate([jnp.zeros((B, 1, C), F32), jnp.cumsum(ext, axis=1)], axis=1)
    pos = pos0 + jnp.arange(L)
    gc = C // POOL_G
    start = POOL_HIST + 1
    pooled = []
    for g, w in enumerate(POOL_WINDOWS):
        sl = slice(g * gc, (g + 1) * gc)
        s = cs[:, start:start + L, sl] - cs[:, start - w:start - w + L, sl]
        cnt = jnp.minimum(pos + 1, w).astype(F32)[None, :, None]
        pooled.append(s / cnt)
    diff = jnp.concatenate(pooled, axis=-1) - ext[:, POOL_HIST:]
    y = jnp.einsum('blgi,gij->blgj', diff.reshape(B, L, POOL_G, gc), lp['w_pool'].astype(F32)).reshape(B, L, C)
    return y * lp['pool_scale'], ext_raw[:, L:]

def trunk_layer(x, pe, pos0, k_past, v_past, S0, h0, conv_c_hist, pool_hist, ffn_hist, lp):
    B, L, _ = x.shape
    dt = x.dtype
    h = rmsnorm(x, lp['norm_mix'])
    z = h @ lp['w_in']
    split_at = [int(s) for s in np.cumsum(IN_SIZES)[:-1]]
    qa, ka, va, qb, fb, ib, gb, xc, gc, xd, gl = jnp.split(z, split_at, axis=-1)
    qa = rmsnorm(qa.reshape(B, L, H_A, HD_A), lp['q_norm'])
    ka = rmsnorm(ka.reshape(B, L, H_A, HD_A), lp['k_norm'])
    va = va.reshape(B, L, H_A, HD_A)
    if k_past is None:
        k_all, v_all = ka, va
    else:
        k_all = jnp.concatenate([k_past.astype(dt), ka], axis=1)
        v_all = jnp.concatenate([v_past.astype(dt), va], axis=1)
    o_a = stick_breaking(qa, k_all, v_all, pos0, lp['sb_bias']).reshape(B, L, BRANCH_W)
    o_b, S_new = hgrn2(qb, fb, ib, gb, S0, lp)
    o_c, h_new, conv_c_new = rg_lru(xc, gc, conv_c_hist, h0, lp)
    o_d, pool_new = pool_mixer(xd, pool_hist, pos0, lp)
    branches = jnp.stack([o_a.astype(dt), o_b.astype(dt), o_c.astype(dt), o_d.astype(dt)], axis=2)
    proj = jnp.einsum('blnc,ncd->blnd', branches, lp['w_branch'])
    gates = jax.nn.sigmoid(gl.reshape(B, L, N_BRANCH, D_MODEL))
    x = x + jnp.sum(gates * proj, axis=2) @ lp['w_out']
    u = rmsnorm(x, lp['norm_ffn']) @ lp['w_up']
    u, ffn_new = causal_dwconv(ffn_hist, u, lp['conv_f_w'], lp['conv_f_b'])
    ua, ub = jnp.split(u, 2, axis=-1)
    x = x + (jax.nn.gelu(ua) * ub) @ lp['w_down']
    x = x + jax.nn.sigmoid(rmsnorm(x, lp['norm_ple']) @ lp['w_ple_gate']) * (pe.astype(dt) @ lp['w_ple'])
    return x, (ka, va, S_new, h_new, conv_c_new, pool_new, ffn_new)

def setup_inputs(seed: int = 0) -> dict:
    key = jax.random.key(seed)
    k = jax.random.split(key, 40)
    nrm = lambda kk, shape, scale=1.0: scale * jax.random.normal(kk, shape, F32)
    n_pages = PAST_LEN // PAGE_SIZE
    n_used = DEC_BATCH * n_pages
    n_pool = n_used + n_used // 4
    n_in = sum(IN_SIZES)
    page_table = jax.random.permutation(k[9], n_pool)[:n_used].reshape(DEC_BATCH, n_pages).astype(jnp.int32)
    a0 = jax.random.uniform(k[24], (DEPTH, W_C), F32, 0.9, 0.999)
    gc = W_D // POOL_G
    return {
        'x_prompt': nrm(k[0], (BATCH, SEQ, D_MODEL)),
        'x_sample': nrm(k[1], (DEC_BATCH, DEC_SEQ, D_MODEL)),
        'cache_k': nrm(k[2], (DEPTH, n_pool, PAGE_SIZE, H_A, HD_A)),
        'cache_v': nrm(k[3], (DEPTH, n_pool, PAGE_SIZE, H_A, HD_A)),
        'state_hgrn': nrm(k[4], (DEPTH, DEC_BATCH, H_B, DK_B, DV_B), 0.3),
        'state_rglru_h': nrm(k[5], (DEPTH, DEC_BATCH, W_C), 0.5),
        'state_rglru_conv': nrm(k[6], (DEPTH, DEC_BATCH, CONV_C - 1, W_C)),
        'state_pool': nrm(k[7], (DEPTH, DEC_BATCH, POOL_HIST, W_D)),
        'state_ffn_conv': nrm(k[8], (DEPTH, DEC_BATCH, CONV_F - 1, 2 * D_FF)),
        'page_table': page_table,
        'p_prompt': nrm(k[10], (DEPTH, BATCH, SEQ, D_PLE)),
        'p_sample': nrm(k[11], (DEPTH, DEC_BATCH, DEC_SEQ, D_PLE)),
        'norm_mix': 1.0 + nrm(k[12], (DEPTH, D_MODEL), 0.05),
        'w_in': nrm(k[13], (DEPTH, D_MODEL, n_in), D_MODEL ** -0.5),
        'q_norm': 1.0 + nrm(k[14], (DEPTH, HD_A), 0.05),
        'k_norm': 1.0 + nrm(k[15], (DEPTH, HD_A), 0.05),
        'sb_bias': SB_BIAS_INIT + nrm(k[37], (DEPTH, H_A), 0.1),
        'lb_logits': nrm(k[16], (DEPTH, H_B * DK_B), 0.5),
        'hgrn_norm': 1.0 + nrm(k[17], (DEPTH, DV_B), 0.05),
        'conv_c_w': nrm(k[18], (DEPTH, CONV_C, W_C), CONV_C ** -0.5),
        'conv_c_b': nrm(k[19], (DEPTH, W_C), 0.01),
        'w_rg_a': nrm(k[20], (DEPTH, H_C, W_C // H_C, W_C // H_C), (W_C // H_C) ** -0.5),
        'b_rg_a': nrm(k[21], (DEPTH, W_C), 0.01),
        'w_rg_x': nrm(k[22], (DEPTH, H_C, W_C // H_C, W_C // H_C), (W_C // H_C) ** -0.5),
        'b_rg_x': nrm(k[23], (DEPTH, W_C), 0.01),
        'lam': jnp.log(a0) - jnp.log1p(-a0),
        'w_pool': nrm(k[25], (DEPTH, POOL_G, gc, gc), gc ** -0.5),
        'pool_scale': 1.0 + nrm(k[26], (DEPTH, W_D), 0.05),
        'w_branch': nrm(k[27], (DEPTH, N_BRANCH, BRANCH_W, D_MODEL), BRANCH_W ** -0.5),
        'w_out': nrm(k[28], (DEPTH, D_MODEL, D_MODEL), D_MODEL ** -0.5),
        'norm_ffn': 1.0 + nrm(k[29], (DEPTH, D_MODEL), 0.05),
        'w_up': nrm(k[30], (DEPTH, D_MODEL, 2 * D_FF), D_MODEL ** -0.5),
        'conv_f_w': nrm(k[31], (DEPTH, CONV_F, 2 * D_FF), CONV_F ** -0.5),
        'conv_f_b': nrm(k[32], (DEPTH, 2 * D_FF), 0.01),
        'w_down': nrm(k[33], (DEPTH, D_FF, D_MODEL), D_FF ** -0.5),
        'norm_ple': 1.0 + nrm(k[34], (DEPTH, D_MODEL), 0.05),
        'w_ple_gate': nrm(k[35], (DEPTH, D_MODEL, D_MODEL), D_MODEL ** -0.5),
        'w_ple': nrm(k[36], (DEPTH, D_PLE, D_MODEL), D_PLE ** -0.5),
    }

def reference(x_prompt, x_sample, cache_k, cache_v, state_hgrn, state_rglru_h, state_rglru_conv,
              state_pool, state_ffn_conv, page_table, p_prompt, p_sample,
              norm_mix, w_in, q_norm, k_norm, sb_bias, lb_logits, hgrn_norm, conv_c_w, conv_c_b,
              w_rg_a, b_rg_a, w_rg_x, b_rg_x, lam, w_pool, pool_scale, w_branch, w_out,
              norm_ffn, w_up, conv_f_w, conv_f_b, w_down, norm_ple, w_ple_gate, w_ple):
    lb_all = jnp.cumsum(jax.nn.softmax(lb_logits.astype(F32), axis=0), axis=0)
    lb_all = lb_all - lb_all[:1]
    B = x_prompt.shape[0]
    DB = x_sample.shape[0]
    dt = x_prompt.dtype
    S0_p = jnp.zeros((B, H_B, DK_B, DV_B), F32)
    h0_p = jnp.zeros((B, W_C), F32)
    convc_p = jnp.zeros((B, CONV_C - 1, W_C), dt)
    pool_p = jnp.zeros((B, POOL_HIST, W_D), dt)
    ffn_p = jnp.zeros((B, CONV_F - 1, 2 * D_FF), dt)
    xp, xs = x_prompt, x_sample
    outs_p, outs_s = [], []
    for i in range(DEPTH):
        lp = {'norm_mix': norm_mix[i], 'w_in': w_in[i], 'q_norm': q_norm[i], 'k_norm': k_norm[i],
              'sb_bias': sb_bias[i],
              'lb': lb_all[i], 'hgrn_norm': hgrn_norm[i], 'conv_c_w': conv_c_w[i], 'conv_c_b': conv_c_b[i],
              'w_rg_a': w_rg_a[i], 'b_rg_a': b_rg_a[i], 'w_rg_x': w_rg_x[i], 'b_rg_x': b_rg_x[i],
              'lam': lam[i], 'w_pool': w_pool[i], 'pool_scale': pool_scale[i], 'w_branch': w_branch[i],
              'w_out': w_out[i], 'norm_ffn': norm_ffn[i], 'w_up': w_up[i], 'conv_f_w': conv_f_w[i],
              'conv_f_b': conv_f_b[i], 'w_down': w_down[i], 'norm_ple': norm_ple[i],
              'w_ple_gate': w_ple_gate[i], 'w_ple': w_ple[i]}
        xp, sp = trunk_layer(xp, p_prompt[i], 0, None, None, S0_p, h0_p, convc_p, pool_p, ffn_p, lp)
        k_past = cache_k[i][page_table].reshape(DB, -1, H_A, HD_A)
        v_past = cache_v[i][page_table].reshape(DB, -1, H_A, HD_A)
        xs, ss = trunk_layer(xs, p_sample[i], k_past.shape[1], k_past, v_past, state_hgrn[i],
                             state_rglru_h[i], state_rglru_conv[i], state_pool[i], state_ffn_conv[i], lp)
        outs_p.append(sp)
        outs_s.append(ss)
    stk = lambda outs, j: jnp.stack([o[j] for o in outs], axis=0)
    return (xp, xs,
            stk(outs_p, 0), stk(outs_p, 1), stk(outs_s, 0), stk(outs_s, 1),
            stk(outs_p, 2), stk(outs_s, 2),
            stk(outs_p, 3), stk(outs_s, 3),
            stk(outs_p, 4), stk(outs_s, 4),
            stk(outs_p, 5), stk(outs_s, 5),
            stk(outs_p, 6), stk(outs_s, 6))


_drawn_inputs = setup_inputs


def setup_inputs(seed=0):
    import zlib

    import numpy as np

    out = dict(_drawn_inputs(seed))
    spreads = {}
    factors = {'cache_k': 8.0,
     'cache_v': 6.347,
     'q_norm': 8.0,
     'sb_bias': 8.0,
     'hgrn_norm': 3.906,
     'b_rg_a': 21.721,
     'b_rg_x': 8.0,
     'pool_scale': 2.913,
     'conv_f_b': 8.0,
     'norm_ple': 28.985}
    for name, (base, spread) in spreads.items():
        noise = np.random.default_rng([zlib.crc32(name.encode()), seed]).standard_normal(out[name].shape)
        drawn = base * np.exp(spread * noise) if base else spread * noise
        out[name] = jnp.asarray(drawn.astype(out[name].dtype))
    for name, factor in factors.items():
        out[name] = (out[name] * factor).astype(out[name].dtype)
    return out
```

```python
from contextlib import ExitStack

import numpy as np

import concourse.bass as bass
from concourse import mybir

F32 = mybir.dt.float32
I32 = mybir.dt.int32
ALU = mybir.AluOpType
ACT = mybir.ActivationFunctionType
ds = bass.ds

P = 128
D = 1024
SEQ = 1024
DB, DL = 8, 4
NS = DB * DL
T = SEQ + NS
KD = D // P
HW = D // 4
HD = 64
NH = 4
PAGES = 4
PAST = PAGES * P
FF = 2816
NF = FF // P
DPLE = 256
KP = DPLE // P
EPS = 1e-6
CH = 128
NCH = SEQ // CH
SPANS = ((0, 512), (512, 512), (1024, NS))
HIST = 15
EXT = HIST + SEQ + DB * (HIST + DL)
XC, FB, QB, KA, XD, GC, GB, QA = range(0, 16, 2)
Z_COLS = (1792, 1024, 768, 256, 2304, 2048, 1536, 0)
BRANCH_AT = (QA, GB, GC, XD)
LEVELS = (64, 32, 16, 8, 4, 2, 1)
NL = len(LEVELS) + 1


def table(*entries):
    at, n = {}, 0
    for name, width in entries:
        at[name] = n
        n += width
    return at, n


PAR, NPAR = table(("norm_mix", KD), ("norm_ffn", KD), ("norm_ple", KD), ("conv_c_w", 8), ("conv_c_b", 2),
                  ("b_rg_a", 2), ("b_rg_x", 2), ("lam", 2), ("pool_scale", 2), ("q_norm", 1), ("k_norm", 1),
                  ("hgrn_norm", 1), ("sb_head", NH), ("sb_row", 1))
CON, NCON = table(("ident", P), ("mean", P), ("headmean", P), ("bd", P), ("strict", P), ("notstrict", P),
                  ("newkeys", NS), ("notnewkeys", NS), ("invw", 2), ("corr", 2 * HIST), ("batch", DB))
NR = 23500
EARLY = 3
LATE = 8 - EARLY
PART = T // 3
UNITS = 4 * EARLY
PLACES = (("start0", 4), ("states0", 3), ("levels0", 3), ("start1", 2), ("states1", 3), ("levels1", 3),
          ("norms", 1), ("normed", 2), ("steps", 8), ("samples", 7))


def parts(place):
    first = 0
    for name, n in PLACES:
        if name == place:
            return range(first, first + n)
        first += n
    assert False, place


assert sum(n for _, n in PLACES) == 3 * UNITS


class Link:

    def __init__(self, eng, sem):
        self.eng, self.sem, self.base, self.n = eng, sem, 0, 0

    def __call__(self, *inss):
        for ins in inss:
            ins.then_inc(self.sem, 1)
            self.n += 1
        self.eng.wait_ge(self.sem, self.base + self.n)

    def rounds(self, times, body):
        first = self.n
        body(0)
        per = self.n - first
        with self.eng.Fori(1, times) as i:
            self.base, self.n = i * per, first
            body(i)
            assert self.n == first + per
        self.base, self.n = 0, first + times * per


def rounds(eng, times, body):
    body(0)
    with eng.Fori(1, times) as i:
        body(i)


def wait_prior(eng, sem, value):
    if not isinstance(value, int) or value > 0:
        eng.wait_ge(sem, value)


def program(nc, a, o):
    with ExitStack() as ctx:
        def sb(name, shape, dt=F32):
            return ctx.enter_context(nc.sbuf_tensor(name, shape, dt))

        sems = {}

        def S(name):
            if name not in sems:
                sems[name] = ctx.enter_context(nc.semaphore(name))
            return sems[name]

        par = sb("par", [P, NPAR])
        con = sb("con", [P, NCON])
        masks = sb("masks", [P, NL, P], I32)
        smasks = sb("smasks", [NS, 3, NS], I32)
        fpar = sb("fpar", [P, NF, 8])
        small = sb("small", [P, 96])
        H = sb("H", [P, KD, T])
        BIG = sb("BIG", [P, 16 * T + NR])
        FH = sb("FH", [P, NF, 2, DB, 2])
        FO = sb("FO", [P, NF, 2, 18])
        Z = BIG[:, 0:16 * T].rearrange("p (c t) -> p c t", c=16)
        R0 = 16 * T
        ps = [ctx.enter_context(nc.psum_tensor(f"ps{s}", [P, 1536], F32)) for s in range(2)]
        pst = [ctx.enter_context(nc.psum_tensor(f"pst{s}", [P, 512], F32)) for s in range(2)]
        gbank = ps[1][:, 1024:1024 + PART]
        gates = nc.dram_tensor("gates", (UNITS, P, T), F32, kind="Internal").ap()

        def pc(name, j=0, n=1):
            return par[:, PAR[name] + j:PAR[name] + j + n]

        def cc(name, n=P, j=0, p=P):
            return con[0:p, CON[name] + j:CON[name] + j + n]

        class Region:

            def __init__(self, at=0):
                self.at = R0 + at

            def take(self, *shape):
                n = 1
                for s in shape:
                    n *= s
                v = BIG[:, self.at:self.at + n]
                self.at += n
                assert self.at <= R0 + NR, self.at - R0
                names = "abcd"[:len(shape)]
                if len(shape) > 1:
                    v = v.rearrange(f"p ({' '.join(names)}) -> p {' '.join(names)}",
                                    **{x: s for x, s in zip(names, shape)})
                return v

        r = Region()
        VT = r.take(NCH + 1, 512)
        base = r.at - R0
        zw = r.take(2, KD, P)
        wvi = r.take(KD, 512)
        wrg = r.take(2, 2, P)
        wpool = r.take(2, P)
        chist = r.take(2, DB, 3)
        ch0 = r.take(2, DB)
        at = r.at - R0
        SS, RS, SQ = r.take(T), r.take(T), r.take(2, T)
        r = Region(at)
        cX, cR, cI = r.take(2, T), r.take(2, T), r.take(2, T)
        cA, cB = r.take(T), r.take(T)
        cext = r.take(DB, 7)
        dE, dF = r.take(EXT), r.take(EXT)
        xin = Z[:, 8:16, :]
        r = Region(base)
        bB = r.take(2, T)
        KF, QF = r.take(2, T), [r.take(2, T), r.take(2, T)]
        QE = r.take(T)
        kdt = Region(r.at - R0).take(NCH + 1, P)
        att = r.take(NCH, 2, P)
        atts = r.take(2, NS)
        Sall = r.take(NCH + 1, P)
        S0 = r.take(2, DB, P)
        vbd = r.take(DB, P)
        bdec = r.take(16)
        assert r.at <= R0 + NR - 2 * KD * P - 2 * PART
        tA = Z[:, XC:XC + 2, :]
        bd_, bE = Z[:, XC, :], Z[:, XC + 1, :]
        rmask = QE
        r = Region(NR - 2 * KD * P - 2 * PART)
        gw = r.take(2, KD, P)
        gstage = r.take(2, PART)
        r = Region(base)
        keep, beta, Pp = r.take(2, SEQ), r.take(2, SEQ), r.take(2, SEQ + 8)
        wT = r.take(2, SEQ)
        QS = r.take(2, 1152)
        QSall = r.take(2, P)
        kp = r.take(2, PAGES, 2, P)
        vp = r.take(2, PAGES, HW)
        negb = r.take(8)
        assert r.at <= R0 + NR - 2 * KD * P - 2 * PART
        qm = Z[:, FB:FB + 4, :]
        r = Region()
        MIX = r.take(KD, T)
        at = r.at - R0
        mwg = r.take(LATE, KD, P)
        early = r.take(EARLY, T)
        mwb = r.take(2, 4, 2, P)
        SIG = r.take(2, T)
        ACC, TMP = r.take(T), r.take(T)
        X = Z[:, 0:KD, :]
        r = Region(at)
        ow = r.take(2, KD, P)
        nSQ, nSS, nRS = r.take(T), r.take(T), r.take(T)
        G = BIG[:, 8 * T:(8 + NF) * T].rearrange("p (c t) -> p c t", c=NF)
        r = Region(14 * T)
        uw = r.take(2, 2, KD, P)
        V = r.take(2, T)
        VB = r.take(T)
        r = Region(14 * T)
        dw = r.take(2, NF, P)
        dSQ, dSS, dRS = r.take(T), r.take(T), H[:, 0, :]
        r = Region()
        pw = r.take(2, KD, P)
        pv = r.take(2, KP, P)
        pe_ = r.take(KP, T)
        sigp = r.take(2, T)
        yout = r.take(2, T)


        def m_slot(u):
            return u % 2 if u < EARLY else 1

        block = ctx.enter_context(nc.Block())

        @block.sync
        def _(sp):
            sp.dma_start(par[:], a["par"]).then_inc(S("params_in"), 16)
            sp.dma_start(con[:], a["con"]).then_inc(S("params_in"), 16)
            for k in range(KD):
                sp.dma_start(xin[:, k, :], a["x"][k]).then_inc(S(f"x_in{k // 2}"), 16)
            for s in range(2):
                sp.dma_start(zw[:, s], a["wz"][s]).then_inc(S(f"zw_in{s}"), 16)
            sp.dma_start(wrg, a["wrg"]).then_inc(S("cd_in"), 16)
            sp.dma_start(wpool, a["wpool"]).then_inc(S("cd_in"), 16)
            sp.dma_start(chist, a["chist"]).then_inc(S("cd_in"), 16)
            sp.dma_start(ch0, a["ch0"]).then_inc(S("cd_in"), 16)
            sp.dma_start(wvi, a["wvi"]).then_inc(S("wvi_in"), 16)
            sp.dma_start(masks[:], a["masks"]).then_inc(S("masks_in"), 16)
            sp.dma_start(smasks[:], a["smasks"]).then_inc(S("masks_in"), 16)
            sp.dma_start(fpar[:], a["fpar"]).then_inc(S("fpar_in"), 16)
            sp.dma_start(FH[:], a["fhist"]).then_inc(S("fpar_in"), 16)

            with sp.Fori(1, 8) as i:
                for s in range(2):
                    sp.wait_ge(S(f"z_done{s}"), i)
                    sp.dma_start(zw[:, s], a["wz"][ds(i * 2 + s, 1)].rearrange("o p k m -> (o p) k m"))\
                        .then_inc(S(f"zw_in{s}"), 16)
            outs = 0

            def out(name, src, idx=None):
                nonlocal outs
                dst = o[name] if idx is None else o[name][idx]
                sp.dma_start(dst, src).then_inc(S("stored"), 16)
                outs += 16

            sp.wait_ge(S("z_out"), 16)
            out("convc_p", Z[:, XC:XC + 2, SEQ - 3:SEQ])
            for i in range(2):
                out("convc_s", Z[:, XC + i, SEQ:T].rearrange("p (b t) -> p b t", b=DB)[:, :, 1:4], i)
                sp.dma_start(o["pool_s"][i][:, :, HIST - DL:], Z[:, XD + i, SEQ:T].rearrange("p (b t) -> p b t", b=DB))\
                    .then_inc(S("stored"), 16)
                sp.dma_start(o["pool_s"][i][:, :, 0:HIST - DL], a["phist"][i][:, :, DL:]).then_inc(S("stored"), 16)
                outs += 32
            out("pool_p", Z[:, XD:XD + 2, SEQ - HIST:SEQ])
            sp.wait_ge(S("stored"), outs)
            sp.sem_inc(S("raw_stored"), 1)
            sp.wait_ge(S("vt_free"), NCH + 1)
            out("v_p", VT[:, 0:NCH, 0:HW])
            out("v_s", VT[0:NS, NCH, 0:HW])
            sp.wait_ge(S("c_scanned"), 2)
            sp.wait_ge(S("c_out"), 2)
            out("h_p", small[:, 40:42])
            out("h_s", small[:, 48:64].rearrange("p (i b) -> p i b", i=2))
            sp.wait_ge(S("cd_over"), 1)
            sp.dma_start(S0[:], a["s0"]).then_inc(S("s0_in"), 16)
            for i in range(2):
                sp.wait_ge(S("b_states"), i + 1)
                out("hgrn_p", Sall[:, NCH, :], i)
                out("hgrn_s", vbd, i)
                sp.wait_ge(S("stored"), outs)
                sp.sem_inc(S("states_stored"), 1)
            sp.wait_ge(S("a_kq"), 2)
            out("k_cm", Z[:, KA:KA + 2, :])
            sp.wait_ge(S("b_over"), 2)
            for kind, buf, used in (("ck", kp, "kp_used"), ("cv", vp, "vp_used")):
                for b in range(DB):
                    if b >= 2:
                        sp.wait_ge(S(used), b - 1)
                    for g in range(PAGES):
                        page = sp.value_load(a["pt"][b:b + 1, g:g + 1], min_val=0, max_val=39)
                        if kind == "ck":
                            sp.dma_start(buf[:, b % 2, g], a["ck"][ds(page, 1)].rearrange("o p i t -> (o p) i t"))\
                                .then_inc(S(f"kp_in{b % 2}"), 16)
                        else:
                            sp.dma_start(buf[:, b % 2, g], a["cv"][ds(page, 1)].rearrange("o p c -> (o p) c"))\
                                .then_inc(S(f"vp_in{b % 2}"), 16)

            sp.wait_ge(S("a_over"), 2)
            sp.wait_ge(S("stored"), outs)
            for s in range(2):
                sp.wait_ge(S(f"gate_stored{s}"), 16 * 3 * UNITS // 2)

            def pieces(x):
                return x.rearrange("o p n k m -> (o p) n k m")
            sp.dma_start(mwb[:, 0], a["wb"][0]).then_inc(S("mw_in0"), 16)
            sp.dma_start(early, gates[0:EARLY].rearrange("n p t -> p n t")).then_inc(S("mw_in0"), 16)
            sp.dma_start(mwg[:, 0:2], a["wgl"][0][:, 0:2]).then_inc(S("mw_in1"), 16)
            sp.dma_start(mwb[:, 1], a["wb"][1]).then_inc(S("mw_in1"), 16)
            sp.dma_start(mwg[:, 2:LATE], a["wgl"][0][:, 2:LATE]).then_inc(S("mw_in2"), 16)
            for k in range(KD):
                sp.dma_start(X[:, k, :], a["x"][k]).then_inc(S("x_again"), 16)
            with sp.Fori(1, 4) as i:
                sp.wait_ge(S("m_proj"), i * 8 - 4)
                sp.dma_start(mwb[:, 0], pieces(a["wb"][ds(i * 2, 1)])).then_inc(S("mw_in0"), 16)
                sp.wait_ge(S("m_sig"), i * 8 + (EARLY - 8))
                sp.dma_start(early, gates[ds(i * EARLY, EARLY)].rearrange("n p t -> p n t")).then_inc(S("mw_in0"), 16)
                sp.wait_ge(S("m_gate"), i * LATE + (2 - LATE))
                sp.dma_start(mwg[:, 0:2], pieces(a["wgl"][ds(i, 1), :, 0:2])).then_inc(S("mw_in1"), 16)
                sp.wait_ge(S("m_gate"), i * LATE)
                sp.dma_start(mwg[:, 2:LATE], pieces(a["wgl"][ds(i, 1), :, 2:LATE])).then_inc(S("mw_in2"), 16)
                sp.wait_ge(S("m_proj"), i * 8)
                sp.dma_start(mwb[:, 1], pieces(a["wb"][ds(i * 2 + 1, 1)])).then_inc(S("mw_in1"), 16)

            def ring(times, buf, src, tag, before, gate):
                for q in range(2):
                    sp.wait_ge(*gate)
                    sp.dma_start(buf[:, q], src[q]).then_inc(S(f"{tag}w_in{q}"), 16)
                with sp.Fori(1, times) as i:
                    for q in range(2):
                        sp.wait_ge(S(f"{tag}_done{q}"), i + before)
                        sp.dma_start(buf[:, q], src[ds(i * 2 + q, 1)].rearrange(
                            "o p k m -> (o p) k m" if len(src.shape) == 4 else "o p h k m -> (o p) h k m"))\
                            .then_inc(S(f"{tag}w_in{q}"), 16)

            ring(4, ow, a["wo"], "r", 0, (S("mix_ready"), 8))
            ring(11, uw, a["wu"], "u", 0, (S("mix_ready"), 8))
            ring(4, dw, a["wd"], "r", 4, (S("g_ready"), NF))
            sp.wait_ge(S("r_added"), 16)
            out("ffn_out", FO[:])
            for k in range(KP):
                sp.dma_start(pe_[:, k, :], a["pe"][k]).then_inc(S("pe_in"), 16)
            for q in range(2):
                sp.dma_start(pw[:, q], a["wpg"][q]).then_inc(S(f"pw_in{q}"), 16)
                sp.dma_start(pv[:, q], a["wpl"][q]).then_inc(S(f"pw_in{q}"), 16)
            with sp.Fori(1, 4) as i:
                for q in range(2):
                    sp.wait_ge(S(f"p_done{q}"), i)
                    sp.dma_start(pw[:, q], a["wpg"][ds(i * 2 + q, 1)].rearrange("o p k m -> (o p) k m"))\
                        .then_inc(S(f"pw_in{q}"), 16)
                    sp.dma_start(pv[:, q], a["wpl"][ds(i * 2 + q, 1)].rearrange("o p k m -> (o p) k m"))\
                        .then_inc(S(f"pw_in{q}"), 16)
            sp.wait_ge(S("stored"), outs)
            sp.wait_ge(S("y_out0"), 64)
            sp.wait_ge(S("y_out1"), 64)

        @block.tensor
        def _(pe):
            def dense(out, w, rhs, kk, first=True, last=True):
                ins = None
                for k in range(kk):
                    for t0, n in SPANS:
                        ins = nc.tensor.matmul(out[:, t0:t0 + n], w[:, k], rhs[:, k, t0:t0 + n],
                                               start=first and k == 0, stop=last and k == kk - 1)
                return ins

            def whole(out, w, rhs):
                ins = None
                for t0, n in SPANS:
                    ins = nc.tensor.matmul(out[:, t0:t0 + n], w, rhs[:, t0:t0 + n], start=True, stop=True)
                return ins

            def gate(p, halves=(0, 1)):
                u, part = divmod(p, 3)
                if 0 in halves:
                    if part == 0:
                        pe.wait_ge(S(f"gw_in{u % 2}"), 16 * (u // 2 + 1))
                    if p:
                        pe.wait_ge(S("gate_out"), p)
                for k in range(4 * halves[0], 4 * halves[-1] + 4):
                    ins = nc.tensor.matmul(gbank, gw[:, u % 2, k], H[:, k, part * PART:part * PART + PART],
                                           start=(k == 0), stop=(k == KD - 1))
                if 1 in halves:
                    ins.then_inc(S("gate_done"), 1)

            pe.wait_ge(S("params_in"), 32)
            pe.wait_ge(S("n1_ss"), 8)
            whole(ps[0], cc("mean"), SS).then_inc(S("norm_sum"), 1)
            pe.wait_ge(S("n1_h"), 8)

            def z_round(i):
                for s in range(2):
                    pe.wait_ge(S(f"zw_in{s}"), i * 16 + 16)
                    wait_prior(pe, S(f"z_free{s}"), i)
                    dense(ps[s], zw[:, s], H, KD).then_inc(S(f"z_done{s}"), 1)
            rounds(pe, 8, z_round)

            pe.wait_ge(S("cd_in"), 64)
            for s in range(2):
                pe.wait_ge(S(f"z_free{s}"), 8)
            for u, (w, x, ready) in enumerate([(wrg[:, 0, 0], cX[:, 0], 1), (wrg[:, 0, 1], cX[:, 0], 1),
                                               (wrg[:, 1, 0], cX[:, 1], 2), (wrg[:, 1, 1], cX[:, 1], 2),
                                               (wpool[:, 0], Z[:, XD], 3), (wpool[:, 1], Z[:, XD + 1], 4)]):
                pe.wait_ge(S("cd_ready"), ready)
                if u >= 2:
                    pe.wait_ge(S("cd_free"), u - 1)
                whole(ps[u % 2], w, x).then_inc(S("cd_done"), 1)

            pe.wait_ge(S("wvi_in"), 16)
            pe.wait_ge(S("cd_free"), 6)
            for t in range(NCH + 1):
                n = P if t < NCH else NS
                if t >= 2:
                    pe.wait_ge(S("vt_free"), t - 1)
                for k in range(KD):
                    ins = nc.tensor.matmul(ps[t % 2][0:n, 0:512], H[:, k, t * P:t * P + n], wvi[:, k, :],
                                           start=(k == 0), stop=(k == KD - 1))
                ins.then_inc(S("vt_done"), 1)
            pe.wait_ge(S("vt_free"), NCH + 1)

            for i in range(2):
                for p in parts(f"start{i}"):
                    gate(p)
                pe.wait_ge(S("b_kd"), i + 1)
                for g in range(3):
                    n = 3 * i + g
                    if n >= 2:
                        pe.wait_ge(S("b_tfree"), n - 1)
                    for c in range(4 * g, min(4 * g + 4, NCH + 1)):
                        m = P if c < NCH else NS
                        ins = nc.tensor.transpose(pst[n % 2][0:m, (c % 4) * P:(c % 4) * P + P],
                                                  bE[:, c * P:c * P + m], cc("ident"))
                    ins.then_inc(S("b_tdone"), 1)
                pe.wait_ge(S("b_tfree"), 3 * i + 3)
                pe.wait_ge(S("b_vbd"), i + 1)
                if i:
                    pe.wait_ge(S("b_over"), 1)
                for c in range(NCH):
                    ins = nc.tensor.matmul(ps[0][:, c * P:c * P + P], kdt[:, c, :],
                                           VT[:, c, HW + i * P:HW + i * P + P], start=(c % 4 == 0), stop=True,
                                           skip_group_check=True)
                for b in range(2):
                    ins = nc.tensor.matmul(ps[1][:, b * 512:b * 512 + 512], kdt[0:NS, NCH, :],
                                           vbd[0:NS, 4 * b:4 * b + 4, :], start=True, stop=True)
                ins.then_inc(S("b_u"), 1)
                for p in parts(f"states{i}"):
                    gate(p)
                pe.wait_ge(S("b_ufree"), 2 * (i + 1))
                for l in range(NL):
                    n = NL * i + l
                    if 1 <= l <= 6:
                        gate(parts(f"levels{i}")[(l - 1) // 2], ((l - 1) % 2,))
                    pe.wait_ge(S("b_factors"), n + 1)
                    for g in range(4):
                        u = 4 * n + g
                        if g + 4 * l >= 4:
                            pe.wait_ge(S("b_afree"), u - 3)
                        bank = ps[g // 2][:, (g % 2) * 512:(g % 2) * 512 + 512]
                        for j in range(4):
                            c, hh = 2 * g + j // 2, j % 2
                            kf = KF[:, l % 2, c * P:c * P + P] if l < NL - 1 else Z[:, FB + i, c * P:c * P + P]
                            ins = nc.tensor.matmul(bank[:, j * P:j * P + P], kf, QF[hh][:, l % 2, c * P:c * P + P],
                                                   start=(j == 0), stop=True, skip_group_check=True)
                        ins.then_inc(S("b_adone"), 1)
                    if l >= 5:
                        m = 3 * i + l - 5
                        if m >= 1:
                            pe.wait_ge(S("b_sfree"), m)
                        for hh in range(2):
                            kf = KF[:, l % 2, SEQ:T] if l < NL - 1 else Z[:, FB + i, SEQ:T]
                            ins = nc.tensor.matmul(pst[0][0:NS, hh * NS:hh * NS + NS], kf,
                                                   QF[hh][:, l % 2, SEQ:T], start=(hh == 0), stop=True,
                                                   skip_group_check=True)
                        ins.then_inc(S("b_sdone"), 1)
                pe.wait_ge(S("b_afree"), 4 * NL * (i + 1))
                pe.wait_ge(S("b_sfree"), 3 * (i + 1))
                for g in range(4):
                    bank = ps[g // 2][:, (g % 2) * 512:(g % 2) * 512 + 512]
                    first = True
                    for hh in range(2):
                        for c in (2 * g, 2 * g + 1):
                            dst = bank[:, (2 * hh + c % 2) * P:(2 * hh + c % 2) * P + P]
                            if c:
                                nc.tensor.matmul(dst, Sall[:, c, :], QE[:, c * P:c * P + P], start=first,
                                                 stop=False, skip_group_check=True)
                                first = False
                            ins = nc.tensor.matmul(dst, VT[:, c, HW + i * P:HW + i * P + P], att[:, c, hh, :],
                                                   start=first, stop=True, skip_group_check=True)
                            first = False
                ins.then_inc(S("b_odone"), 1)
                pe.wait_ge(S("s0_in"), 16)
                first = True
                for hh in range(2):
                    for b in range(DB):
                        c0 = hh * NS + b * DL
                        nc.tensor.matmul(pst[1][:, c0:c0 + DL], S0[:, i, b, :], QE[:, SEQ + b * DL:SEQ + b * DL + DL],
                                         start=first, stop=False, skip_group_check=True)
                        first = False
                    ins = nc.tensor.matmul(pst[1][:, hh * NS:hh * NS + NS], VT[0:NS, NCH, HW + i * P:HW + i * P + P],
                                           atts[0:NS, hh, :], start=False, stop=True, skip_group_check=True)
                ins.then_inc(S("b_osdone"), 1)
                pe.wait_ge(S("b_osq"), i + 1)
                pe.wait_ge(S("b_ofree"), i + 1)
                whole(ps[0], cc("headmean"), bE).then_inc(S("b_ms"), 1)

            for p in parts("norms"):
                gate(p)
            for j in range(4):
                if j == 1:
                    pe.wait_ge(S("gate_out"), parts("norms")[-1] + 1)
                pe.wait_ge(S("a_sq"), j + 1)
                if j == 0:
                    pe.wait_ge(S("b_over"), 2)
                if j >= 2:
                    pe.wait_ge(S("a_rs"), j - 1)
                whole(ps[j % 2], cc("headmean"), (keep.rearrange("p a b -> p (a b)"), wT.rearrange("p a b -> p (a b)"))[j % 2])\
                    .then_inc(S("a_ms"), 1)
            pe.wait_ge(S("a_rs"), 4)
            for p in parts("normed"):
                gate(p)
            pe.wait_ge(S("a_qm"), 1)
            tgroups = [0]
            for n in range(32):
                tgroups.append(tgroups[-1] + (n // 4 + 4) // 4)

            def scores(n):
                i, h = n // 4, n % 4
                if n >= 2:
                    pe.wait_ge(S("a_scfree"), n - 1)
                w = (i + 1) * P
                for c0 in range(0, w, 512):
                    m = min(512, w - c0)
                    ins = nc.tensor.matmul(ps[n % 2][:, c0:c0 + m], qm[:, h, i * P:i * P + P],
                                           Z[:, KA + h // 2, c0:c0 + m], start=True, stop=True)
                ins.then_inc(S("a_sc"), 1)

            def transposes(n):
                i = n // 4
                pe.wait_ge(S("a_w"), n + 1)
                for g in range(tgroups[n], tgroups[n + 1]):
                    if g >= 2:
                        pe.wait_ge(S("a_tfree"), g - 1)
                    j0 = 4 * (g - tgroups[n])
                    for j in range(j0, min(j0 + 4, i + 1)):
                        ins = nc.tensor.transpose(pst[g % 2][:, (j - j0) * P:(j - j0) * P + P],
                                                  beta[:, n % 2, j * P:j * P + P], cc("ident"))
                    ins.then_inc(S("a_tdone"), 1)

            def values(n):
                i, h = n // 4, n % 4
                pe.wait_ge(S("a_tfree"), tgroups[n + 1])
                if h == 0 and i >= 1:
                    pe.wait_ge(S("a_ofree"), i)
                for j in range(i + 1):
                    ins = nc.tensor.matmul(ps[0][:, 1024 + h * P:1024 + h * P + P],
                                           VT[:, j, (h // 2) * P:(h // 2) * P + P], wT[:, n % 2, j * P:j * P + P],
                                           start=(h == 0 and j == 0), stop=(j == i), skip_group_check=True)
                ins.then_inc(S("a_pv"), 1)

            for n in range(34):
                if n < 32:
                    scores(n)
                    if n % 4 == 1:
                        gate(parts("steps")[n // 4])
                if 1 <= n <= 32:
                    transposes(n - 1)
                if n >= 2:
                    values(n - 2)
            pe.wait_ge(S("a_scfree"), 32)
            pe.wait_ge(S("a_qs"), 1)
            for b in range(DB):
                if b:
                    gate(parts("samples")[b - 1])
                pe.wait_ge(S(f"kp_in{b % 2}"), 64 * (b // 2 + 1))
                for i in range(2):
                    ins = nc.tensor.matmul(ps[0][:, 0:PAST], QS[:, i, b * P:b * P + P], kp[:, b % 2, :, i, :],
                                           start=(b == 0 and i == 0), stop=(b == DB - 1 and i == 1))
                ins.then_inc(S("kp_used"), 1)
            for i in range(2):
                ins = nc.tensor.matmul(ps[0][:, PAST:PAST + NS], QSall[:, i, :], Z[:, KA + i, SEQ:T],
                                       start=(i == 0), stop=(i == 1))
            ins.then_inc(S("as_sc"), 1)
            pe.wait_ge(S("as_w"), 1)
            for j in range(PAGES):
                ins = nc.tensor.transpose(pst[0][:, j * P:j * P + P], beta[:, 0, j * P:j * P + P], cc("ident"))
            ins = nc.tensor.transpose(pst[1][0:NS, 0:P], beta[:, 0, PAST:PAST + NS], cc("ident"))
            ins.then_inc(S("as_t"), 1)
            pe.wait_ge(S("as_tfree"), 2)
            for i in range(2):
                nc.tensor.matmul(ps[1][:, i * P:i * P + P], VT[0:NS, NCH, i * P:i * P + P], wT[0:NS, 1, 0:P],
                                 start=(i == 0), stop=False, skip_group_check=True)
            for b in range(DB):
                pe.wait_ge(S(f"vp_in{b % 2}"), 64 * (b // 2 + 1))
                for i in range(2):
                    for g in range(PAGES):
                        ins = nc.tensor.matmul(ps[1][:, i * P + 16 * b:i * P + 16 * b + 16],
                                               vp[:, b % 2, g, i * P:i * P + P],
                                               wT[:, 0, g * P + 16 * b:g * P + 16 * b + 16],
                                               start=False, stop=(g == PAGES - 1), skip_group_check=True)
                ins.then_inc(S("vp_used"), 1)
            pe.wait_ge(S("a_over"), 2)

            def m_round(i):
                for u in range(8):
                    q, n = divmod(u, 4)
                    if u in (0, EARLY, EARLY + 2):
                        w = {0: 0, EARLY: 1, EARLY + 2: 2}[u]
                        pe.wait_ge(S(f"mw_in{w}"), (i + 1) * (16 if w == 2 else 32))
                    if u >= EARLY:
                        if u == EARLY:
                            pe.wait_ge(S("m_pfree"), i * 8 + EARLY)
                        else:
                            pe.wait_ge(S("m_sig"), i * 8 + u)
                        dense(ps[0], mwg[:, u - EARLY], H, KD).then_inc(S("m_gate"), 1)
                    elif u == 0:
                        wait_prior(pe, S("m_sig"), i * 8)
                    else:
                        wait_prior(pe, S("m_pfree"), i * 8 + (u - 1))
                    if u >= EARLY or u == 1:
                        wait_prior(pe, S("m_pfree"), i * 8 + (u if u > 1 else 0))
                    dense(ps[m_slot(u)], mwb[:, q, n], Z[:, BRANCH_AT[n]:BRANCH_AT[n] + 2, :], 2)\
                        .then_inc(S("m_proj"), 1)
            rounds(pe, 4, m_round)

            def slots(before, rhs, kk, w, fed):
                pe.wait_ge(*fed)

                def body(i):
                    for q in range(2):
                        pe.wait_ge(S(f"rw_in{q}"), i * 16 + 16 * (before + 1))
                        wait_prior(pe, S(f"r_free{q}"), i + before)
                        dense(ps[q], w[:, q], rhs, kk).then_inc(S(f"r_done{q}"), 1)
                rounds(pe, 4, body)

            pe.wait_ge(S("m_sig"), 32)
            slots(0, MIX, KD, ow, (S("mix_ready"), 8))
            pe.wait_ge(S("r_ss"), 8)
            whole(ps[0], cc("mean"), nSS).then_inc(S("norm_sum"), 1)
            pe.wait_ge(S("n2_h"), 8)

            def u_round(i):
                for q in range(2):
                    pe.wait_ge(S(f"uw_in{q}"), i * 16 + 16)
                    wait_prior(pe, S("u_free0"), i * 2 + q)
                    dense(ps[0], uw[:, q, 0], H, KD).then_inc(S("u_a"), 1)
                    wait_prior(pe, S("u_free1"), i * 2 + q)
                    dense(ps[1], uw[:, q, 1], H, KD).then_inc(S(f"u_done{q}"), 1)
            rounds(pe, 11, u_round)
            pe.wait_ge(S("u_free0"), 22)
            pe.wait_ge(S("u_free1"), 22)
            slots(4, G, NF, dw, (S("g_ready"), NF))
            pe.wait_ge(S("r_ss"), 16)
            whole(ps[0], cc("mean"), dSS).then_inc(S("norm_sum"), 1)
            pe.wait_ge(S("n3_h"), 8)
            pe.wait_ge(S("pe_in"), 16 * KP)

            def p_round(i):
                for q in range(2):
                    pe.wait_ge(S(f"pw_in{q}"), i * 32 + 32)
                    wait_prior(pe, S("p_gfree"), i * 2 + q)
                    dense(ps[0], pw[:, q], H, KD).then_inc(S("p_gate"), 1)
                    wait_prior(pe, S("p_efree"), i * 2 + q)
                    dense(ps[1], pv[:, q], pe_, KP).then_inc(S(f"p_done{q}"), 1)
            rounds(pe, 4, p_round)

        @block.scalar
        def _(act):
            link = Link(act, S("act_chain"))

            def rstd(src, dst):
                link(nc.scalar.activation(dst, src, ACT.Ln, bias=epsc))
                return nc.scalar.activation(dst, dst, ACT.Exp, scale=-0.5)

            epsc = small[:, 90:91]
            act.wait_ge(S("consts"), 1)
            for k in range(KD):
                act.wait_ge(S(f"x_in{k // 2}"), 32)
                if k >= 2:
                    act.wait_ge(S("n1_ss"), k - 1)
                nc.scalar.activation(SQ[:, k % 2], xin[:, k, :], ACT.Square).then_inc(S("n1_sq"), 1)
            act.preload_act_table_set("natural_log_exp_and_others")
            act.wait_ge(S("norm_sum"), 1)
            rstd(ps[0][:, 0:T], RS).then_inc(S("norm_rs"), 1)

            act.wait_ge(S("c_abs"), 1)
            nc.scalar.activation(small[:, 4:6], small[:, 2:4], ACT.Exp, scale=-1.0).then_inc(S("c_exp"), 1)

            def z_round(i):
                for s in range(2):
                    act.wait_ge(S(f"z_done{s}"), i + 1)
                    ins = nc.scalar.activation(Z[:, ds(i * 2 + s, 1), :] if not isinstance(i, int) else Z[:, i * 2 + s:i * 2 + s + 1, :],
                                               ps[s][:, 0:T].rearrange("p (o t) -> p o t", o=1), ACT.Copy)
                    ins.then_inc(S(f"z_free{s}"), 1)
                    act.wait_ge(S(f"z_free{s}"), i + 1)
                    act.sem_inc(S("z_out"), 1)
            rounds(act, 8, z_round)

            for i in range(2):
                act.wait_ge(S("cd_done"), 2 * i + 1)
                nc.scalar.activation(cR[:, i], ps[0][:, 0:T], ACT.Sigmoid, bias=pc("b_rg_a", i)).then_inc(S("cd_free"), 1)
                act.wait_ge(S("cd_done"), 2 * i + 2)
                ins = nc.scalar.activation(cI[:, i], ps[1][:, 0:T], ACT.Sigmoid, bias=pc("b_rg_x", i))
                ins.then_inc(S("cd_free"), 1)
            act.wait_ge(S("raw_stored"), 1)
            for i in range(2):
                act.wait_ge(S("cd_done"), 5 + i)
                nc.scalar.activation(Z[:, XD + i, :], ps[i][:, 0:T], ACT.Copy, scale=pc("pool_scale", i))\
                    .then_inc(S("cd_free"), 1)
            act.wait_ge(S("cd_free"), 4)
            act.wait_ge(S("c_lam"), 1)
            for i in range(2):
                if i:
                    act.wait_ge(S("c_scanned"), 1)
                link(nc.scalar.activation(cA, cR[:, i], ACT.Exp, scale=small[:, 20 + i:21 + i]))
                nc.scalar.activation(cB, cA, ACT.Square).then_inc(S("c_a"), 1)
                nc.scalar.activation(cR[:, i], cR[:, i], ACT.Tanh, scale=small[:, 22 + i:23 + i]).then_inc(S("c_a"), 1)
                act.wait_ge(S("c_1ma2"), i + 1)
                nc.scalar.activation(cB, cB, ACT.Sqrt).then_inc(S("c_sqrt"), 1)
                nc.scalar.activation(Z[:, GC + i, :], Z[:, GC + i, :], ACT.Gelu_apprx_tanh).then_inc(S("c_gelu"), 1)

            for t in range(NCH + 1):
                n = P if t < NCH else NS
                act.wait_ge(S("vt_done"), t + 1)
                nc.scalar.activation(VT[0:n, t, :], ps[t % 2][0:n, 0:512], ACT.Copy).then_inc(S("vt_free"), 1)

            def gate_out(p):
                act.wait_ge(S("gate_done"), p + 1)
                if p >= 2:
                    act.wait_ge(S(f"gate_stored{p % 2}"), 16 * (p // 2))
                nc.scalar.activation(gstage[:, p % 2], gbank, ACT.Copy).then_inc(S("gate_out"), 1)

            f2, q2, g2 = Z[:, FB:FB + 2, :], Z[:, QB:QB + 2, :], Z[:, GB:GB + 2, :]
            act.wait_ge(S("cd_over"), 1)
            link(nc.scalar.activation(tA, f2, ACT.Abs))
            link(nc.scalar.activation(tA, tA, ACT.Exp, scale=-1.0))
            nc.scalar.activation(tA, tA, ACT.Ln, bias=1.0).then_inc(S("b_act_pre"), 1)
            act.wait_ge(S("b_dve_pre"), 1)
            nc.scalar.activation(f2, f2, ACT.Sigmoid, scale=-1.0).then_inc(S("b_act_pre"), 1)
            nc.scalar.activation(tA, q2, ACT.Sigmoid).then_inc(S("b_act_pre"), 1)
            gate_out(parts("start0")[0])
            act.wait_ge(S("b_dve_pre"), 2)
            nc.scalar.activation(tA, g2, ACT.Sigmoid).then_inc(S("b_act_pre"), 1)
            gate_out(parts("start0")[1])
            act.wait_ge(S("b_dve_pre"), 3)
            act.preload_act_table_set("natural_log_exp_and_others")
            for i in range(2):
                b = bB[:, i]
                if i == 0:
                    act.wait_ge(S("b_cum"), 2)
                if i:
                    act.wait_ge(S("b_over"), 1)
                nc.scalar.activation(bE, b, ACT.Exp).then_inc(S("b_eb"), 1)
                nc.scalar.activation(bdec[:, 0:8], b[:, CH - 1:SEQ:CH], ACT.Exp).then_inc(S("b_dec"), 1)
                nc.scalar.activation(bdec[:, 8:16], b[:, SEQ + DL - 1:T:DL], ACT.Exp).then_inc(S("b_dec"), 1)
                act.wait_ge(S("b_kdiff"), i + 1)
                nc.scalar.activation(bE, bd_, ACT.Exp, scale=-1.0).then_inc(S("b_kexp"), 1)
                gate_out(parts(f"start{i}")[-2 if i == 0 else 0])
                for g in range(3):
                    act.wait_ge(S("b_tdone"), 3 * i + g + 1)
                    w = min(4, NCH + 1 - 4 * g) * P
                    m = P if g < 2 else NS
                    nc.scalar.activation(kdt[0:m, 4 * g:4 * g + w // P, :].rearrange("p c m -> p (c m)"),
                                         pst[(3 * i + g) % 2][0:m, 0:w], ACT.Copy).then_inc(S("b_tfree"), 1)
                gate_out(parts(f"start{i}")[-1])
                for p in parts(f"states{i}"):
                    gate_out(p)
                for l, m in enumerate(LEVELS):
                    n = len(LEVELS) * i + l
                    nt = T if m <= 2 else SEQ
                    act.wait_ge(S("b_diff"), n + 1)
                    if l == 0:
                        act.wait_ge(S("b_tdone"), 3 * i + 3)
                    dv = bd_[:, 0:nt].rearrange("p (n h m) -> p n h m", h=2, m=m)
                    kv = KF[:, l % 2, 0:nt].rearrange("p (n h m) -> p n h m", h=2, m=m)
                    ev = bE[:, 0:nt].rearrange("p (n h m) -> p n h m", h=2, m=m)
                    nc.scalar.activation(kv[:, :, 0, :], dv[:, :, 0, :], ACT.Exp, scale=-1.0).then_inc(S("b_exps"), 1)
                    nc.scalar.activation(ev[:, :, 1, :], dv[:, :, 1, :], ACT.Exp).then_inc(S("b_exps"), 1)
                    if l in (2, 4, 6):
                        gate_out(parts(f"levels{i}")[l // 2 - 1])
                act.wait_ge(S("b_ofree"), i + 1)
                nc.scalar.activation(bE, bd_, ACT.Square).then_inc(S("b_osq"), 1)
                act.wait_ge(S("b_ms"), i + 1)
                rstd(ps[0][:, 0:T], bE).then_inc(S("b_rs"), 1)

            def a_rs(j):
                act.wait_ge(S("a_ms"), j + 1)
                if j >= 2:
                    act.wait_ge(S("a_normed"), j - 1)
                rstd(ps[j % 2][:, 0:T], beta.rearrange("p a b -> p (a b)")[:, 0:T] if j % 2 == 0 else
                     Pp.rearrange("p a b -> p (a b)")[:, 0:T]).then_inc(S("a_rs"), 1)

            kf_, wf_ = keep.rearrange("p a b -> p (a b)"), wT.rearrange("p a b -> p (a b)")
            order = (KA, KA + 1, QA, QA + 1)
            act.wait_ge(S("b_over"), 2)
            for j in range(4):
                if j >= 2:
                    act.wait_ge(S("a_ms"), j - 1)
                nc.scalar.activation((kf_, wf_)[j % 2][:, 0:T], Z[:, order[j], :], ACT.Square).then_inc(S("a_sq"), 1)
                if j == 0:
                    for p in parts("norms"):
                        gate_out(p)
                if j >= 1:
                    a_rs(j - 1)
            a_rs(3)
            for p in parts("normed"):
                gate_out(p)
            act.wait_ge(S("a_qm"), 1)
            tg = [0]
            for n in range(32):
                tg.append(tg[-1] + (n // 4 + 4) // 4)

            def sticks(n):
                i, h = n // 4, n % 4
                w = (i + 1) * P
                act.wait_ge(S("a_sc"), n + 1)
                if n >= 2:
                    act.wait_ge(S("a_tdone"), tg[n - 1])
                nc.scalar.activation(keep[:, n % 2, 0:w], ps[n % 2][:, 0:w], ACT.Sigmoid,
                                     scale=-HD ** -0.5, bias=negb[:, h:h + 1]).then_inc(S("a_stick"), 1)
                nc.scalar.activation(beta[:, n % 2, 0:w], ps[n % 2][:, 0:w], ACT.Sigmoid,
                                     scale=HD ** -0.5, bias=pc("sb_head", h)).then_inc(S("a_scfree"), 1)

            def turned(n):
                i = n // 4
                for g in range(tg[n], tg[n + 1]):
                    j0 = 4 * (g - tg[n])
                    w = (min(j0 + 4, i + 1) - j0) * P
                    act.wait_ge(S("a_tdone"), g + 1)
                    if n >= 2:
                        act.wait_ge(S("a_pv"), n - 1)
                    nc.scalar.activation(wT[:, n % 2, j0 * P:j0 * P + w], pst[g % 2][:, 0:w], ACT.Copy)\
                        .then_inc(S("a_tfree"), 1)

            for n in range(33):
                if n < 32:
                    sticks(n)
                if n >= 1:
                    turned(n - 1)
                if n < 32 and n % 4 == 1:
                    gate_out(parts("steps")[n // 4])
            for p in parts("samples"):
                gate_out(p)
            act.wait_ge(S("as_sc"), 1)
            act.wait_ge(S("a_tdone"), tg[32])
            nc.scalar.activation(keep[:, 0, 0:PAST + NS], ps[0][:, 0:PAST + NS], ACT.Sigmoid,
                                 scale=-HD ** -0.5, bias=negb[:, 4:5]).then_inc(S("as_stick"), 1)
            nc.scalar.activation(beta[:, 0, 0:PAST + NS], ps[0][:, 0:PAST + NS], ACT.Sigmoid,
                                 scale=HD ** -0.5, bias=pc("sb_row")).then_inc(S("as_stick"), 1)
            act.wait_ge(S("as_t"), 1)
            act.wait_ge(S("a_pv"), 32)
            nc.scalar.activation(wT[:, 0, 0:PAST], pst[0][:, 0:PAST], ACT.Copy).then_inc(S("as_tfree"), 1)
            nc.scalar.activation(wT[0:NS, 1, 0:P], pst[1][0:NS, 0:P], ACT.Copy).then_inc(S("as_tfree"), 1)

            def m_round(i):
                for u in range(8):
                    if u < EARLY:
                        act.wait_ge(S("mw_in0"), i * 32 + 32)
                    else:
                        act.wait_ge(S("m_gate"), i * LATE + (u - EARLY + 1))
                    if u >= 2 or not isinstance(i, int):
                        act.wait_ge(S("m_pfree"), i * 8 + (u - 1))
                    nc.scalar.activation(SIG[:, u % 2], early[:, u] if u < EARLY else ps[0][:, 0:T], ACT.Sigmoid)\
                        .then_inc(S("m_sig"), 1)
            act.wait_ge(S("a_over"), 2)
            rounds(act, 4, m_round)

            def squares(before, dst):
                def body(i):
                    for q in range(2):
                        act.wait_ge(S("r_added"), i * 2 + (q + 1 + 2 * before))
                        src = X[:, i * 2 + q:i * 2 + q + 1, :] if isinstance(i, int) else X[:, ds(i * 2 + q, 1), :]
                        wait_prior(act, S("r_ss"), i * 2 + (q + 2 * before))
                        nc.scalar.activation(dst.rearrange("p (o t) -> p o t", o=1), src, ACT.Square)\
                            .then_inc(S("r_sq"), 1)
                rounds(act, 4, body)

            squares(0, nSQ)
            act.preload_act_table_set("natural_log_exp_and_others")
            act.wait_ge(S("norm_sum"), 2)
            rstd(ps[0][:, 0:T], nRS).then_inc(S("norm_rs"), 1)

            act.wait_ge(S("fpar_in"), 32)
            act.wait_ge(S("n2_h"), 8)

            def u_round(i):
                def at(x, q):
                    c = i * 2 + q
                    return x[:, c:c + 1] if isinstance(i, int) else x[:, ds(c, 1)]

                for q in range(2):
                    for half in range(2):
                        act.wait_ge(S("u_a") if half == 0 else S(f"u_done{q}"),
                                    i * 2 + (q + 1) if half == 0 else i + 1)
                        if half == 0:
                            if q or not isinstance(i, int):
                                act.wait_ge(S("g_ready"), i * 2 + q)
                            fp = small[:, 64:72]
                            link(nc.scalar.activation(fp.rearrange("p (o e) -> p o e", o=1), at(fpar, q), ACT.Copy))
                        src = ps[half][:, 0:T]
                        nc.scalar.activation(V[:, half], src, ACT.Identity, scale=fp[:, 4 * half + 2:4 * half + 3],
                                             bias=fp[:, 4 * half + 3:4 * half + 4]).then_inc(S("u_tap"), 1)
                        fo = at(FO, q)[:, :, half, :]
                        nc.scalar.activation(fo[:, :, 0:2], src[:, SEQ - 2:SEQ].rearrange("p (o e) -> p o e", o=1),
                                             ACT.Copy).then_inc(S("fo"), 1)
                        link(nc.scalar.activation(
                            fo[:, :, 2:18].rearrange("p o (b e) -> p (o b) e", b=DB),
                            src[:, SEQ:T].rearrange("p (b t) -> p b t", b=DB)[:, :, 2:4], ACT.Copy))
                        act.wait_ge(S("fo"), i * 4 + (2 * q + half + 1))
                        act.sem_inc(S(f"u_read{half}"), 1)
                    act.wait_ge(S("u_free0"), i * 2 + (q + 1))
                    nc.scalar.activation(V[:, 0], V[:, 0], ACT.Gelu_apprx_tanh).then_inc(S("u_gelu"), 1)
            link.rounds(11, u_round)

            squares(4, dSQ)
            act.preload_act_table_set("natural_log_exp_and_others")
            act.wait_ge(S("norm_sum"), 3)
            rstd(ps[0][:, 0:T], dRS).then_inc(S("norm_rs"), 1)

            def p_round(i):
                for q in range(2):
                    act.wait_ge(S("p_gate"), i * 2 + (q + 1))
                    if not isinstance(i, int):
                        act.wait_ge(S("y_ready"), i * 2 + (q - 1))
                    nc.scalar.activation(sigp[:, q], ps[0][:, 0:T], ACT.Sigmoid).then_inc(S("p_gfree"), 1)
            rounds(act, 4, p_round)

        @block.vector
        def _(dve):
            v = nc.vector
            link = Link(dve, S("dve_chain"))
            v.memset(small[:, 90:91], EPS).then_inc(S("consts"), 1)
            for k in range(KD):
                dve.wait_ge(S("n1_sq"), k + 1)
                if k == 0:
                    v.tensor_copy(SS, SQ[:, 0]).then_inc(S("n1_ss"), 1)
                else:
                    dve.wait_ge(S("n1_ss"), k)
                    v.tensor_tensor(SS, SS, SQ[:, k % 2], ALU.add).then_inc(S("n1_ss"), 1)
            dve.wait_ge(S("params_in"), 32)
            link(v.tensor_scalar(small[:, 0:2], pc("lam", 0, 2), -1.0, 0.0, ALU.mult, ALU.max))
            v.scalar_tensor_tensor(small[:, 2:4], small[:, 0:2], 2.0, pc("lam", 0, 2), ALU.mult, ALU.add)\
                .then_inc(S("c_abs"), 1)
            dve.wait_ge(S("norm_rs"), 1)
            for k in range(KD):
                v.scalar_tensor_tensor(H[:, k, :], xin[:, k, :], pc("norm_mix", k), RS, ALU.mult, ALU.mult)\
                    .then_inc(S("n1_h"), 1)
            dve.wait_ge(S("c_exp"), 1)
            e_, s_, s2, p_ = small[:, 4:6], small[:, 6:8], small[:, 8:10], small[:, 10:12]
            link(v.tensor_scalar(p_, e_, 2.0, None, ALU.add))
            link(v.reciprocal(p_, p_))
            link(v.tensor_tensor(s_, e_, p_, ALU.mult))
            link(v.tensor_tensor(s2, s_, s_, ALU.mult))
            link(v.tensor_scalar(p_, s2, 1.0 / 17, None, ALU.mult))
            for n in range(7, 0, -1):
                link(v.scalar_tensor_tensor(p_, p_, 1.0 / (2 * n + 1), s2, ALU.add, ALU.mult))
            link(v.tensor_scalar(p_, p_, 1.0, 2.0, ALU.add, ALU.mult))
            link(v.tensor_tensor(p_, p_, s_, ALU.mult))
            link(v.tensor_tensor(p_, p_, small[:, 0:2], ALU.add))
            link(v.tensor_scalar(small[:, 20:22], p_, -8.0, None, ALU.mult),
                 v.tensor_scalar(small[:, 22:24], p_, 8.0, None, ALU.mult))
            dve.sem_inc(S("c_lam"), 1)

            dve.wait_ge(S("cd_in"), 64)
            for i in range(2):
                dve.wait_ge(S(f"z_free{i}"), 1)
                x, y = Z[:, XC + i, :], cX[:, i]
                w = [pc("conv_c_w", 2 * j + i) for j in range(4)]
                link(v.tensor_copy(cext[:, :, 0:3], chist[:, i]),
                     v.tensor_copy(cext[:, :, 3:7], x[:, SEQ:T].rearrange("p (b t) -> p b t", b=DB)))
                ys = y[:, SEQ:T].rearrange("p (b t) -> p b t", b=DB)
                link(v.tensor_scalar(y[:, 0:SEQ], x[:, 0:SEQ], w[3], pc("conv_c_b", i), ALU.mult, ALU.add),
                     v.tensor_scalar(ys, cext[:, :, 3:7], w[3], pc("conv_c_b", i), ALU.mult, ALU.add))
                for j in (2, 1, 0):
                    d = 3 - j
                    link(v.scalar_tensor_tensor(y[:, d:SEQ], x[:, 0:SEQ - d], w[j], y[:, d:SEQ], ALU.mult, ALU.add),
                         v.scalar_tensor_tensor(ys, cext[:, :, j:j + 4], w[j], ys, ALU.mult, ALU.add))
                dve.sem_inc(S("cd_ready"), 1)

            for i in range(2):
                dve.wait_ge(S(f"z_free{i}"), XD // 2 + 1)
                x = Z[:, XD + i, :]
                dEs = dE[:, HIST + SEQ:EXT].rearrange("p (b t) -> p b t", b=DB)
                if i == 0:
                    link(v.memset(dE[:, 0:HIST], 0.0))
                dve.wait_ge(S("pool_in"), 16 * (i + 1))
                link(v.tensor_copy(dE[:, HIST:HIST + SEQ], x[:, 0:SEQ]),
                     v.tensor_copy(dEs[:, :, HIST:], x[:, SEQ:T].rearrange("p (b t) -> p b t", b=DB)))
                src, dst = dE, dF
                for w in ((1, 2), (1, 2, 4, 8))[i]:
                    top = w == (2, 8)[i]
                    if top:
                        link(v.tensor_tensor(dst[HD:P, 2 * w - 1:EXT], src[HD:P, 2 * w - 1:EXT],
                                             src[HD:P, w - 1:EXT - w], ALU.add),
                             v.tensor_copy(dst[0:HD, HIST:EXT], src[0:HD, HIST:EXT]))
                    else:
                        link(v.tensor_tensor(dst[:, 2 * w - 1:EXT], src[:, 2 * w - 1:EXT], src[:, w - 1:EXT - w],
                                             ALU.add))
                    src, dst = dst, src
                link(v.tensor_tensor(src[:, HIST:2 * HIST], src[:, HIST:2 * HIST], cc("corr", HIST, i * HIST),
                                     ALU.mult))
                dve.wait_ge(S("raw_stored"), 1)
                ss = src[:, HIST + SEQ:EXT].rearrange("p (b t) -> p b t", b=DB)[:, :, HIST:]
                xs = x[:, SEQ:T].rearrange("p (b t) -> p b t", b=DB)
                link(v.scalar_tensor_tensor(x[:, 0:SEQ], src[:, HIST:HIST + SEQ], cc("invw", 1, i), x[:, 0:SEQ],
                                            ALU.mult, ALU.subtract),
                     v.scalar_tensor_tensor(xs, ss, cc("invw", 1, i), xs, ALU.mult, ALU.subtract))
                dve.sem_inc(S("cd_ready"), 1)

            for i in range(2):
                dve.wait_ge(S("c_a"), 2 * i + 2)
                v.scalar_tensor_tensor(cB, cB, 1.0, cR[:, i], ALU.add, ALU.mult).then_inc(S("c_1ma2"), 1)
                link(v.tensor_tensor(cI[:, i], cI[:, i], cX[:, i], ALU.mult))
                dve.wait_ge(S("c_sqrt"), i + 1)
                link(v.tensor_tensor(cI[:, i], cI[:, i], cB, ALU.mult))
                a0, u0 = cA[:, SEQ:T:DL], cI[:, i, SEQ:T:DL]
                link(v.tensor_tensor(small[:, 24:32], a0, ch0[:, i], ALU.mult))
                link(v.tensor_tensor(u0, u0, small[:, 24:32], ALU.add), v.memset(a0, 0.0))
                link(v.tensor_tensor_scan(cX[:, i], cA, cI[:, i], 0.0, ALU.mult, ALU.add))
                link(v.tensor_copy(small[:, 40 + i:41 + i], cX[:, i, SEQ - 1:SEQ]),
                     v.tensor_copy(small[:, 48 + 8 * i:56 + 8 * i], cX[:, i, SEQ + DL - 1:T:DL]))
                dve.sem_inc(S("c_scanned"), 1)
                dve.wait_ge(S("c_gelu"), i + 1)
                v.tensor_tensor(Z[:, GC + i, :], Z[:, GC + i, :], cX[:, i], ALU.mult).then_inc(S("c_out"), 1)
            dve.wait_ge(S("c_out"), 2)
            dve.wait_ge(S("cd_free"), 6)
            dve.wait_ge(S("vt_free"), NCH + 1)
            dve.sem_inc(S("cd_over"), 1)

            f2, q2, g2 = Z[:, FB:FB + 2, :], Z[:, QB:QB + 2, :], Z[:, GB:GB + 2, :]
            link(v.memset(rmask, 1.0))
            link(v.memset(rmask[:, 0:SEQ:CH], 0.0), v.memset(rmask[:, SEQ:T:DL], 0.0))
            for buf in (KF, QF[0], QF[1]):
                link(v.memset(buf, 0.0))
            dve.wait_ge(S("b_act_pre"), 1)
            link(v.scalar_tensor_tensor(bB, f2, 0.0, tA, ALU.min, ALU.subtract))
            dve.sem_inc(S("b_dve_pre"), 1)
            for i in range(2):
                v.tensor_tensor_scan(bB[:, i], rmask, bB[:, i], 0.0, ALU.mult, ALU.add).then_inc(S("b_cum"), 1)
            dve.wait_ge(S("b_act_pre"), 3)
            v.tensor_tensor(q2, q2, tA, ALU.mult).then_inc(S("b_dve_pre"), 1)
            dve.wait_ge(S("b_act_pre"), 4)
            v.tensor_tensor(g2, g2, tA, ALU.mult).then_inc(S("b_dve_pre"), 1)
            dve.wait_ge(S("b_dve_pre"), 2)
            dve.wait_ge(S("b_dve_pre"), 3)
            dve.wait_ge(S("b_cum"), 2)
            dve.wait_ge(S("masks_in"), 32)
            dve.wait_ge(S("b_act_pre"), 2)
            for i in range(2):
                b, kk, qq, gg = bB[:, i], Z[:, FB + i, :], Z[:, QB + i, :], Z[:, GB + i, :]
                bp, bs = b[:, 0:SEQ].rearrange("p (c t) -> p c t", c=NCH), b[:, SEQ:T].rearrange("p (c t) -> p c t", c=DB)
                dp = bd_[:, 0:SEQ].rearrange("p (c t) -> p c t", c=NCH)
                dss = bd_[:, SEQ:T].rearrange("p (c t) -> p c t", c=DB)
                dve.wait_ge(S("b_eb"), i + 1)
                link(v.tensor_tensor(QE, qq, bE, ALU.mult))
                link(v.tensor_tensor(dp, bp, bp[:, :, CH - 1:CH].to_broadcast([P, NCH, CH]), ALU.subtract),
                     v.tensor_tensor(dss, bs, bs[:, :, DL - 1:DL].to_broadcast([P, DB, DL]), ALU.subtract))
                dve.sem_inc(S("b_kdiff"), 1)
                dve.wait_ge(S("b_kexp"), i + 1)
                v.tensor_tensor(bE, bE, kk, ALU.mult).then_inc(S("b_kd"), 1)
                if i:
                    dve.wait_ge(S("states_stored"), 1)
                for bb in range(DB):
                    ins = v.tensor_scalar(vbd[0:NS, bb, :], VT[0:NS, NCH, HW + i * P:HW + i * P + P],
                                          cc("batch", 1, bb, NS), None, ALU.mult)
                    link(ins)
                dve.sem_inc(S("b_vbd"), 1)
                dve.wait_ge(S("b_u"), i + 1)
                dve.wait_ge(S("b_dec"), 2 * i + 2)
                UBp = KF.rearrange("p a b -> p (a b)")[:, 0:NCH * P].rearrange("p (c m) -> p c m", c=NCH)
                bdb = cc("bd").rearrange("p (o m) -> p o m", o=1).to_broadcast([P, NCH, P])
                up = ps[0][:, 0:SEQ].rearrange("p (c m) -> p c m", c=NCH)
                us_ = ps[1][:, 0:SEQ].rearrange("p (c m) -> p c m", c=NCH)
                v.tensor_tensor(UBp, up, bdb, ALU.mult).then_inc(S("b_ufree"), 1)
                dve.wait_ge(S("b_ufree"), 2 * i + 1)
                link(v.tensor_copy(Sall[:, 1, :], UBp[:, 0, :]))
                for c in range(1, NCH):
                    link(v.scalar_tensor_tensor(Sall[:, c + 1, :], Sall[:, c, :], bdec[:, c:c + 1], UBp[:, c, :],
                                                ALU.mult, ALU.add))
                v.tensor_tensor(UBp, us_, bdb, ALU.mult).then_inc(S("b_ufree"), 1)
                dve.wait_ge(S("b_ufree"), 2 * i + 2)
                dve.wait_ge(S("s0_in"), 16)
                for bb in range(DB):
                    link(v.scalar_tensor_tensor(vbd[:, bb, :], S0[:, i, bb, :], bdec[:, 8 + bb:9 + bb],
                                                UBp[:, bb, :], ALU.mult, ALU.add))
                dve.sem_inc(S("b_states"), 1)
                link(v.memset(KF, 0.0), v.memset(att, 0.0), v.memset(atts[0:NS], 0.0))

                def differences(l, m):
                    if l:
                        dve.wait_ge(S("b_exps"), 2 * (len(LEVELS) * i + l))
                    nt = T if m <= 2 else SEQ
                    bv = b[:, 0:nt].rearrange("p (n w) -> p n w", w=2 * m)
                    dv = bd_[:, 0:nt].rearrange("p (n w) -> p n w", w=2 * m)
                    if l >= 2:
                        dve.wait_ge(S("b_adone"), 4 * (NL * i + l - 1))
                    if l >= 7:
                        dve.wait_ge(S("b_sdone"), 3 * i + l - 6)
                    v.tensor_tensor(dv, bv, bv[:, :, m - 1:m].to_broadcast([P, nt // (2 * m), 2 * m]), ALU.subtract)\
                        .then_inc(S("b_diff"), 1)

                def factors(l, m):
                    nt = T if m <= 2 else SEQ
                    dve.wait_ge(S("b_exps"), 2 * (len(LEVELS) * i + l + 1))

                    def halves(x):
                        return x[:, 0:nt].rearrange("p (n h m) -> p n h m", h=2, m=m)
                    kv = halves(KF[:, l % 2])[:, :, 0, :]
                    link(v.tensor_tensor(kv, kv, halves(kk)[:, :, 0, :], ALU.mult),
                         *[v.tensor_tensor(halves(QF[hh][hh * HD:hh * HD + HD, l % 2])[:, :, 1, :],
                                           halves(qq[hh * HD:hh * HD + HD])[:, :, 1, :],
                                           halves(bE[hh * HD:hh * HD + HD])[:, :, 1, :], ALU.mult) for hh in range(2)])
                    dve.sem_inc(S("b_factors"), 1)

                def select(l):
                    n = NL * i + l
                    for g in range(4):
                        dve.wait_ge(S("b_adone"), 4 * n + g + 1)
                        bank = ps[g // 2][:, (g % 2) * 512:(g % 2) * 512 + 512].rearrange("p (a m) -> p a m", a=4)
                        v.copy_predicated(att[:, 2 * g:2 * g + 2].rearrange("p c h m -> p (c h) m"),
                                          masks[:, l:l + 1, :].to_broadcast([P, 4, P]), bank).then_inc(S("b_afree"), 1)
                    if l >= 5:
                        dve.wait_ge(S("b_sdone"), 3 * i + l - 4)
                        v.copy_predicated(atts[0:NS], smasks[:, l - 5:l - 4, :].to_broadcast([NS, 2, NS]),
                                          pst[0][0:NS, 0:2 * NS].rearrange("p (h t) -> p h t", h=2))\
                            .then_inc(S("b_sfree"), 1)

                for l in range(NL + 1):
                    if l < NL - 1:
                        differences(l, LEVELS[l])
                    if l >= 1:
                        select(l - 1)
                    if l < NL - 1:
                        factors(l, LEVELS[l])
                    elif l == NL - 1:
                        dve.wait_ge(S("b_adone"), 4 * (NL * i + l - 1))
                        dve.wait_ge(S("b_sdone"), 3 * i + 1)
                        link(*[v.tensor_copy(QF[hh][hh * HD:hh * HD + HD, l % 2], qq[hh * HD:hh * HD + HD])
                               for hh in range(2)])
                        dve.sem_inc(S("b_factors"), 1)
                dve.wait_ge(S("b_odone"), i + 1)
                dve.wait_ge(S("b_exps"), 2 * len(LEVELS) * (i + 1))
                for hh in range(2):
                    rows = slice(hh * HD, hh * HD + HD)
                    for g in range(4):
                        bank = ps[g // 2][rows, (g % 2) * 512 + hh * 256:(g % 2) * 512 + hh * 256 + 256]
                        v.tensor_copy(bd_[rows, g * 256:g * 256 + 256], bank).then_inc(S("b_oc"), 1)
                dve.wait_ge(S("b_osdone"), i + 1)
                for hh in range(2):
                    rows = slice(hh * HD, hh * HD + HD)
                    v.tensor_copy(bd_[rows, SEQ:T], pst[1][rows, hh * NS:hh * NS + NS]).then_inc(S("b_oc"), 1)
                dve.wait_ge(S("b_oc"), 10 * (i + 1))
                dve.sem_inc(S("b_ofree"), 1)
                link(v.tensor_tensor(gg, gg, bd_, ALU.mult))
                dve.wait_ge(S("b_rs"), i + 1)
                dve.wait_ge(S("states_stored"), i + 1)
                link(v.scalar_tensor_tensor(gg, gg, pc("hgrn_norm"), bE, ALU.mult, ALU.mult))
                dve.sem_inc(S("b_over"), 1)

            link(v.tensor_scalar(negb[:, 0:NH + 1], par[:, PAR["sb_head"]:PAR["sb_head"] + NH + 1], -1.0, None,
                                 ALU.mult), v.memset(QS, 0.0), v.memset(qm, 0.0))
            rs = (beta.rearrange("p a b -> p (a b)")[:, 0:T], Pp.rearrange("p a b -> p (a b)")[:, 0:T])
            for j in range(4):
                dve.wait_ge(S("a_rs"), j + 1)
                if j < 2:
                    link(v.scalar_tensor_tensor(Z[:, KA + j, :], Z[:, KA + j, :], pc("k_norm"), rs[j % 2], ALU.mult,
                                                ALU.mult))
                    dve.sem_inc(S("a_kq"), 1)
                else:
                    for hh in range(2):
                        rows = slice(hh * HD, hh * HD + HD)
                        link(v.scalar_tensor_tensor(qm[rows, 2 * (j - 2) + hh, :], Z[rows, QA + j - 2, :],
                                                    pc("q_norm")[rows], rs[j % 2][rows], ALU.mult, ALU.mult))
                dve.sem_inc(S("a_normed"), 1)
            for h in range(NH):
                rows = slice((h % 2) * HD, (h % 2) * HD + HD)
                src = qm[rows, h, SEQ:T].rearrange("p (b t) -> p b t", b=DB)
                link(v.tensor_copy(QS[rows, h // 2, :].rearrange("p (b c) -> p b c", c=144)[:, :, 4 * h:4 * h + 4],
                                   src))
            for i in range(2):
                link(v.memset(QSall[:, i], 0.0))
                for hh in range(2):
                    h = 2 * i + hh
                    rows = slice(hh * HD, hh * HD + HD)
                    link(v.tensor_copy(QSall[rows, i, :].rearrange("p (b c) -> p b c", c=16)[:, :, 4 * h:4 * h + 4],
                                       qm[rows, h, SEQ:T].rearrange("p (b t) -> p b t", b=DB)))
            dve.sem_inc(S("a_qs"), 1)
            for s in range(2):
                link(v.memset(Pp[:, s, :], 1.0))
            dve.sem_inc(S("a_qm"), 1)

            def broken(s, w, d0, dn, yes, no):
                link(v.tensor_tensor(beta[:, s, d0:d0 + dn], beta[:, s, d0:d0 + dn], yes, ALU.mult),
                     v.tensor_tensor(keep[:, s, d0:d0 + dn], keep[:, s, d0:d0 + dn], no, ALU.max))
                if w < SEQ:
                    link(v.memset(Pp[:, s, w:w + 1], 1.0))
                link(v.tensor_tensor_scan(Pp[:, s, 0:w][:, ::-1], keep[:, s, 0:w][:, ::-1], keep[:, s, 0:w][:, ::-1],
                                          1.0, ALU.mult, ALU.bypass))
                return v.tensor_tensor(beta[:, s, 0:w], beta[:, s, 0:w], Pp[:, s, 1:w + 1], ALU.mult)

            def heads_out(i):
                dve.wait_ge(S("a_pv"), 4 * i + 4)
                for h in range(NH):
                    rows = slice((h % 2) * HD, (h % 2) * HD + HD)
                    v.tensor_copy(Z[rows, QA + h // 2, i * P:i * P + P],
                                  ps[0][rows, 1024 + h * P:1024 + h * P + P]).then_inc(S("a_oc"), 1)
                dve.wait_ge(S("a_oc"), 4 * i + 4)
                dve.sem_inc(S("a_ofree"), 1)

            for n in range(32):
                i = n // 4
                dve.wait_ge(S("a_stick"), n + 1)
                dve.wait_ge(S("a_scfree"), n + 1)
                if n:
                    dve.wait_ge(S("a_w"), n)
                broken(n % 2, (i + 1) * P, i * P, P, cc("strict"), cc("notstrict")).then_inc(S("a_w"), 1)
                if n % 4 == 1 and i >= 1:
                    heads_out(i - 1)
            heads_out(7)
            dve.wait_ge(S("as_stick"), 2)
            broken(0, PAST + NS, PAST, NS, cc("newkeys", NS), cc("notnewkeys", NS)).then_inc(S("as_w"), 1)
            dve.wait_ge(S("vp_used"), DB)
            for h in range(NH):
                rows = slice((h % 2) * HD, (h % 2) * HD + HD)
                link(v.tensor_copy(Z[rows, QA + h // 2, SEQ:T].rearrange("p (b t) -> p b t", b=DB),
                                   ps[1][rows, (h // 2) * P:(h // 2) * P + P].rearrange(
                                       "p (b c) -> p b c", c=16)[:, :, 4 * h:4 * h + 4]))
            dve.sem_inc(S("a_over"), 2)

            def m_round(i):
                for q in range(2):
                    for n in range(4):
                        u = 4 * q + n
                        dve.wait_ge(S("m_sig"), i * 8 + (u + 1))
                        dve.wait_ge(S("m_proj"), i * 8 + (u + 1))
                        dst = ACC if n == 0 else TMP
                        v.tensor_tensor(dst, SIG[:, u % 2], ps[m_slot(u)][:, 0:T], ALU.mult)\
                            .then_inc(S("m_pfree"), 1)
                        dve.wait_ge(S("m_pfree"), i * 8 + (u + 1))
                        if 0 < n < 3:
                            link(v.tensor_tensor(ACC, ACC, TMP, ALU.add))
                    c = i * 2 + q
                    dst = MIX[:, c:c + 1, :] if isinstance(i, int) else MIX[:, ds(c, 1), :]
                    v.tensor_tensor(dst, ACC.rearrange("p (o t) -> p o t", o=1),
                                    TMP.rearrange("p (o t) -> p o t", o=1), ALU.add).then_inc(S("mix_ready"), 1)
                    dve.wait_ge(S("mix_ready"), i * 2 + (q + 1))
            link.rounds(4, m_round)

            def residual(before, sq, ss):
                link(v.memset(ss, 0.0))

                def body(i):
                    for q in range(2):
                        c = i * 2 + q
                        x = X[:, c:c + 1, :] if isinstance(i, int) else X[:, ds(c, 1), :]
                        dve.wait_ge(S(f"r_done{q}"), i + (before + 1))
                        v.tensor_tensor(x, x, ps[q][:, 0:T].rearrange("p (o t) -> p o t", o=1), ALU.add)\
                            .then_inc(S("r_added"), 1)
                        dve.wait_ge(S("r_added"), i * 2 + (q + 1 + 2 * before))
                        dve.sem_inc(S(f"r_free{q}"), 1)
                        dve.wait_ge(S("r_sq"), i * 2 + (q + 1 + 2 * before))
                        v.tensor_tensor(ss, ss, sq, ALU.add).then_inc(S("r_ss"), 1)
                        dve.wait_ge(S("r_ss"), i * 2 + (q + 1 + 2 * before))
                rounds(dve, 4, body)

            dve.wait_ge(S("x_again"), 16 * KD)
            residual(0, nSQ, nSS)
            dve.wait_ge(S("norm_rs"), 2)
            for k in range(KD):
                v.scalar_tensor_tensor(H[:, k, :], X[:, k, :], pc("norm_ffn", k), nRS, ALU.mult, ALU.mult)\
                    .then_inc(S("n2_h"), 1)

            dve.wait_ge(S("fpar_in"), 32)

            def u_round(i):
                for q in range(2):
                    c = i * 2 + q
                    fp = small[:, 64:72]
                    for half in range(2):
                        dve.wait_ge(S("u_tap"), i * 4 + (2 * q + half + 1))
                        dve.wait_ge(S(f"u_read{half}"), i * 2 + (q + 1))
                        y, x = V[:, half], ps[half][:, 0:T]
                        w0, w1 = fp[:, 4 * half:4 * half + 1], fp[:, 4 * half + 1:4 * half + 2]
                        ys = y[:, SEQ:T].rearrange("p (b t) -> p b t", b=DB)
                        xs = x[:, SEQ:T].rearrange("p (b t) -> p b t", b=DB)
                        fh = (FH[:, c, half] if isinstance(i, int) else
                              FH[:, ds(c, 1), half].rearrange("p o b t -> p (o b) t"))
                        link(v.scalar_tensor_tensor(y[:, 1:SEQ], x[:, 0:SEQ - 1], w1, y[:, 1:SEQ], ALU.mult, ALU.add),
                             v.scalar_tensor_tensor(ys[:, :, 1:], xs[:, :, 0:3], w1, ys[:, :, 1:], ALU.mult, ALU.add),
                             v.scalar_tensor_tensor(ys[:, :, 0:1], fh[:, :, 1:2], w1, ys[:, :, 0:1], ALU.mult,
                                                    ALU.add))
                        link(v.scalar_tensor_tensor(y[:, 2:SEQ], x[:, 0:SEQ - 2], w0, y[:, 2:SEQ], ALU.mult, ALU.add),
                             v.scalar_tensor_tensor(ys[:, :, 2:], xs[:, :, 0:2], w0, ys[:, :, 2:], ALU.mult, ALU.add),
                             v.scalar_tensor_tensor(ys[:, :, 0:2], fh, w0, ys[:, :, 0:2], ALU.mult, ALU.add))
                        dve.sem_inc(S(f"u_free{half}"), 1)
                    dve.wait_ge(S("u_gelu"), i * 2 + (q + 1))
                    dst = G[:, c:c + 1, :] if isinstance(i, int) else G[:, ds(c, 1), :]
                    v.tensor_tensor(dst, V[:, 0].rearrange("p (o t) -> p o t", o=1),
                                    V[:, 1].rearrange("p (o t) -> p o t", o=1), ALU.mult).then_inc(S("g_ready"), 1)
            link.rounds(11, u_round)

            dve.wait_ge(S("g_ready"), NF)
            residual(4, dSQ, dSS)
            dve.wait_ge(S("norm_rs"), 3)
            for k in list(range(1, KD)) + [0]:
                if k == 0:
                    dve.wait_ge(S("n3_h"), KD - 1)
                v.scalar_tensor_tensor(H[:, k, :], X[:, k, :], pc("norm_ple", k), dRS, ALU.mult, ALU.mult)\
                    .then_inc(S("n3_h"), 1)

            def p_round(i):
                for q in range(2):
                    c = i * 2 + q
                    dve.wait_ge(S("p_gfree"), i * 2 + (q + 1))
                    dve.wait_ge(S(f"p_done{q}"), i + 1)
                    v.tensor_tensor(sigp[:, q], sigp[:, q], ps[1][:, 0:T], ALU.mult).then_inc(S("p_efree"), 1)
                    dve.wait_ge(S("p_efree"), i * 2 + (q + 1))
                    wait_prior(dve, S(f"y_out{q}"), i * 16)
                    x = X[:, c:c + 1, :] if isinstance(i, int) else X[:, ds(c, 1), :]
                    v.tensor_tensor(yout[:, q:q + 1, :], x, sigp[:, q:q + 1, :], ALU.add).then_inc(S("y_ready"), 1)
            rounds(dve, 4, p_round)

        @block.gpsimd
        def _(pool):
            for i in range(2):
                if i:
                    pool.wait_ge(S("cd_ready"), 3)
                pool.dma_start(dE[:, HIST + SEQ:EXT].rearrange("p (b t) -> p b t", b=DB)[:, :, 0:HIST],
                                   a["phist"][i]).then_inc(S("pool_in"), 16)

            pool.wait_ge(S("cd_over"), 1)
            for s in range(2):
                pool.dma_start(gw[:, s], a["wge"][s]).then_inc(S(f"gw_in{s}"), 16)

            def gates_out(i, more):
                for s in range(2):
                    for part in range(3):
                        m = 3 * s + part
                        pool.wait_ge(S("gate_out"), i * 6 + (m + 1))
                        pool.dma_start(gates[ds(i * 2 + s, 1), :, part * PART:part * PART + PART].rearrange(
                            "o p t -> (o p) t"), gstage[:, m % 2]).then_inc(S(f"gate_stored{m % 2}"), 16)
                    if more:
                        pool.dma_start(gw[:, s], a["wge"][ds(i * 2 + (s + 2), 1)].rearrange("o p k m -> (o p) k m"))\
                            .then_inc(S(f"gw_in{s}"), 16)
            rounds(pool, UNITS // 2 - 1, lambda i: gates_out(i, True))
            gates_out(UNITS // 2 - 1, False)

            def y_round(i):
                for q in range(2):
                    pool.wait_ge(S("y_ready"), i * 2 + (q + 1))
                    dst = (o["y"][i * 2 + q] if isinstance(i, int) else
                           o["y"][ds(i * 2 + q, 1)].rearrange("o p t -> (o p) t"))
                    pool.dma_start(dst, yout[:, q]).then_inc(S(f"y_out{q}"), 16)
            rounds(pool, 4, y_round)


_OUTS = [("y", (KD, P, T)), ("k_cm", (P, 2, T)), ("v_p", (P, NCH, HW)), ("v_s", (NS, HW)),
         ("hgrn_p", (2, P, P)), ("hgrn_s", (2, P, DB, P)), ("h_p", (P, 2)), ("h_s", (P, 2, DB)),
         ("convc_p", (P, 2, 3)), ("convc_s", (2, P, DB, 3)), ("pool_p", (P, 2, HIST)), ("pool_s", (2, P, DB, HIST)),
         ("ffn_out", (P, NF, 2, 18))]


def constants():
    con = np.zeros((P, NCON), np.float32)

    def put(name, x):
        con[:x.shape[0], CON[name]:CON[name] + x.shape[1]] = x
    i = np.arange(P)
    head = i // HD
    put("ident", np.eye(P))
    put("mean", np.full((P, P), 1.0 / D))
    put("headmean", (head[:, None] == head[None]) / HD)
    put("bd", head[:, None] == head[None])
    put("strict", i[None] < i[:, None])
    put("notstrict", i[None] >= i[:, None])
    j = np.arange(NS)
    new = (i[:, None] // 16 == j[None] // DL) & (j[None] % DL < i[:, None] % DL)
    put("newkeys", new)
    put("notnewkeys", ~new)
    win = np.array([[2, 8], [4, 16]])[head]
    put("invw", 1.0 / win)
    t = np.arange(HIST)
    for k in range(2):
        con[:, CON["corr"] + k * HIST:CON["corr"] + (k + 1) * HIST] = \
            win[:, k:k + 1] / np.minimum(t[None] + 1, win[:, k:k + 1])
    put("batch", j[:, None] // DL == np.arange(DB)[None])
    masks = np.zeros((P, NL, P), np.int32)
    s, t = i[:, None], i[None]
    for n, m in enumerate(LEVELS):
        masks[:, n] = (s // (2 * m) == t // (2 * m)) & (s % (2 * m) < m) & (t % (2 * m) >= m)
    masks[:, NL - 1] = s == t
    return con, masks, np.ascontiguousarray(masks[:NS, 5:8, :NS])


def kernel(**inputs):
    import concourse.bacc as bacc
    from concourse.bass_utils import run_bass_kernel_spmd

    x = {k: np.asarray(v) for k, v in inputs.items()}

    def tokens(p, s):
        y = np.concatenate([p.reshape(SEQ, -1), s.reshape(NS, -1)], 0).T
        return y.reshape(-1, P, T)

    def weights(w):
        k, m = w.shape
        return w.reshape(k // P, P, m // P, P).transpose(2, 1, 0, 3)

    def cols(w):
        return w.reshape(-1, P).T

    w_in = x["w_in"][0]
    wz = np.concatenate([w_in[:, c:c + 256] for c in Z_COLS], 1)
    wg = w_in[:, 2560:].reshape(KD, P, 4, 4, 2, P).transpose(3, 1, 4, 2, 0, 5).reshape(4, P, 8, KD, P)
    wb = x["w_branch"][0].reshape(4, 2, P, KD, P).transpose(3, 2, 0, 1, 4)
    wvi = np.concatenate([w_in[:, 512:768], w_in[:, 1280:1536]], 1).reshape(KD, P, 512).transpose(1, 0, 2)

    def blockdiag(w):
        y = np.zeros((P, 2, P), w.dtype)
        for h in range(4):
            r = (h % 2) * HD
            y[r:r + HD, h // 2, r:r + HD] = w[h]
        return y

    wrg = np.stack([blockdiag(x["w_rg_a"][0]), blockdiag(x["w_rg_x"][0])], 2)
    par = np.zeros((P, NPAR), np.float32)

    def put(name, v):
        par[:, PAR[name]:PAR[name] + v.shape[1]] = v
    for name in ("norm_mix", "norm_ffn", "norm_ple", "conv_c_b", "b_rg_a", "b_rg_x", "lam", "pool_scale"):
        put(name, cols(x[name][0]))
    put("conv_c_w", cols(x["conv_c_w"][0]))
    for name in ("q_norm", "k_norm", "hgrn_norm"):
        put(name, np.tile(x[name][0], 2)[:, None])
    put("sb_head", np.broadcast_to(x["sb_bias"][0], (P, NH)))
    put("sb_row", x["sb_bias"][0][(np.arange(P) % 16) // 4][:, None])
    cw = x["conv_f_w"][0].reshape(3, 2, NF, P)
    fpar = np.concatenate([cw, x["conv_f_b"][0].reshape(1, 2, NF, P)], 0).transpose(3, 2, 1, 0).reshape(P, NF, 8)
    fhist = x["state_ffn_conv"][0].reshape(DB, 2, 2, NF, P).transpose(4, 3, 2, 0, 1)
    s0 = np.zeros((P, 2, DB, P), np.float32)
    for h in range(4):
        r = (h % 2) * HD
        s0[r:r + HD, h // 2, :, r:r + HD] = x["state_hgrn"][0][:, h].transpose(1, 0, 2)
    con, masks, smasks = constants()
    arrays = {
        "x": tokens(x["x_prompt"], x["x_sample"]),
        "wz": weights(wz), "wge": wg[:, :, 0:EARLY].transpose(0, 2, 1, 3, 4).reshape(UNITS, P, KD, P),
        "wgl": wg[:, :, EARLY:], "wb": wb, "wvi": wvi, "wrg": wrg, "wpool": blockdiag(x["w_pool"][0]),
        "wo": weights(x["w_out"][0]),
        "wu": x["w_up"][0].reshape(KD, P, 2, NF, P).transpose(3, 1, 2, 0, 4),
        "wd": weights(x["w_down"][0]), "wpg": weights(x["w_ple_gate"][0]), "wpl": weights(x["w_ple"][0]),
        "pe": tokens(x["p_prompt"][0], x["p_sample"][0]),
        "par": par, "fpar": fpar, "fhist": fhist, "con": con, "masks": masks, "smasks": smasks,
        "chist": x["state_rglru_conv"][0].reshape(DB, 3, 2, P).transpose(3, 2, 0, 1),
        "ch0": x["state_rglru_h"][0].reshape(DB, 2, P).transpose(2, 1, 0),
        "phist": x["state_pool"][0].reshape(DB, HIST, 2, P).transpose(2, 3, 0, 1),
        "s0": s0,
        "ck": x["cache_k"][0].reshape(-1, P, 2, P).transpose(0, 3, 2, 1),
        "cv": x["cache_v"][0].reshape(-1, P, HW),
        "pt": x["page_table"],
    }
    nc = bacc.Bacc("TRN2", target_bir_lowering=False, num_devices=1)
    arrays = {f"in_{k}": np.ascontiguousarray(v) for k, v in arrays.items()}
    ins = {k[3:]: nc.dram_tensor(k, v.shape, mybir.dt.from_np(v.dtype), kind="ExternalInput").ap()
           for k, v in arrays.items()}
    outs = {n: nc.dram_tensor(f"out_{n}", s, F32, kind="ExternalOutput").ap() for n, s in _OUTS}
    program(nc, ins, outs)
    got = run_bass_kernel_spmd(nc, [arrays], core_ids=[0]).results[0]
    g = {n: np.asarray(got[f"out_{n}"]) for n, _ in _OUTS}

    y = g["y"].reshape(D, T).T
    k = g["k_cm"].transpose(2, 1, 0).reshape(T, NH, HD)

    def heads(s):
        return [s[h // 2][(h % 2) * HD:(h % 2) * HD + HD, ..., (h % 2) * HD:(h % 2) * HD + HD] for h in range(4)]

    fo = g["ffn_out"].transpose(3, 2, 1, 0).reshape(18, 2 * FF)
    c = np.ascontiguousarray
    return (c(y[:SEQ].reshape(1, SEQ, D)), c(y[SEQ:].reshape(DB, DL, D)),
            c(k[:SEQ].reshape(1, 1, SEQ, NH, HD)),
            c(g["v_p"].transpose(1, 0, 2).reshape(1, 1, SEQ, NH, HD)),
            c(k[SEQ:].reshape(1, DB, DL, NH, HD)), c(g["v_s"].reshape(1, DB, DL, NH, HD)),
            c(np.stack(heads(g["hgrn_p"]))[None, None]),
            c(np.stack(heads(g["hgrn_s"])).transpose(2, 0, 1, 3)[None]),
            c(g["h_p"].T.reshape(1, 1, HW)), c(g["h_s"].transpose(2, 1, 0).reshape(1, DB, HW)),
            c(g["convc_p"].transpose(2, 1, 0).reshape(1, 1, 3, HW)),
            c(g["convc_s"].transpose(2, 3, 0, 1).reshape(1, DB, 3, HW)),
            c(g["pool_p"].transpose(2, 1, 0).reshape(1, 1, HIST, HW)),
            c(g["pool_s"].transpose(2, 3, 0, 1).reshape(1, DB, HIST, HW)),
            c(fo[:2].reshape(1, 1, 2, 2 * FF)), c(fo[2:].reshape(1, DB, 2, 2 * FF)))
```

```python
from contextlib import ExitStack

import numpy as np

import concourse.bass as bass
from concourse import mybir

F32 = mybir.dt.float32
F32R = mybir.dt.float32r
I32 = mybir.dt.int32
ALU = mybir.AluOpType
ACT = mybir.ActivationFunctionType
ds = bass.ds

P = 128
D = 1024
SEQ = 1024
DB, DL = 8, 4
NS = DB * DL
T = SEQ + NS
KD = D // P
HW = D // 4
HD = 64
NH = 4
PAGES = 4
PAST = PAGES * P
FF = 2816
NF = FF // P
DPLE = 256
KP = DPLE // P
EPS = 1e-6
CH = 128
NCH = SEQ // CH
SPANS = ((0, 512), (512, 512), (1024, NS))
HIST = 15
EXT = HIST + SEQ + DB * (HIST + DL)
XC, FB, QB, KA, XD, GC, GB, QA = range(0, 16, 2)
Z_COLS = (1792, 1024, 768, 256, 2304, 2048, 1536, 0)
BRANCH_AT = (QA, GB, GC, XD)
LEVELS = (64, 32, 16, 8, 4, 2, 1)
NL = len(LEVELS) + 1


def table(*entries):
    at, n = {}, 0
    for name, width in entries:
        at[name] = n
        n += width
    return at, n


PAR, NPAR = table(("norm_mix", KD), ("norm_ffn", KD), ("norm_ple", KD), ("conv_c_w", 8), ("conv_c_b", 2),
                  ("b_rg_a", 2), ("b_rg_x", 2), ("lam", 2), ("pool_scale", 2), ("q_norm", 1), ("k_norm", 1),
                  ("hgrn_norm", 1), ("sb_head", NH), ("sb_row", 1))
CON, NCON = table(("ident", P), ("mean", P), ("headmean", P), ("bd", P), ("strict", P), ("notstrict", P),
                  ("newkeys", NS), ("notnewkeys", NS), ("invw", 2), ("corr", 2 * HIST), ("batch", DB))
NR = 23500
EARLY = 3
LATE = 8 - EARLY
PART = T // 3
UNITS = 4 * EARLY
PLACES = (("start0", 4), ("states0", 3), ("levels0", 3), ("start1", 2), ("states1", 3), ("levels1", 3),
          ("norms", 1), ("normed", 2), ("steps", 8), ("samples", 7))


def parts(place):
    first = 0
    for name, n in PLACES:
        if name == place:
            return range(first, first + n)
        first += n
    assert False, place


assert sum(n for _, n in PLACES) == 3 * UNITS


class Link:

    def __init__(self, eng, sem):
        self.eng, self.sem, self.base, self.n = eng, sem, 0, 0

    def __call__(self, *inss):
        for ins in inss:
            ins.then_inc(self.sem, 1)
            self.n += 1
        self.eng.wait_ge(self.sem, self.base + self.n)

    def rounds(self, times, body):
        first = self.n
        body(0)
        per = self.n - first
        with self.eng.Fori(1, times) as i:
            self.base, self.n = i * per, first
            body(i)
            assert self.n == first + per
        self.base, self.n = 0, first + times * per


def rounds(eng, times, body):
    body(0)
    with eng.Fori(1, times) as i:
        body(i)


def wait_prior(eng, sem, value):
    if not isinstance(value, int) or value > 0:
        eng.wait_ge(sem, value)


def program(nc, a, o):
    with ExitStack() as ctx:
        def sb(name, shape, dt=F32):
            return ctx.enter_context(nc.sbuf_tensor(name, shape, dt))

        sems = {}

        def S(name):
            if name not in sems:
                sems[name] = ctx.enter_context(nc.semaphore(name))
            return sems[name]

        par = sb("par", [P, NPAR])
        con = sb("con", [P, NCON])
        masks = sb("masks", [P, NL, P], I32)
        smasks = sb("smasks", [NS, 3, NS], I32)
        fpar = sb("fpar", [P, NF, 8])
        small = sb("small", [P, 96])
        arena_at = -(-nc.sbuf_base // 32) * 32
        H = sb("H", [P, KD, T])
        BIG = sb("BIG", [P, 16 * T + NR])
        assert nc.sbuf_base == arena_at + 4 * (24 * T + NR)
        FH = sb("FH", [P, NF, 2, DB, 2])
        FO = sb("FO", [P, NF, 2, 18])
        Z = BIG[:, 0:16 * T].rearrange("p (c t) -> p c t", c=16)
        R0 = 16 * T
        ps = [ctx.enter_context(nc.psum_tensor(f"ps{s}", [P, 1536], F32)) for s in range(2)]
        pst = [ctx.enter_context(nc.psum_tensor(f"pst{s}", [P, 512], F32)) for s in range(2)]
        gbank = ps[1][:, 1024:1024 + PART]
        gates = nc.dram_tensor("gates", (UNITS, P, T), F32, kind="Internal").ap()

        def rounded(name, word, *shape):
            at = arena_at + 4 * (8 * T + word)
            return nc.alloc_sbuf_tensor_at(name, [P, *shape], F32R, offset=at, align_bytes=32)[:]

        def pc(name, j=0, n=1):
            return par[:, PAR[name] + j:PAR[name] + j + n]

        def cc(name, n=P, j=0, p=P):
            return con[0:p, CON[name] + j:CON[name] + j + n]

        class Region:

            def __init__(self, at=0):
                self.at = R0 + at

            def take(self, *shape):
                n = 1
                for s in shape:
                    n *= s
                v = BIG[:, self.at:self.at + n]
                self.at += n
                assert self.at <= R0 + NR, self.at - R0
                names = "abcd"[:len(shape)]
                if len(shape) > 1:
                    v = v.rearrange(f"p ({' '.join(names)}) -> p {' '.join(names)}",
                                    **{x: s for x, s in zip(names, shape)})
                return v

        r = Region()
        VT = r.take(NCH + 1, 512)
        base = r.at - R0
        zw = r.take(2, KD, P)
        wvi = r.take(KD, 512)
        wrg = r.take(2, 2, P)
        wpool = r.take(2, P)
        chist = r.take(2, DB, 3)
        ch0 = r.take(2, DB)
        at = r.at - R0
        SS, RS, SQ = r.take(T), r.take(T), r.take(2, T)
        r = Region(at)
        cX, cR, cI = r.take(2, T), r.take(2, T), r.take(2, T)
        cA, cB = r.take(T), r.take(T)
        cext = r.take(DB, 7)
        dE, dF = r.take(EXT), r.take(EXT)
        xin = Z[:, 8:16, :]
        r = Region(base)
        bB = r.take(2, T)
        KF, QF = r.take(2, T), [r.take(2, T), r.take(2, T)]
        QE = r.take(T)
        kdt = Region(r.at - R0).take(NCH + 1, P)
        att = r.take(NCH, 2, P)
        atts = r.take(2, NS)
        Sall = r.take(NCH + 1, P)
        S0 = r.take(2, DB, P)
        vbd = r.take(DB, P)
        bdec = r.take(16)
        assert r.at <= R0 + NR - 2 * KD * P - 2 * PART
        tA = Z[:, XC:XC + 2, :]
        bd_, bE = Z[:, XC, :], Z[:, XC + 1, :]
        rmask = QE
        r = Region(NR - 2 * KD * P - 2 * PART)
        gw = r.take(2, KD, P)
        gstage = r.take(2, PART)
        r = Region(base)
        keep, beta, Pp = r.take(2, SEQ), r.take(2, SEQ), r.take(2, SEQ + 8)
        wT = r.take(2, SEQ)
        QS = r.take(2, 1152)
        QSall = r.take(2, P)
        pages = r.take(5, PAST * 2)
        negb = r.take(8)
        assert r.at <= R0 + NR - 2 * KD * P - 2 * PART
        qm = Z[:, FB:FB + 4, :]
        kp = [x.rearrange("p (g i t) -> p g i t", g=PAGES, i=2) for x in
              (pages[:, 0], pages[:, 1], Z[:, XC, 0:PAST * 2], Z[:, XC + 1, 0:PAST * 2])]
        vp = [x.rearrange("p (g c) -> p g c", g=PAGES) for x in
              (*(pages[:, 2 + b] for b in range(3)), *(qm[:, h, 0:PAST * 2] for h in range(NH)), keep[:, 1])]
        r = Region()
        MIX = r.take(KD, T)
        at = r.at - R0
        mwg = r.take(LATE, KD, P)
        early = r.take(EARLY, T)
        mwb = r.take(2, 4, 2, P)
        SIG = r.take(2, T)
        ACC, TMP = r.take(T), r.take(T)
        X = Z[:, 0:KD, :]
        r = Region(at)
        ow = r.take(2, KD, P)
        nSQ, nSS, nRS, ntmp = r.take(T), r.take(T), r.take(T), r.take(2, T)
        uraw = r.take(2, KD, P)
        Uh = rounded("Uh", r.at, 2, KD, P)
        Ul = rounded("Ul", r.at + 2 * KD * P, 2, KD, P)
        assert r.at + 4 * KD * P <= R0 + NR
        Hh, Hl = rounded("Hh", -8 * T, KD, T), rounded("Hl", 8 * T, KD, T)
        Gh, Gl = rounded("Gh", R0, 2, T), rounded("Gl", R0 + 2 * T, 2, T)
        Dh, Dl = rounded("Dh", R0 + 4 * T, 2, KD, P), rounded("Dl", R0 + 4 * T + 2 * KD * P, 2, KD, P)
        assert 4 * T + 4 * KD * P <= at
        draw = Region(at).take(2, KD, P)
        V = Region(at + 2 * KD * P).take(2, T)
        dSQ, dSS, dRS = ntmp[:, 0], ntmp[:, 1], nRS
        r = Region()
        pw = r.take(2, KD, P)
        pv = r.take(2, KP, P)
        pe_ = r.take(KP, T)
        sigp = r.take(2, T)
        yout = r.take(2, T)


        def m_slot(u):
            return u % 2 if u < EARLY else 1

        block = ctx.enter_context(nc.Block())

        @block.sync
        def _(sp):
            sp.dma_start(par[:], a["par"]).then_inc(S("params_in"), 16)
            sp.dma_start(con[:], a["con"]).then_inc(S("params_in"), 16)
            for k in range(KD):
                sp.dma_start(xin[:, k, :], a["x"][k]).then_inc(S(f"x_in{k // 2}"), 16)
            for s in range(2):
                sp.dma_start(zw[:, s], a["wz"][s]).then_inc(S(f"zw_in{s}"), 16)
            sp.dma_start(wrg, a["wrg"]).then_inc(S("cd_in"), 16)
            sp.dma_start(wpool, a["wpool"]).then_inc(S("cd_in"), 16)
            sp.dma_start(chist, a["chist"]).then_inc(S("cd_in"), 16)
            sp.dma_start(ch0, a["ch0"]).then_inc(S("cd_in"), 16)
            sp.dma_start(wvi, a["wvi"]).then_inc(S("wvi_in"), 16)
            sp.dma_start(masks[:], a["masks"]).then_inc(S("tables_in"), 16)
            sp.dma_start(smasks[:], a["smasks"]).then_inc(S("tables_in"), 16)
            sp.dma_start(fpar[:], a["fpar"]).then_inc(S("tables_in"), 16)
            sp.dma_start(FH[:], a["fhist"]).then_inc(S("tables_in"), 16)

            with sp.Fori(1, 8) as i:
                for s in range(2):
                    sp.wait_ge(S(f"z_done{s}"), i)
                    sp.dma_start(zw[:, s], a["wz"][ds(i * 2 + s, 1)].rearrange("o p k m -> (o p) k m"))\
                        .then_inc(S(f"zw_in{s}"), 16)
            outs = 0

            def out(name, src, idx=None):
                nonlocal outs
                dst = o[name] if idx is None else o[name][idx]
                sp.dma_start(dst, src).then_inc(S("stored"), 16)
                outs += 16

            for s in range(2):
                sp.wait_ge(S(f"z_free{s}"), 8)
            out("convc_p", Z[:, XC:XC + 2, SEQ - 3:SEQ])
            for i in range(2):
                out("convc_s", Z[:, XC + i, SEQ:T].rearrange("p (b t) -> p b t", b=DB)[:, :, 1:4], i)
                sp.dma_start(o["pool_s"][i][:, :, HIST - DL:], Z[:, XD + i, SEQ:T].rearrange("p (b t) -> p b t", b=DB))\
                    .then_inc(S("stored"), 16)
                sp.dma_start(o["pool_s"][i][:, :, 0:HIST - DL], a["phist"][i][:, :, DL:]).then_inc(S("stored"), 16)
                outs += 32
            out("pool_p", Z[:, XD:XD + 2, SEQ - HIST:SEQ])
            sp.wait_ge(S("stored"), outs)
            sp.sem_inc(S("raw_stored"), 1)
            sp.wait_ge(S("vt_free"), NCH + 1)
            out("v_p", VT[:, 0:NCH, 0:HW])
            out("v_s", VT[0:NS, NCH, 0:HW])
            sp.wait_ge(S("c_scanned"), 2)
            sp.wait_ge(S("c_out"), 2)
            out("h_p", small[:, 40:42])
            out("h_s", small[:, 48:64].rearrange("p (i b) -> p i b", i=2))
            sp.wait_ge(S("cd_over"), 1)
            sp.dma_start(S0[:], a["s0"]).then_inc(S("s0_in"), 16)
            for i in range(2):
                sp.wait_ge(S("b_states"), i + 1)
                out("hgrn_p", Sall[:, NCH, :], i)
                out("hgrn_s", vbd, i)
                sp.wait_ge(S("stored"), outs)
                sp.sem_inc(S("states_stored"), 1)
            sp.wait_ge(S("a_kq"), 2)
            out("k_cm", Z[:, KA:KA + 2, :])
            sp.wait_ge(S("b_over"), 2)
            for b in range(DB):
                if b == 3:
                    sp.wait_ge(S("a_sc"), 32)
                if b >= 4:
                    sp.wait_ge(S("kp_used"), b - 3)
                if b == 7:
                    sp.wait_ge(S("a_w"), 32)
                for g in range(PAGES):
                    page = sp.value_load(a["pt"][b:b + 1, g:g + 1], min_val=0, max_val=39)
                    sp.dma_start(kp[b % 4][:, g], a["ck"][ds(page, 1)].rearrange("o p i t -> (o p) i t"))\
                        .then_inc(S(f"pages_in{b % 4}"), 16)
                    sp.dma_start(vp[b][:, g], a["cv"][ds(page, 1)].rearrange("o p c -> (o p) c"))\
                        .then_inc(S(f"pages_in{b % 4}"), 16)

            sp.wait_ge(S("a_over"), 2)
            sp.wait_ge(S("stored"), outs)
            for s in range(2):
                sp.wait_ge(S(f"gate_stored{s}"), 16 * 3 * UNITS // 2)

            def pieces(x):
                return x.rearrange("o p n k m -> (o p) n k m")
            sp.dma_start(mwb[:, 0], a["wb"][0]).then_inc(S("mw_in0"), 16)
            sp.dma_start(early, gates[0:EARLY].rearrange("n p t -> p n t")).then_inc(S("mw_in0"), 16)
            sp.dma_start(mwg[:, 0:2], a["wgl"][0][:, 0:2]).then_inc(S("mw_in1"), 16)
            sp.dma_start(mwb[:, 1], a["wb"][1]).then_inc(S("mw_in1"), 16)
            sp.dma_start(mwg[:, 2:LATE], a["wgl"][0][:, 2:LATE]).then_inc(S("mw_in2"), 16)
            for k in range(KD):
                sp.dma_start(X[:, k, :], a["x"][k]).then_inc(S("x_again"), 16)
            with sp.Fori(1, 4) as i:
                sp.wait_ge(S("m_proj"), i * 8 - 4)
                sp.dma_start(mwb[:, 0], pieces(a["wb"][ds(i * 2, 1)])).then_inc(S("mw_in0"), 16)
                sp.wait_ge(S("m_sig"), i * 8 + (EARLY - 8))
                sp.dma_start(early, gates[ds(i * EARLY, EARLY)].rearrange("n p t -> p n t")).then_inc(S("mw_in0"), 16)
                sp.wait_ge(S("m_gate"), i * LATE + (2 - LATE))
                sp.dma_start(mwg[:, 0:2], pieces(a["wgl"][ds(i, 1), :, 0:2])).then_inc(S("mw_in1"), 16)
                sp.wait_ge(S("m_gate"), i * LATE)
                sp.dma_start(mwg[:, 2:LATE], pieces(a["wgl"][ds(i, 1), :, 2:LATE])).then_inc(S("mw_in2"), 16)
                sp.wait_ge(S("m_proj"), i * 8)
                sp.dma_start(mwb[:, 1], pieces(a["wb"][ds(i * 2 + 1, 1)])).then_inc(S("mw_in1"), 16)

            for q in range(2):
                sp.wait_ge(S("mix_ready"), 8)
                sp.dma_start(ow[:, q], a["wo"][q]).then_inc(S(f"rw_in{q}"), 16)

            def up_weights(c):
                for half in range(2):
                    if not isinstance(c, int) or c:
                        sp.wait_ge(S("u_lo"), c * 2 + (half - 1))
                    src = a["wu"][c, :, half] if isinstance(c, int) else \
                        a["wu"][ds(c, 1), :, half].rearrange("o p k m -> (o p) k m")
                    sp.dma_start(uraw[:, half], src).then_inc(S(f"uw_in{half}"), 16)
            up_weights(0)
            with sp.Fori(1, 4) as i:
                for q in range(2):
                    sp.wait_ge(S(f"r_done{q}"), i)
                    sp.dma_start(ow[:, q], a["wo"][ds(i * 2 + q, 1)].rearrange("o p k m -> (o p) k m"))\
                        .then_inc(S(f"rw_in{q}"), 16)
            up_weights(1)
            sp.wait_ge(S("n2_h"), 8)
            sp.dma_start(draw, a["wd"][0]).then_inc(S("d_in"), 16)
            with sp.Fori(1, 11) as i:
                up_weights(i * 2)
                sp.wait_ge(S("d_lo"), i)
                sp.dma_start(draw, a["wd"][ds(i, 1)].rearrange("o p k d m -> (o p) k d m")).then_inc(S("d_in"), 16)
                up_weights(i * 2 + 1)
            sp.wait_ge(S("d_added"), 88)
            out("ffn_out", FO[:])
            for k in range(KP):
                sp.dma_start(pe_[:, k, :], a["pe"][k]).then_inc(S("pe_in"), 16)
            for q in range(2):
                sp.dma_start(pw[:, q], a["wpg"][q]).then_inc(S(f"pw_in{q}"), 16)
                sp.dma_start(pv[:, q], a["wpl"][q]).then_inc(S(f"pw_in{q}"), 16)
            with sp.Fori(1, 4) as i:
                for q in range(2):
                    sp.wait_ge(S(f"p_done{q}"), i)
                    sp.dma_start(pw[:, q], a["wpg"][ds(i * 2 + q, 1)].rearrange("o p k m -> (o p) k m"))\
                        .then_inc(S(f"pw_in{q}"), 16)
                    sp.dma_start(pv[:, q], a["wpl"][ds(i * 2 + q, 1)].rearrange("o p k m -> (o p) k m"))\
                        .then_inc(S(f"pw_in{q}"), 16)
            sp.wait_ge(S("stored"), outs)
            sp.wait_ge(S("y_out0"), 64)
            sp.wait_ge(S("y_out1"), 64)

        @block.tensor
        def _(pe):
            def dense(out, w, rhs, kk, first=True, last=True):
                ins = None
                for k in range(kk):
                    for t0, n in SPANS:
                        ins = nc.tensor.matmul(out[:, t0:t0 + n], w[:, k], rhs[:, k, t0:t0 + n],
                                               start=first and k == 0, stop=last and k == kk - 1)
                return ins

            def whole(out, w, rhs):
                ins = None
                for t0, n in SPANS:
                    ins = nc.tensor.matmul(out[:, t0:t0 + n], w, rhs[:, t0:t0 + n], start=True, stop=True)
                return ins

            def gate(p, halves=(0, 1)):
                u, part = divmod(p, 3)
                if 0 in halves:
                    if part == 0:
                        pe.wait_ge(S(f"gw_in{u % 2}"), 16 * (u // 2 + 1))
                    if p:
                        pe.wait_ge(S("gate_out"), p)
                for k in range(4 * halves[0], 4 * halves[-1] + 4):
                    ins = nc.tensor.matmul(gbank, gw[:, u % 2, k], H[:, k, part * PART:part * PART + PART],
                                           start=(k == 0), stop=(k == KD - 1))
                if 1 in halves:
                    ins.then_inc(S("gate_done"), 1)

            pe.wait_ge(S("params_in"), 32)
            pe.wait_ge(S("n1_ss"), 8)
            whole(ps[0], cc("mean"), SS).then_inc(S("norm_sum"), 1)
            pe.wait_ge(S("n1_h"), 8)

            def z_round(i):
                for s in range(2):
                    pe.wait_ge(S(f"zw_in{s}"), i * 16 + 16)
                    wait_prior(pe, S(f"z_free{s}"), i)
                    dense(ps[s], zw[:, s], H, KD).then_inc(S(f"z_done{s}"), 1)
            rounds(pe, 8, z_round)

            pe.wait_ge(S("cd_in"), 64)
            for s in range(2):
                pe.wait_ge(S(f"z_free{s}"), 8)
            for u, (w, x, ready) in enumerate([(wrg[:, 0, 0], cX[:, 0], 1), (wrg[:, 0, 1], cX[:, 0], 1),
                                               (wrg[:, 1, 0], cX[:, 1], 2), (wrg[:, 1, 1], cX[:, 1], 2),
                                               (wpool[:, 0], Z[:, XD], 3), (wpool[:, 1], Z[:, XD + 1], 4)]):
                pe.wait_ge(S("cd_ready"), ready)
                if u >= 2:
                    pe.wait_ge(S("cd_free"), u - 1)
                whole(ps[u % 2], w, x).then_inc(S("cd_done"), 1)

            pe.wait_ge(S("wvi_in"), 16)
            pe.wait_ge(S("cd_free"), 6)
            for t in range(NCH + 1):
                n = P if t < NCH else NS
                if t >= 2:
                    pe.wait_ge(S("vt_free"), t - 1)
                for k in range(KD):
                    ins = nc.tensor.matmul(ps[t % 2][0:n, 0:512], H[:, k, t * P:t * P + n], wvi[:, k, :],
                                           start=(k == 0), stop=(k == KD - 1))
                ins.then_inc(S("vt_done"), 1)
            pe.wait_ge(S("vt_free"), NCH + 1)

            for i in range(2):
                for p in parts(f"start{i}"):
                    gate(p)
                pe.wait_ge(S("b_kd"), i + 1)
                for g in range(3):
                    n = 3 * i + g
                    if n >= 2:
                        pe.wait_ge(S("b_tfree"), n - 1)
                    for c in range(4 * g, min(4 * g + 4, NCH + 1)):
                        m = P if c < NCH else NS
                        ins = nc.tensor.transpose(pst[n % 2][0:m, (c % 4) * P:(c % 4) * P + P],
                                                  bE[:, c * P:c * P + m], cc("ident"))
                    ins.then_inc(S("b_tdone"), 1)
                pe.wait_ge(S("b_tfree"), 3 * i + 3)
                pe.wait_ge(S("b_vbd"), i + 1)
                if i:
                    pe.wait_ge(S("b_over"), 1)
                for c in range(NCH):
                    ins = nc.tensor.matmul(ps[0][:, c * P:c * P + P], kdt[:, c, :],
                                           VT[:, c, HW + i * P:HW + i * P + P], start=(c % 4 == 0), stop=True,
                                           skip_group_check=True)
                for b in range(2):
                    ins = nc.tensor.matmul(ps[1][:, b * 512:b * 512 + 512], kdt[0:NS, NCH, :],
                                           vbd[0:NS, 4 * b:4 * b + 4, :], start=True, stop=True)
                ins.then_inc(S("b_u"), 1)
                for p in parts(f"states{i}"):
                    gate(p)
                pe.wait_ge(S("b_ufree"), 2 * (i + 1))
                for l in range(NL):
                    n = NL * i + l
                    if 1 <= l <= 6:
                        gate(parts(f"levels{i}")[(l - 1) // 2], ((l - 1) % 2,))
                    pe.wait_ge(S("b_factors"), n + 1)
                    for g in range(4):
                        u = 4 * n + g
                        if g + 4 * l >= 4:
                            pe.wait_ge(S("b_afree"), u - 3)
                        bank = ps[g // 2][:, (g % 2) * 512:(g % 2) * 512 + 512]
                        for j in range(4):
                            c, hh = 2 * g + j // 2, j % 2
                            kf = KF[:, l % 2, c * P:c * P + P] if l < NL - 1 else Z[:, FB + i, c * P:c * P + P]
                            ins = nc.tensor.matmul(bank[:, j * P:j * P + P], kf, QF[hh][:, l % 2, c * P:c * P + P],
                                                   start=(j == 0), stop=True, skip_group_check=True)
                        ins.then_inc(S("b_adone"), 1)
                    if l >= 5:
                        m = 3 * i + l - 5
                        if m >= 1:
                            pe.wait_ge(S("b_sfree"), m)
                        for hh in range(2):
                            kf = KF[:, l % 2, SEQ:T] if l < NL - 1 else Z[:, FB + i, SEQ:T]
                            ins = nc.tensor.matmul(pst[0][0:NS, hh * NS:hh * NS + NS], kf,
                                                   QF[hh][:, l % 2, SEQ:T], start=(hh == 0), stop=True,
                                                   skip_group_check=True)
                        ins.then_inc(S("b_sdone"), 1)
                pe.wait_ge(S("b_afree"), 4 * NL * (i + 1))
                pe.wait_ge(S("b_sfree"), 3 * (i + 1))
                for g in range(4):
                    bank = ps[g // 2][:, (g % 2) * 512:(g % 2) * 512 + 512]
                    first = True
                    for hh in range(2):
                        for c in (2 * g, 2 * g + 1):
                            dst = bank[:, (2 * hh + c % 2) * P:(2 * hh + c % 2) * P + P]
                            if c:
                                nc.tensor.matmul(dst, Sall[:, c, :], QE[:, c * P:c * P + P], start=first,
                                                 stop=False, skip_group_check=True)
                                first = False
                            ins = nc.tensor.matmul(dst, VT[:, c, HW + i * P:HW + i * P + P], att[:, c, hh, :],
                                                   start=first, stop=True, skip_group_check=True)
                            first = False
                ins.then_inc(S("b_odone"), 1)
                pe.wait_ge(S("s0_in"), 16)
                first = True
                for hh in range(2):
                    for b in range(DB):
                        c0 = hh * NS + b * DL
                        nc.tensor.matmul(pst[1][:, c0:c0 + DL], S0[:, i, b, :], QE[:, SEQ + b * DL:SEQ + b * DL + DL],
                                         start=first, stop=False, skip_group_check=True)
                        first = False
                    ins = nc.tensor.matmul(pst[1][:, hh * NS:hh * NS + NS], VT[0:NS, NCH, HW + i * P:HW + i * P + P],
                                           atts[0:NS, hh, :], start=False, stop=True, skip_group_check=True)
                ins.then_inc(S("b_osdone"), 1)
                pe.wait_ge(S("b_osq"), i + 1)
                pe.wait_ge(S("b_ofree"), i + 1)
                whole(ps[0], cc("headmean"), bE).then_inc(S("b_ms"), 1)

            for p in parts("norms"):
                gate(p)
            for j in range(4):
                if j == 1:
                    pe.wait_ge(S("gate_out"), parts("norms")[-1] + 1)
                pe.wait_ge(S("a_sq"), j + 1)
                if j == 0:
                    pe.wait_ge(S("b_over"), 2)
                if j >= 2:
                    pe.wait_ge(S("a_rs"), j - 1)
                whole(ps[j % 2], cc("headmean"), (keep.rearrange("p a b -> p (a b)"), wT.rearrange("p a b -> p (a b)"))[j % 2])\
                    .then_inc(S("a_ms"), 1)
            pe.wait_ge(S("a_rs"), 4)
            for p in parts("normed"):
                gate(p)
            pe.wait_ge(S("a_qm"), 1)
            tgroups = [0]
            for n in range(32):
                tgroups.append(tgroups[-1] + (n // 4 + 4) // 4)

            def scores(n):
                i, h = n // 4, n % 4
                if n >= 2:
                    pe.wait_ge(S("a_scfree"), n - 1)
                w = (i + 1) * P
                for c0 in range(0, w, 512):
                    m = min(512, w - c0)
                    ins = nc.tensor.matmul(ps[n % 2][:, c0:c0 + m], qm[:, h, i * P:i * P + P],
                                           Z[:, KA + h // 2, c0:c0 + m], start=True, stop=True)
                ins.then_inc(S("a_sc"), 1)

            def transposes(n):
                i = n // 4
                pe.wait_ge(S("a_w"), n + 1)
                for g in range(tgroups[n], tgroups[n + 1]):
                    if g >= 2:
                        pe.wait_ge(S("a_tfree"), g - 1)
                    j0 = 4 * (g - tgroups[n])
                    for j in range(j0, min(j0 + 4, i + 1)):
                        ins = nc.tensor.transpose(pst[g % 2][:, (j - j0) * P:(j - j0) * P + P],
                                                  beta[:, n % 2, j * P:j * P + P], cc("ident"))
                    ins.then_inc(S("a_tdone"), 1)

            def values(n):
                i, h = n // 4, n % 4
                pe.wait_ge(S("a_tfree"), tgroups[n + 1])
                if h == 0 and i >= 1:
                    pe.wait_ge(S("a_ofree"), i)
                for j in range(i + 1):
                    ins = nc.tensor.matmul(ps[0][:, 1024 + h * P:1024 + h * P + P],
                                           VT[:, j, (h // 2) * P:(h // 2) * P + P], wT[:, n % 2, j * P:j * P + P],
                                           start=(h == 0 and j == 0), stop=(j == i), skip_group_check=True)
                ins.then_inc(S("a_pv"), 1)

            for n in range(34):
                if n < 32:
                    scores(n)
                    if n % 4 == 1:
                        gate(parts("steps")[n // 4])
                if 1 <= n <= 32:
                    transposes(n - 1)
                if n >= 2:
                    values(n - 2)
            pe.wait_ge(S("a_scfree"), 32)
            pe.wait_ge(S("a_qs"), 1)
            for b in range(DB):
                if b:
                    gate(parts("samples")[b - 1])
                pe.wait_ge(S(f"pages_in{b % 4}"), 32 * PAGES * (b // 4 + 1))
                for i in range(2):
                    ins = nc.tensor.matmul(ps[0][:, 0:PAST], QS[:, i, b * P:b * P + P], kp[b % 4][:, :, i, :],
                                           start=(b == 0 and i == 0), stop=(b == DB - 1 and i == 1))
                ins.then_inc(S("kp_used"), 1)
            for i in range(2):
                ins = nc.tensor.matmul(ps[0][:, PAST:PAST + NS], QSall[:, i, :], Z[:, KA + i, SEQ:T],
                                       start=(i == 0), stop=(i == 1))
            ins.then_inc(S("as_sc"), 1)
            pe.wait_ge(S("as_w"), 1)
            for j in range(PAGES):
                ins = nc.tensor.transpose(pst[0][:, j * P:j * P + P], beta[:, 0, j * P:j * P + P], cc("ident"))
            ins = nc.tensor.transpose(pst[1][0:NS, 0:P], beta[:, 0, PAST:PAST + NS], cc("ident"))
            ins.then_inc(S("as_t"), 1)
            pe.wait_ge(S("as_tfree"), 2)
            for i in range(2):
                nc.tensor.matmul(ps[1][:, i * P:i * P + P], VT[0:NS, NCH, i * P:i * P + P], wT[0:NS, 1, 0:P],
                                 start=(i == 0), stop=False, skip_group_check=True)
            for b in range(DB):
                for i in range(2):
                    for g in range(PAGES):
                        ins = nc.tensor.matmul(ps[1][:, i * P + 16 * b:i * P + 16 * b + 16],
                                               vp[b][:, g, i * P:i * P + P],
                                               wT[:, 0, g * P + 16 * b:g * P + 16 * b + 16],
                                               start=False, stop=(g == PAGES - 1), skip_group_check=True)
                ins.then_inc(S("vp_used"), 1)
            pe.wait_ge(S("a_over"), 2)

            def m_round(i):
                for u in range(8):
                    q, n = divmod(u, 4)
                    if u in (0, EARLY, EARLY + 2):
                        w = {0: 0, EARLY: 1, EARLY + 2: 2}[u]
                        pe.wait_ge(S(f"mw_in{w}"), (i + 1) * (16 if w == 2 else 32))
                    if u >= EARLY:
                        if u == EARLY:
                            pe.wait_ge(S("m_pfree"), i * 8 + EARLY)
                        else:
                            pe.wait_ge(S("m_sig"), i * 8 + u)
                        dense(ps[0], mwg[:, u - EARLY], H, KD).then_inc(S("m_gate"), 1)
                    elif u == 0:
                        wait_prior(pe, S("m_sig"), i * 8)
                    else:
                        wait_prior(pe, S("m_pfree"), i * 8 + (u - 1))
                    if u >= EARLY or u == 1:
                        wait_prior(pe, S("m_pfree"), i * 8 + (u if u > 1 else 0))
                    dense(ps[m_slot(u)], mwb[:, q, n], Z[:, BRANCH_AT[n]:BRANCH_AT[n] + 2, :], 2)\
                        .then_inc(S("m_proj"), 1)
            rounds(pe, 4, m_round)

            pe.wait_ge(S("m_sig"), 32)
            pe.wait_ge(S("mix_ready"), 8)

            def o_round(i):
                for q in range(2):
                    pe.wait_ge(S(f"rw_in{q}"), i * 16 + 16)
                    if q or not isinstance(i, int):
                        wait_prior(pe, S("r_added"), i * 2 + (q - 1) if not isinstance(i, int) else 0)
                    dense(ps[q], ow[:, q], MIX, KD).then_inc(S(f"r_done{q}"), 1)
            rounds(pe, 4, o_round)
            pe.wait_ge(S("r_ss"), 8)
            whole(ps[0], cc("mean"), nSS).then_inc(S("norm_sum"), 1)
            pe.wait_ge(S("norm_rs"), 2)

            def dense3(out, w, x, kk, ready=None):
                for k in range(kk):
                    if ready is not None:
                        pe.wait_ge(ready, k + 1)
                    for wp, xp in ((0, 0), (0, 1), (1, 0)):
                        for t0, n in SPANS:
                            ins = nc.tensor.matmul(out[:, t0:t0 + n], w[wp][:, k], x[xp][:, k, t0:t0 + n],
                                                   start=(k == 0 and wp == xp), stop=(k == kk - 1 and wp == 1))
                return ins

            def down(i):
                pe.wait_ge(S("g_ready"), i * 2 + 2)
                pe.wait_ge(S("d_lo"), i + 1)
                for d in range(KD):
                    if d < 2:
                        pe.wait_ge(S(f"u_free{d}"), (i * 2 + 3) if not isinstance(i, int) or i < 10 else 22)
                    else:
                        pe.wait_ge(S("d_added"), i * 8 + (d - 1))
                    dense3(ps[d % 2], (Dh[:, :, d], Dl[:, :, d]), (Gh, Gl), 2).then_inc(S("d_done"), 1)

            def u_round(i):
                first = isinstance(i, int) and i == 0
                for q in range(2):
                    for half in range(2):
                        pe.wait_ge(S("u_lo"), i * 4 + (2 * q + half + 1))
                        if q == 0:
                            wait_prior(pe, S(f"u_free{half}"), i * 2)
                        elif first:
                            pe.wait_ge(S(f"u_free{half}"), 1)
                        else:
                            pe.wait_ge(S("d_added"), i * 8 + (half - 1))
                        dense3(ps[half], (Uh[:, half], Ul[:, half]), (Hh, Hl), KD,
                               S("n2_h") if first and q == half == 0 else None).then_inc(S(f"u_done{half}"), 1)
                    if q == 0 and not first:
                        down(i - 1)
            rounds(pe, 11, u_round)
            down(10)
            pe.wait_ge(S("r_ss"), 16)
            whole(ps[0], cc("mean"), dSS).then_inc(S("norm_sum"), 1)
            pe.wait_ge(S("n2_h"), 16)
            pe.wait_ge(S("pe_in"), 16 * KP)

            def p_round(i):
                for q in range(2):
                    pe.wait_ge(S(f"pw_in{q}"), i * 32 + 32)
                    wait_prior(pe, S("p_gfree"), i * 2 + q)
                    dense(ps[0], pw[:, q], H, KD).then_inc(S("p_gate"), 1)
                    wait_prior(pe, S("p_efree"), i * 2 + q)
                    dense(ps[1], pv[:, q], pe_, KP).then_inc(S(f"p_done{q}"), 1)
            rounds(pe, 4, p_round)

        @block.scalar
        def _(act):
            link = Link(act, S("act_chain"))

            def rstd(src, dst):
                link(nc.scalar.activation(dst, src, ACT.Ln, bias=epsc))
                return nc.scalar.activation(dst, dst, ACT.Exp, scale=-0.5)

            epsc = small[:, 90:91]
            act.wait_ge(S("consts"), 1)
            for k in range(KD):
                act.wait_ge(S(f"x_in{k // 2}"), 32)
                if k >= 2:
                    act.wait_ge(S("n1_ss"), k - 1)
                nc.scalar.activation(SQ[:, k % 2], xin[:, k, :], ACT.Square).then_inc(S("n1_sq"), 1)
            act.preload_act_table_set("natural_log_exp_and_others")
            act.wait_ge(S("norm_sum"), 1)
            rstd(ps[0][:, 0:T], RS).then_inc(S("norm_rs"), 1)

            act.wait_ge(S("c_abs"), 1)
            nc.scalar.activation(small[:, 4:6], small[:, 2:4], ACT.Exp, scale=-1.0).then_inc(S("c_exp"), 1)

            def z_round(i):
                for s in range(2):
                    act.wait_ge(S(f"z_done{s}"), i + 1)
                    ins = nc.scalar.activation(Z[:, ds(i * 2 + s, 1), :] if not isinstance(i, int) else Z[:, i * 2 + s:i * 2 + s + 1, :],
                                               ps[s][:, 0:T].rearrange("p (o t) -> p o t", o=1), ACT.Copy)
                    ins.then_inc(S(f"z_free{s}"), 1)
            rounds(act, 8, z_round)

            for i in range(2):
                act.wait_ge(S("cd_done"), 2 * i + 1)
                nc.scalar.activation(cR[:, i], ps[0][:, 0:T], ACT.Sigmoid, bias=pc("b_rg_a", i)).then_inc(S("cd_free"), 1)
                act.wait_ge(S("cd_done"), 2 * i + 2)
                ins = nc.scalar.activation(cI[:, i], ps[1][:, 0:T], ACT.Sigmoid, bias=pc("b_rg_x", i))
                ins.then_inc(S("cd_free"), 1)
            act.wait_ge(S("raw_stored"), 1)
            for i in range(2):
                act.wait_ge(S("cd_done"), 5 + i)
                nc.scalar.activation(Z[:, XD + i, :], ps[i][:, 0:T], ACT.Copy, scale=pc("pool_scale", i))\
                    .then_inc(S("cd_free"), 1)
            act.wait_ge(S("cd_free"), 4)
            act.wait_ge(S("c_lam"), 1)
            for i in range(2):
                if i:
                    act.wait_ge(S("c_scanned"), 1)
                link(nc.scalar.activation(cA, cR[:, i], ACT.Exp, scale=small[:, 20 + i:21 + i]))
                nc.scalar.activation(cB, cA, ACT.Square).then_inc(S("c_a"), 1)
                nc.scalar.activation(cR[:, i], cR[:, i], ACT.Tanh, scale=small[:, 22 + i:23 + i]).then_inc(S("c_a"), 1)
                act.wait_ge(S("c_1ma2"), i + 1)
                nc.scalar.activation(cB, cB, ACT.Sqrt).then_inc(S("c_sqrt"), 1)
                nc.scalar.activation(Z[:, GC + i, :], Z[:, GC + i, :], ACT.Gelu_apprx_tanh).then_inc(S("c_gelu"), 1)

            for t in range(NCH + 1):
                n = P if t < NCH else NS
                act.wait_ge(S("vt_done"), t + 1)
                nc.scalar.activation(VT[0:n, t, :], ps[t % 2][0:n, 0:512], ACT.Copy).then_inc(S("vt_free"), 1)

            def gate_out(p):
                act.wait_ge(S("gate_done"), p + 1)
                if p >= 2:
                    act.wait_ge(S(f"gate_stored{p % 2}"), 16 * (p // 2))
                nc.scalar.activation(gstage[:, p % 2], gbank, ACT.Copy).then_inc(S("gate_out"), 1)

            f2, q2, g2 = Z[:, FB:FB + 2, :], Z[:, QB:QB + 2, :], Z[:, GB:GB + 2, :]
            act.wait_ge(S("cd_over"), 1)
            link(nc.scalar.activation(tA, f2, ACT.Abs))
            link(nc.scalar.activation(tA, tA, ACT.Exp, scale=-1.0))
            nc.scalar.activation(tA, tA, ACT.Ln, bias=1.0).then_inc(S("b_act_pre"), 1)
            act.wait_ge(S("b_dve_pre"), 1)
            nc.scalar.activation(f2, f2, ACT.Sigmoid, scale=-1.0).then_inc(S("b_act_pre"), 1)
            nc.scalar.activation(tA, q2, ACT.Sigmoid).then_inc(S("b_act_pre"), 1)
            gate_out(parts("start0")[0])
            act.wait_ge(S("b_dve_pre"), 2)
            nc.scalar.activation(tA, g2, ACT.Sigmoid).then_inc(S("b_act_pre"), 1)
            gate_out(parts("start0")[1])
            act.wait_ge(S("b_dve_pre"), 3)
            act.preload_act_table_set("natural_log_exp_and_others")
            for i in range(2):
                b = bB[:, i]
                if i == 0:
                    act.wait_ge(S("b_cum"), 2)
                if i:
                    act.wait_ge(S("b_over"), 1)
                nc.scalar.activation(bE, b, ACT.Exp).then_inc(S("b_eb"), 1)
                nc.scalar.activation(bdec[:, 0:8], b[:, CH - 1:SEQ:CH], ACT.Exp).then_inc(S("b_dec"), 1)
                nc.scalar.activation(bdec[:, 8:16], b[:, SEQ + DL - 1:T:DL], ACT.Exp).then_inc(S("b_dec"), 1)
                act.wait_ge(S("b_kdiff"), i + 1)
                nc.scalar.activation(bE, bd_, ACT.Exp, scale=-1.0).then_inc(S("b_kexp"), 1)
                gate_out(parts(f"start{i}")[-2 if i == 0 else 0])
                for g in range(3):
                    act.wait_ge(S("b_tdone"), 3 * i + g + 1)
                    w = min(4, NCH + 1 - 4 * g) * P
                    m = P if g < 2 else NS
                    nc.scalar.activation(kdt[0:m, 4 * g:4 * g + w // P, :].rearrange("p c m -> p (c m)"),
                                         pst[(3 * i + g) % 2][0:m, 0:w], ACT.Copy).then_inc(S("b_tfree"), 1)
                gate_out(parts(f"start{i}")[-1])
                for p in parts(f"states{i}"):
                    gate_out(p)
                for l, m in enumerate(LEVELS):
                    n = len(LEVELS) * i + l
                    nt = T if m <= 2 else SEQ
                    act.wait_ge(S("b_diff"), n + 1)
                    if l == 0:
                        act.wait_ge(S("b_tdone"), 3 * i + 3)
                    dv = bd_[:, 0:nt].rearrange("p (n h m) -> p n h m", h=2, m=m)
                    kv = KF[:, l % 2, 0:nt].rearrange("p (n h m) -> p n h m", h=2, m=m)
                    ev = bE[:, 0:nt].rearrange("p (n h m) -> p n h m", h=2, m=m)
                    nc.scalar.activation(kv[:, :, 0, :], dv[:, :, 0, :], ACT.Exp, scale=-1.0).then_inc(S("b_exps"), 1)
                    nc.scalar.activation(ev[:, :, 1, :], dv[:, :, 1, :], ACT.Exp).then_inc(S("b_exps"), 1)
                    if l in (2, 4, 6):
                        gate_out(parts(f"levels{i}")[l // 2 - 1])
                act.wait_ge(S("b_ofree"), i + 1)
                nc.scalar.activation(bE, bd_, ACT.Square).then_inc(S("b_osq"), 1)
                act.wait_ge(S("b_ms"), i + 1)
                rstd(ps[0][:, 0:T], bE).then_inc(S("b_rs"), 1)

            def a_rs(j):
                act.wait_ge(S("a_ms"), j + 1)
                if j >= 2:
                    act.wait_ge(S("a_normed"), j - 1)
                rstd(ps[j % 2][:, 0:T], beta.rearrange("p a b -> p (a b)")[:, 0:T] if j % 2 == 0 else
                     Pp.rearrange("p a b -> p (a b)")[:, 0:T]).then_inc(S("a_rs"), 1)

            kf_, wf_ = keep.rearrange("p a b -> p (a b)"), wT.rearrange("p a b -> p (a b)")
            order = (KA, KA + 1, QA, QA + 1)
            act.wait_ge(S("b_over"), 2)
            for j in range(4):
                if j >= 2:
                    act.wait_ge(S("a_ms"), j - 1)
                nc.scalar.activation((kf_, wf_)[j % 2][:, 0:T], Z[:, order[j], :], ACT.Square).then_inc(S("a_sq"), 1)
                if j == 0:
                    for p in parts("norms"):
                        gate_out(p)
                if j >= 1:
                    a_rs(j - 1)
            a_rs(3)
            for p in parts("normed"):
                gate_out(p)
            act.wait_ge(S("a_qm"), 1)
            tg = [0]
            for n in range(32):
                tg.append(tg[-1] + (n // 4 + 4) // 4)

            def sticks(n):
                i, h = n // 4, n % 4
                w = (i + 1) * P
                act.wait_ge(S("a_sc"), n + 1)
                if n >= 2:
                    act.wait_ge(S("a_tdone"), tg[n - 1])
                nc.scalar.activation(keep[:, n % 2, 0:w], ps[n % 2][:, 0:w], ACT.Sigmoid,
                                     scale=-HD ** -0.5, bias=negb[:, h:h + 1]).then_inc(S("a_stick"), 1)
                nc.scalar.activation(beta[:, n % 2, 0:w], ps[n % 2][:, 0:w], ACT.Sigmoid,
                                     scale=HD ** -0.5, bias=pc("sb_head", h)).then_inc(S("a_scfree"), 1)

            def turned(n):
                i = n // 4
                for g in range(tg[n], tg[n + 1]):
                    j0 = 4 * (g - tg[n])
                    w = (min(j0 + 4, i + 1) - j0) * P
                    act.wait_ge(S("a_tdone"), g + 1)
                    if n >= 2:
                        act.wait_ge(S("a_pv"), n - 1)
                    nc.scalar.activation(wT[:, n % 2, j0 * P:j0 * P + w], pst[g % 2][:, 0:w], ACT.Copy)\
                        .then_inc(S("a_tfree"), 1)

            for n in range(33):
                if n < 32:
                    sticks(n)
                if n >= 1:
                    turned(n - 1)
                if n < 32 and n % 4 == 1:
                    gate_out(parts("steps")[n // 4])
            for p in parts("samples"):
                gate_out(p)
            act.wait_ge(S("as_sc"), 1)
            act.wait_ge(S("a_tdone"), tg[32])
            nc.scalar.activation(keep[:, 0, 0:PAST + NS], ps[0][:, 0:PAST + NS], ACT.Sigmoid,
                                 scale=-HD ** -0.5, bias=negb[:, 4:5]).then_inc(S("as_stick"), 1)
            nc.scalar.activation(beta[:, 0, 0:PAST + NS], ps[0][:, 0:PAST + NS], ACT.Sigmoid,
                                 scale=HD ** -0.5, bias=pc("sb_row")).then_inc(S("as_stick"), 1)
            act.wait_ge(S("as_t"), 1)
            act.wait_ge(S("a_pv"), 32)
            nc.scalar.activation(wT[:, 0, 0:PAST], pst[0][:, 0:PAST], ACT.Copy).then_inc(S("as_tfree"), 1)
            nc.scalar.activation(wT[0:NS, 1, 0:P], pst[1][0:NS, 0:P], ACT.Copy).then_inc(S("as_tfree"), 1)

            def m_round(i):
                for u in range(8):
                    if u < EARLY:
                        act.wait_ge(S("mw_in0"), i * 32 + 32)
                    else:
                        act.wait_ge(S("m_gate"), i * LATE + (u - EARLY + 1))
                    if u >= 2 or not isinstance(i, int):
                        act.wait_ge(S("m_pfree"), i * 8 + (u - 1))
                    nc.scalar.activation(SIG[:, u % 2], early[:, u] if u < EARLY else ps[0][:, 0:T], ACT.Sigmoid)\
                        .then_inc(S("m_sig"), 1)
            act.wait_ge(S("a_over"), 2)
            rounds(act, 4, m_round)

            def up_high(c, half):
                act.wait_ge(S(f"uw_in{half}"), c * 16 + 16)
                nc.scalar.activation(Uh[:, half], uraw[:, half], ACT.Copy).then_inc(S("u_hi"), 1)

            for half in range(2):
                up_high(0, half)

            def o_squares(i):
                for q in range(2):
                    act.wait_ge(S("r_added"), i * 2 + (q + 1))
                    src = X[:, i * 2 + q:i * 2 + q + 1, :] if isinstance(i, int) else X[:, ds(i * 2 + q, 1), :]
                    wait_prior(act, S("r_ss"), i * 2 + q)
                    nc.scalar.activation(nSQ.rearrange("p (o t) -> p o t", o=1), src, ACT.Square)\
                        .then_inc(S("r_sq"), 1)
            rounds(act, 4, o_squares)
            act.preload_act_table_set("natural_log_exp_and_others")
            act.wait_ge(S("norm_sum"), 2)
            rstd(ps[0][:, 0:T], nRS).then_inc(S("norm_rs"), 1)
            for k in range(KD):
                act.wait_ge(S("split_raw"), k + 1)
                nc.scalar.activation(Hh[:, k], ntmp[:, k % 2], ACT.Copy).then_inc(S("split_hi"), 1)

            act.wait_ge(S("tables_in"), 64)

            def u_round(i, last=False):
                def at(x, q):
                    c = i * 2 + q
                    return x[:, c:c + 1] if isinstance(i, int) else x[:, ds(c, 1)]

                for q in range(2):
                    for half in range(2):
                        act.wait_ge(S(f"u_done{half}"), i * 2 + (q + 1))
                        if half == 0:
                            if q or not isinstance(i, int) or i:
                                act.wait_ge(S("g_ready"), i * 2 + q)
                            fp = small[:, 64:72]
                            link(nc.scalar.activation(fp.rearrange("p (o e) -> p o e", o=1), at(fpar, q), ACT.Copy))
                        src = ps[half][:, 0:T]
                        nc.scalar.activation(V[:, half], src, ACT.Identity, scale=fp[:, 4 * half + 2:4 * half + 3],
                                             bias=fp[:, 4 * half + 3:4 * half + 4]).then_inc(S("u_tap"), 1)
                        fo = at(FO, q)[:, :, half, :]
                        nc.scalar.activation(fo[:, :, 0:2], src[:, SEQ - 2:SEQ].rearrange("p (o e) -> p o e", o=1),
                                             ACT.Copy).then_inc(S(f"u_read{half}"), 1)
                        nc.scalar.activation(
                            fo[:, :, 2:18].rearrange("p o (b e) -> p (o b) e", b=DB),
                            src[:, SEQ:T].rearrange("p (b t) -> p b t", b=DB)[:, :, 2:4], ACT.Copy)\
                            .then_inc(S(f"u_read{half}"), 1)
                        if not (last and q):
                            up_high(i * 2 + (q + 1), half)
                        if q == 1 and half == 0:
                            act.wait_ge(S("d_in"), i * 16 + 16)
                            wait_prior(act, S("d_done"), i * 8)
                            nc.scalar.activation(Dh, draw, ACT.Copy).then_inc(S("d_hi"), 1)
                    act.wait_ge(S("u_free0"), i * 2 + (q + 1))
                    nc.scalar.activation(V[:, 0], V[:, 0], ACT.Gelu_apprx_tanh).then_inc(S("u_gelu"), 1)
                    act.wait_ge(S("split_raw"), i * 2 + (KD + q + 1))
                    nc.scalar.activation(Gh[:, q], V[:, 0], ACT.Copy).then_inc(S("split_hi"), 1)
            link.rounds(10, u_round)
            u_round(10, True)

            act.preload_act_table_set("natural_log_exp_and_others")
            for d in range(KD):
                act.wait_ge(S("d_added"), 80 + d + 1)
                if d:
                    act.wait_ge(S("r_ss"), 8 + d)
                nc.scalar.activation(dSQ, X[:, d, :], ACT.Square).then_inc(S("r_sq"), 1)
            act.wait_ge(S("norm_sum"), 3)
            rstd(ps[0][:, 0:T], dRS).then_inc(S("norm_rs"), 1)

            def p_round(i):
                for q in range(2):
                    act.wait_ge(S("p_gate"), i * 2 + (q + 1))
                    if not isinstance(i, int):
                        act.wait_ge(S("y_ready"), i * 2 + (q - 1))
                    nc.scalar.activation(sigp[:, q], ps[0][:, 0:T], ACT.Sigmoid).then_inc(S("p_gfree"), 1)
            rounds(act, 4, p_round)

        @block.vector
        def _(dve):
            v = nc.vector
            link = Link(dve, S("dve_chain"))
            v.memset(small[:, 90:91], EPS).then_inc(S("consts"), 1)
            for k in range(KD):
                dve.wait_ge(S("n1_sq"), k + 1)
                if k == 0:
                    v.tensor_copy(SS, SQ[:, 0]).then_inc(S("n1_ss"), 1)
                else:
                    dve.wait_ge(S("n1_ss"), k)
                    v.tensor_tensor(SS, SS, SQ[:, k % 2], ALU.add).then_inc(S("n1_ss"), 1)
            dve.wait_ge(S("params_in"), 32)
            link(v.tensor_scalar(small[:, 0:2], pc("lam", 0, 2), -1.0, 0.0, ALU.mult, ALU.max))
            v.scalar_tensor_tensor(small[:, 2:4], small[:, 0:2], 2.0, pc("lam", 0, 2), ALU.mult, ALU.add)\
                .then_inc(S("c_abs"), 1)
            dve.wait_ge(S("norm_rs"), 1)
            for k in range(KD):
                v.scalar_tensor_tensor(H[:, k, :], xin[:, k, :], pc("norm_mix", k), RS, ALU.mult, ALU.mult)\
                    .then_inc(S("n1_h"), 1)
            dve.wait_ge(S("c_exp"), 1)
            e_, s_, s2, p_ = small[:, 4:6], small[:, 6:8], small[:, 8:10], small[:, 10:12]
            link(v.tensor_scalar(p_, e_, 2.0, None, ALU.add))
            link(v.reciprocal(p_, p_))
            link(v.tensor_tensor(s_, e_, p_, ALU.mult))
            link(v.tensor_tensor(s2, s_, s_, ALU.mult))
            link(v.tensor_scalar(p_, s2, 1.0 / 17, None, ALU.mult))
            for n in range(7, 0, -1):
                link(v.scalar_tensor_tensor(p_, p_, 1.0 / (2 * n + 1), s2, ALU.add, ALU.mult))
            link(v.tensor_scalar(p_, p_, 1.0, 2.0, ALU.add, ALU.mult))
            link(v.tensor_tensor(p_, p_, s_, ALU.mult))
            link(v.tensor_tensor(p_, p_, small[:, 0:2], ALU.add))
            link(v.tensor_scalar(small[:, 20:22], p_, -8.0, None, ALU.mult),
                 v.tensor_scalar(small[:, 22:24], p_, 8.0, None, ALU.mult))
            dve.sem_inc(S("c_lam"), 1)

            dve.wait_ge(S("cd_in"), 64)
            for i in range(2):
                dve.wait_ge(S(f"z_free{i}"), 1)
                x, y = Z[:, XC + i, :], cX[:, i]
                w = [pc("conv_c_w", 2 * j + i) for j in range(4)]
                link(v.tensor_copy(cext[:, :, 0:3], chist[:, i]),
                     v.tensor_copy(cext[:, :, 3:7], x[:, SEQ:T].rearrange("p (b t) -> p b t", b=DB)))
                ys = y[:, SEQ:T].rearrange("p (b t) -> p b t", b=DB)
                link(v.tensor_scalar(y[:, 0:SEQ], x[:, 0:SEQ], w[3], pc("conv_c_b", i), ALU.mult, ALU.add),
                     v.tensor_scalar(ys, cext[:, :, 3:7], w[3], pc("conv_c_b", i), ALU.mult, ALU.add))
                for j in (2, 1, 0):
                    d = 3 - j
                    link(v.scalar_tensor_tensor(y[:, d:SEQ], x[:, 0:SEQ - d], w[j], y[:, d:SEQ], ALU.mult, ALU.add),
                         v.scalar_tensor_tensor(ys, cext[:, :, j:j + 4], w[j], ys, ALU.mult, ALU.add))
                dve.sem_inc(S("cd_ready"), 1)

            for i in range(2):
                dve.wait_ge(S(f"z_free{i}"), XD // 2 + 1)
                x = Z[:, XD + i, :]
                dEs = dE[:, HIST + SEQ:EXT].rearrange("p (b t) -> p b t", b=DB)
                if i == 0:
                    link(v.memset(dE[:, 0:HIST], 0.0))
                dve.wait_ge(S("pool_in"), 16 * (i + 1))
                link(v.tensor_copy(dE[:, HIST:HIST + SEQ], x[:, 0:SEQ]),
                     v.tensor_copy(dEs[:, :, HIST:], x[:, SEQ:T].rearrange("p (b t) -> p b t", b=DB)))
                src, dst = dE, dF
                for w in ((1, 2), (1, 2, 4, 8))[i]:
                    top = w == (2, 8)[i]
                    if top:
                        link(v.tensor_tensor(dst[HD:P, 2 * w - 1:EXT], src[HD:P, 2 * w - 1:EXT],
                                             src[HD:P, w - 1:EXT - w], ALU.add),
                             v.tensor_copy(dst[0:HD, HIST:EXT], src[0:HD, HIST:EXT]))
                    else:
                        link(v.tensor_tensor(dst[:, 2 * w - 1:EXT], src[:, 2 * w - 1:EXT], src[:, w - 1:EXT - w],
                                             ALU.add))
                    src, dst = dst, src
                link(v.tensor_tensor(src[:, HIST:2 * HIST], src[:, HIST:2 * HIST], cc("corr", HIST, i * HIST),
                                     ALU.mult))
                dve.wait_ge(S("raw_stored"), 1)
                ss = src[:, HIST + SEQ:EXT].rearrange("p (b t) -> p b t", b=DB)[:, :, HIST:]
                xs = x[:, SEQ:T].rearrange("p (b t) -> p b t", b=DB)
                link(v.scalar_tensor_tensor(x[:, 0:SEQ], src[:, HIST:HIST + SEQ], cc("invw", 1, i), x[:, 0:SEQ],
                                            ALU.mult, ALU.subtract),
                     v.scalar_tensor_tensor(xs, ss, cc("invw", 1, i), xs, ALU.mult, ALU.subtract))
                dve.sem_inc(S("cd_ready"), 1)

            for i in range(2):
                dve.wait_ge(S("c_a"), 2 * i + 2)
                v.scalar_tensor_tensor(cB, cB, 1.0, cR[:, i], ALU.add, ALU.mult).then_inc(S("c_1ma2"), 1)
                link(v.tensor_tensor(cI[:, i], cI[:, i], cX[:, i], ALU.mult))
                dve.wait_ge(S("c_sqrt"), i + 1)
                link(v.tensor_tensor(cI[:, i], cI[:, i], cB, ALU.mult))
                a0, u0 = cA[:, SEQ:T:DL], cI[:, i, SEQ:T:DL]
                link(v.tensor_tensor(small[:, 24:32], a0, ch0[:, i], ALU.mult))
                link(v.tensor_tensor(u0, u0, small[:, 24:32], ALU.add), v.memset(a0, 0.0))
                link(v.tensor_tensor_scan(cX[:, i], cA, cI[:, i], 0.0, ALU.mult, ALU.add))
                link(v.tensor_copy(small[:, 40 + i:41 + i], cX[:, i, SEQ - 1:SEQ]),
                     v.tensor_copy(small[:, 48 + 8 * i:56 + 8 * i], cX[:, i, SEQ + DL - 1:T:DL]))
                dve.sem_inc(S("c_scanned"), 1)
                dve.wait_ge(S("c_gelu"), i + 1)
                v.tensor_tensor(Z[:, GC + i, :], Z[:, GC + i, :], cX[:, i], ALU.mult).then_inc(S("c_out"), 1)
            dve.wait_ge(S("c_out"), 2)
            dve.wait_ge(S("cd_free"), 6)
            dve.wait_ge(S("vt_free"), NCH + 1)
            dve.sem_inc(S("cd_over"), 1)

            f2, q2, g2 = Z[:, FB:FB + 2, :], Z[:, QB:QB + 2, :], Z[:, GB:GB + 2, :]
            link(v.memset(rmask, 1.0))
            link(v.memset(rmask[:, 0:SEQ:CH], 0.0), v.memset(rmask[:, SEQ:T:DL], 0.0))
            for buf in (KF, QF[0], QF[1]):
                link(v.memset(buf, 0.0))
            dve.wait_ge(S("b_act_pre"), 1)
            link(v.scalar_tensor_tensor(bB, f2, 0.0, tA, ALU.min, ALU.subtract))
            dve.sem_inc(S("b_dve_pre"), 1)
            for i in range(2):
                v.tensor_tensor_scan(bB[:, i], rmask, bB[:, i], 0.0, ALU.mult, ALU.add).then_inc(S("b_cum"), 1)
            dve.wait_ge(S("b_act_pre"), 3)
            v.tensor_tensor(q2, q2, tA, ALU.mult).then_inc(S("b_dve_pre"), 1)
            dve.wait_ge(S("b_act_pre"), 4)
            v.tensor_tensor(g2, g2, tA, ALU.mult).then_inc(S("b_dve_pre"), 1)
            dve.wait_ge(S("b_dve_pre"), 2)
            dve.wait_ge(S("b_dve_pre"), 3)
            dve.wait_ge(S("b_cum"), 2)
            dve.wait_ge(S("tables_in"), 64)
            dve.wait_ge(S("b_act_pre"), 2)
            for i in range(2):
                b, kk, qq, gg = bB[:, i], Z[:, FB + i, :], Z[:, QB + i, :], Z[:, GB + i, :]
                bp, bs = b[:, 0:SEQ].rearrange("p (c t) -> p c t", c=NCH), b[:, SEQ:T].rearrange("p (c t) -> p c t", c=DB)
                dp = bd_[:, 0:SEQ].rearrange("p (c t) -> p c t", c=NCH)
                dss = bd_[:, SEQ:T].rearrange("p (c t) -> p c t", c=DB)
                dve.wait_ge(S("b_eb"), i + 1)
                link(v.tensor_tensor(QE, qq, bE, ALU.mult))
                link(v.tensor_tensor(dp, bp, bp[:, :, CH - 1:CH].to_broadcast([P, NCH, CH]), ALU.subtract),
                     v.tensor_tensor(dss, bs, bs[:, :, DL - 1:DL].to_broadcast([P, DB, DL]), ALU.subtract))
                dve.sem_inc(S("b_kdiff"), 1)
                dve.wait_ge(S("b_kexp"), i + 1)
                v.tensor_tensor(bE, bE, kk, ALU.mult).then_inc(S("b_kd"), 1)
                if i:
                    dve.wait_ge(S("states_stored"), 1)
                for bb in range(DB):
                    ins = v.tensor_scalar(vbd[0:NS, bb, :], VT[0:NS, NCH, HW + i * P:HW + i * P + P],
                                          cc("batch", 1, bb, NS), None, ALU.mult)
                    link(ins)
                dve.sem_inc(S("b_vbd"), 1)
                dve.wait_ge(S("b_u"), i + 1)
                dve.wait_ge(S("b_dec"), 2 * i + 2)
                UBp = KF.rearrange("p a b -> p (a b)")[:, 0:NCH * P].rearrange("p (c m) -> p c m", c=NCH)
                bdb = cc("bd").rearrange("p (o m) -> p o m", o=1).to_broadcast([P, NCH, P])
                up = ps[0][:, 0:SEQ].rearrange("p (c m) -> p c m", c=NCH)
                us_ = ps[1][:, 0:SEQ].rearrange("p (c m) -> p c m", c=NCH)
                v.tensor_tensor(UBp, up, bdb, ALU.mult).then_inc(S("b_ufree"), 1)
                dve.wait_ge(S("b_ufree"), 2 * i + 1)
                link(v.tensor_copy(Sall[:, 1, :], UBp[:, 0, :]))
                for c in range(1, NCH):
                    link(v.scalar_tensor_tensor(Sall[:, c + 1, :], Sall[:, c, :], bdec[:, c:c + 1], UBp[:, c, :],
                                                ALU.mult, ALU.add))
                v.tensor_tensor(UBp, us_, bdb, ALU.mult).then_inc(S("b_ufree"), 1)
                dve.wait_ge(S("b_ufree"), 2 * i + 2)
                dve.wait_ge(S("s0_in"), 16)
                for bb in range(DB):
                    link(v.scalar_tensor_tensor(vbd[:, bb, :], S0[:, i, bb, :], bdec[:, 8 + bb:9 + bb],
                                                UBp[:, bb, :], ALU.mult, ALU.add))
                dve.sem_inc(S("b_states"), 1)
                link(v.memset(KF, 0.0), v.memset(att, 0.0), v.memset(atts[0:NS], 0.0))

                def differences(l, m):
                    if l:
                        dve.wait_ge(S("b_exps"), 2 * (len(LEVELS) * i + l))
                    nt = T if m <= 2 else SEQ
                    bv = b[:, 0:nt].rearrange("p (n w) -> p n w", w=2 * m)
                    dv = bd_[:, 0:nt].rearrange("p (n w) -> p n w", w=2 * m)
                    if l >= 2:
                        dve.wait_ge(S("b_adone"), 4 * (NL * i + l - 1))
                    if l >= 7:
                        dve.wait_ge(S("b_sdone"), 3 * i + l - 6)
                    v.tensor_tensor(dv, bv, bv[:, :, m - 1:m].to_broadcast([P, nt // (2 * m), 2 * m]), ALU.subtract)\
                        .then_inc(S("b_diff"), 1)

                def factors(l, m):
                    nt = T if m <= 2 else SEQ
                    dve.wait_ge(S("b_exps"), 2 * (len(LEVELS) * i + l + 1))

                    def halves(x):
                        return x[:, 0:nt].rearrange("p (n h m) -> p n h m", h=2, m=m)
                    kv = halves(KF[:, l % 2])[:, :, 0, :]
                    link(v.tensor_tensor(kv, kv, halves(kk)[:, :, 0, :], ALU.mult),
                         *[v.tensor_tensor(halves(QF[hh][hh * HD:hh * HD + HD, l % 2])[:, :, 1, :],
                                           halves(qq[hh * HD:hh * HD + HD])[:, :, 1, :],
                                           halves(bE[hh * HD:hh * HD + HD])[:, :, 1, :], ALU.mult) for hh in range(2)])
                    dve.sem_inc(S("b_factors"), 1)

                def select(l):
                    n = NL * i + l
                    for g in range(4):
                        dve.wait_ge(S("b_adone"), 4 * n + g + 1)
                        bank = ps[g // 2][:, (g % 2) * 512:(g % 2) * 512 + 512].rearrange("p (a m) -> p a m", a=4)
                        v.copy_predicated(att[:, 2 * g:2 * g + 2].rearrange("p c h m -> p (c h) m"),
                                          masks[:, l:l + 1, :].to_broadcast([P, 4, P]), bank).then_inc(S("b_afree"), 1)
                    if l >= 5:
                        dve.wait_ge(S("b_sdone"), 3 * i + l - 4)
                        v.copy_predicated(atts[0:NS], smasks[:, l - 5:l - 4, :].to_broadcast([NS, 2, NS]),
                                          pst[0][0:NS, 0:2 * NS].rearrange("p (h t) -> p h t", h=2))\
                            .then_inc(S("b_sfree"), 1)

                for l in range(NL + 1):
                    if l < NL - 1:
                        differences(l, LEVELS[l])
                    if l >= 1:
                        select(l - 1)
                    if l < NL - 1:
                        factors(l, LEVELS[l])
                    elif l == NL - 1:
                        dve.wait_ge(S("b_adone"), 4 * (NL * i + l - 1))
                        dve.wait_ge(S("b_sdone"), 3 * i + 1)
                        link(*[v.tensor_copy(QF[hh][hh * HD:hh * HD + HD, l % 2], qq[hh * HD:hh * HD + HD])
                               for hh in range(2)])
                        dve.sem_inc(S("b_factors"), 1)
                dve.wait_ge(S("b_odone"), i + 1)
                dve.wait_ge(S("b_exps"), 2 * len(LEVELS) * (i + 1))
                for hh in range(2):
                    rows = slice(hh * HD, hh * HD + HD)
                    for g in range(4):
                        bank = ps[g // 2][rows, (g % 2) * 512 + hh * 256:(g % 2) * 512 + hh * 256 + 256]
                        v.tensor_copy(bd_[rows, g * 256:g * 256 + 256], bank).then_inc(S("b_oc"), 1)
                dve.wait_ge(S("b_osdone"), i + 1)
                for hh in range(2):
                    rows = slice(hh * HD, hh * HD + HD)
                    v.tensor_copy(bd_[rows, SEQ:T], pst[1][rows, hh * NS:hh * NS + NS]).then_inc(S("b_oc"), 1)
                dve.wait_ge(S("b_oc"), 10 * (i + 1))
                dve.sem_inc(S("b_ofree"), 1)
                link(v.tensor_tensor(gg, gg, bd_, ALU.mult))
                dve.wait_ge(S("b_rs"), i + 1)
                dve.wait_ge(S("states_stored"), i + 1)
                link(v.scalar_tensor_tensor(gg, gg, pc("hgrn_norm"), bE, ALU.mult, ALU.mult))
                dve.sem_inc(S("b_over"), 1)

            link(v.tensor_scalar(negb[:, 0:NH + 1], par[:, PAR["sb_head"]:PAR["sb_head"] + NH + 1], -1.0, None,
                                 ALU.mult), v.memset(QS, 0.0), v.memset(qm, 0.0))
            rs = (beta.rearrange("p a b -> p (a b)")[:, 0:T], Pp.rearrange("p a b -> p (a b)")[:, 0:T])
            for j in range(4):
                dve.wait_ge(S("a_rs"), j + 1)
                if j < 2:
                    link(v.scalar_tensor_tensor(Z[:, KA + j, :], Z[:, KA + j, :], pc("k_norm"), rs[j % 2], ALU.mult,
                                                ALU.mult))
                    dve.sem_inc(S("a_kq"), 1)
                else:
                    for hh in range(2):
                        rows = slice(hh * HD, hh * HD + HD)
                        link(v.scalar_tensor_tensor(qm[rows, 2 * (j - 2) + hh, :], Z[rows, QA + j - 2, :],
                                                    pc("q_norm")[rows], rs[j % 2][rows], ALU.mult, ALU.mult))
                dve.sem_inc(S("a_normed"), 1)
            for h in range(NH):
                rows = slice((h % 2) * HD, (h % 2) * HD + HD)
                src = qm[rows, h, SEQ:T].rearrange("p (b t) -> p b t", b=DB)
                link(v.tensor_copy(QS[rows, h // 2, :].rearrange("p (b c) -> p b c", c=144)[:, :, 4 * h:4 * h + 4],
                                   src))
            for i in range(2):
                link(v.memset(QSall[:, i], 0.0))
                for hh in range(2):
                    h = 2 * i + hh
                    rows = slice(hh * HD, hh * HD + HD)
                    link(v.tensor_copy(QSall[rows, i, :].rearrange("p (b c) -> p b c", c=16)[:, :, 4 * h:4 * h + 4],
                                       qm[rows, h, SEQ:T].rearrange("p (b t) -> p b t", b=DB)))
            dve.sem_inc(S("a_qs"), 1)
            for s in range(2):
                link(v.memset(Pp[:, s, :], 1.0))
            dve.sem_inc(S("a_qm"), 1)

            def broken(s, w, d0, dn, yes, no):
                link(v.tensor_tensor(beta[:, s, d0:d0 + dn], beta[:, s, d0:d0 + dn], yes, ALU.mult),
                     v.tensor_tensor(keep[:, s, d0:d0 + dn], keep[:, s, d0:d0 + dn], no, ALU.max))
                if w < SEQ:
                    link(v.memset(Pp[:, s, w:w + 1], 1.0))
                link(v.tensor_tensor_scan(Pp[:, s, 0:w][:, ::-1], keep[:, s, 0:w][:, ::-1], keep[:, s, 0:w][:, ::-1],
                                          1.0, ALU.mult, ALU.bypass))
                return v.tensor_tensor(beta[:, s, 0:w], beta[:, s, 0:w], Pp[:, s, 1:w + 1], ALU.mult)

            def heads_out(i):
                dve.wait_ge(S("a_pv"), 4 * i + 4)
                for h in range(NH):
                    rows = slice((h % 2) * HD, (h % 2) * HD + HD)
                    v.tensor_copy(Z[rows, QA + h // 2, i * P:i * P + P],
                                  ps[0][rows, 1024 + h * P:1024 + h * P + P]).then_inc(S("a_oc"), 1)
                dve.wait_ge(S("a_oc"), 4 * i + 4)
                dve.sem_inc(S("a_ofree"), 1)

            for n in range(32):
                i = n // 4
                dve.wait_ge(S("a_stick"), n + 1)
                dve.wait_ge(S("a_scfree"), n + 1)
                if n:
                    dve.wait_ge(S("a_w"), n)
                broken(n % 2, (i + 1) * P, i * P, P, cc("strict"), cc("notstrict")).then_inc(S("a_w"), 1)
                if n % 4 == 1 and i >= 1:
                    heads_out(i - 1)
            heads_out(7)
            dve.wait_ge(S("as_stick"), 2)
            broken(0, PAST + NS, PAST, NS, cc("newkeys", NS), cc("notnewkeys", NS)).then_inc(S("as_w"), 1)
            dve.wait_ge(S("vp_used"), DB)
            for h in range(NH):
                rows = slice((h % 2) * HD, (h % 2) * HD + HD)
                link(v.tensor_copy(Z[rows, QA + h // 2, SEQ:T].rearrange("p (b t) -> p b t", b=DB),
                                   ps[1][rows, (h // 2) * P:(h // 2) * P + P].rearrange(
                                       "p (b c) -> p b c", c=16)[:, :, 4 * h:4 * h + 4]))
            dve.sem_inc(S("a_over"), 2)

            def m_round(i):
                for q in range(2):
                    for n in range(4):
                        u = 4 * q + n
                        dve.wait_ge(S("m_sig"), i * 8 + (u + 1))
                        dve.wait_ge(S("m_proj"), i * 8 + (u + 1))
                        dst = ACC if n == 0 else TMP
                        v.tensor_tensor(dst, SIG[:, u % 2], ps[m_slot(u)][:, 0:T], ALU.mult)\
                            .then_inc(S("m_pfree"), 1)
                        dve.wait_ge(S("m_pfree"), i * 8 + (u + 1))
                        if 0 < n < 3:
                            link(v.tensor_tensor(ACC, ACC, TMP, ALU.add))
                    c = i * 2 + q
                    dst = MIX[:, c:c + 1, :] if isinstance(i, int) else MIX[:, ds(c, 1), :]
                    v.tensor_tensor(dst, ACC.rearrange("p (o t) -> p o t", o=1),
                                    TMP.rearrange("p (o t) -> p o t", o=1), ALU.add).then_inc(S("mix_ready"), 1)
                    dve.wait_ge(S("mix_ready"), i * 2 + (q + 1))
            link.rounds(4, m_round)

            dve.wait_ge(S("x_again"), 16 * KD)
            link(v.memset(nSS, 0.0))

            def o_round(i):
                for q in range(2):
                    c = i * 2 + q
                    x = X[:, c:c + 1, :] if isinstance(i, int) else X[:, ds(c, 1), :]
                    dve.wait_ge(S(f"r_done{q}"), i + 1)
                    v.tensor_tensor(x, x, ps[q][:, 0:T].rearrange("p (o t) -> p o t", o=1), ALU.add)\
                        .then_inc(S("r_added"), 1)
                    dve.wait_ge(S("r_sq"), i * 2 + (q + 1))
                    v.tensor_tensor(nSS, nSS, nSQ, ALU.add).then_inc(S("r_ss"), 1)
                    dve.wait_ge(S("r_ss"), i * 2 + (q + 1))
            rounds(dve, 4, o_round)
            dve.wait_ge(S("norm_rs"), 2)

            def normed(k):
                if k >= 2:
                    dve.wait_ge(S("n2_h"), k - 1)
                v.scalar_tensor_tensor(ntmp[:, k % 2], X[:, k, :], pc("norm_ffn", k), nRS, ALU.mult, ALU.mult)\
                    .then_inc(S("split_raw"), 1)

            normed(0)
            for k in range(KD):
                if k < KD - 1:
                    normed(k + 1)
                dve.wait_ge(S("split_hi"), k + 1)
                v.tensor_tensor(Hl[:, k], ntmp[:, k % 2], Hh[:, k].bitcast(F32), ALU.subtract)\
                    .then_inc(S("n2_h"), 1)

            dve.wait_ge(S("tables_in"), 64)

            def u_round(i):
                for q in range(2):
                    c = i * 2 + q
                    fp = small[:, 64:72]
                    for half in range(2):
                        dve.wait_ge(S("u_tap"), i * 4 + (2 * q + half + 1))
                        dve.wait_ge(S(f"u_read{half}"), i * 4 + (2 * q + 2))
                        y, x = V[:, half], ps[half][:, 0:T]
                        w0, w1 = fp[:, 4 * half:4 * half + 1], fp[:, 4 * half + 1:4 * half + 2]
                        ys = y[:, SEQ:T].rearrange("p (b t) -> p b t", b=DB)
                        xs = x[:, SEQ:T].rearrange("p (b t) -> p b t", b=DB)
                        fh = (FH[:, c, half] if isinstance(i, int) else
                              FH[:, ds(c, 1), half].rearrange("p o b t -> p (o b) t"))
                        link(v.scalar_tensor_tensor(y[:, 1:SEQ], x[:, 0:SEQ - 1], w1, y[:, 1:SEQ], ALU.mult, ALU.add),
                             v.scalar_tensor_tensor(ys[:, :, 1:], xs[:, :, 0:3], w1, ys[:, :, 1:], ALU.mult, ALU.add),
                             v.scalar_tensor_tensor(ys[:, :, 0:1], fh[:, :, 1:2], w1, ys[:, :, 0:1], ALU.mult,
                                                    ALU.add))
                        link(v.scalar_tensor_tensor(y[:, 2:SEQ], x[:, 0:SEQ - 2], w0, y[:, 2:SEQ], ALU.mult, ALU.add),
                             v.scalar_tensor_tensor(ys[:, :, 2:], xs[:, :, 0:2], w0, ys[:, :, 2:], ALU.mult, ALU.add),
                             v.scalar_tensor_tensor(ys[:, :, 0:2], fh, w0, ys[:, :, 0:2], ALU.mult, ALU.add))
                        dve.sem_inc(S(f"u_free{half}"), 1)
                    if q == 0 and not isinstance(i, int):
                        for d in range(KD):
                            dve.wait_ge(S("d_done"), i * 8 + (d - 7))
                            v.tensor_tensor(X[:, d, :], X[:, d, :], ps[d % 2][:, 0:T], ALU.add)\
                                .then_inc(S("d_added"), 1)
                    dve.wait_ge(S("u_gelu"), i * 2 + (q + 1))
                    v.tensor_tensor(V[:, 0], V[:, 0], V[:, 1], ALU.mult).then_inc(S("split_raw"), 1)
                    dve.wait_ge(S("split_hi"), i * 2 + (KD + q + 1))
                    v.tensor_tensor(Gl[:, q], V[:, 0], Gh[:, q].bitcast(F32), ALU.subtract)\
                        .then_inc(S("g_ready"), 1)
            link.rounds(11, u_round)

            link(v.memset(dSS, 0.0))
            for d in range(KD):
                dve.wait_ge(S("d_done"), 80 + d + 1)
                v.tensor_tensor(X[:, d, :], X[:, d, :], ps[d % 2][:, 0:T], ALU.add).then_inc(S("d_added"), 1)
                dve.wait_ge(S("r_sq"), 8 + d + 1)
                if d:
                    dve.wait_ge(S("r_ss"), 8 + d)
                v.tensor_tensor(dSS, dSS, dSQ, ALU.add).then_inc(S("r_ss"), 1)
            dve.wait_ge(S("norm_rs"), 3)
            for k in range(KD):
                v.scalar_tensor_tensor(H[:, k, :], X[:, k, :], pc("norm_ple", k), dRS, ALU.mult, ALU.mult)\
                    .then_inc(S("n2_h"), 1)

            def p_round(i):
                for q in range(2):
                    c = i * 2 + q
                    dve.wait_ge(S("p_gfree"), i * 2 + (q + 1))
                    dve.wait_ge(S(f"p_done{q}"), i + 1)
                    v.tensor_tensor(sigp[:, q], sigp[:, q], ps[1][:, 0:T], ALU.mult).then_inc(S("p_efree"), 1)
                    dve.wait_ge(S("p_efree"), i * 2 + (q + 1))
                    wait_prior(dve, S(f"y_out{q}"), i * 16)
                    x = X[:, c:c + 1, :] if isinstance(i, int) else X[:, ds(c, 1), :]
                    v.tensor_tensor(yout[:, q:q + 1, :], x, sigp[:, q:q + 1, :], ALU.add).then_inc(S("y_ready"), 1)
            rounds(dve, 4, p_round)

        @block.gpsimd
        def _(pool):
            for i in range(2):
                if i:
                    pool.wait_ge(S("cd_ready"), 3)
                pool.dma_start(dE[:, HIST + SEQ:EXT].rearrange("p (b t) -> p b t", b=DB)[:, :, 0:HIST],
                                   a["phist"][i]).then_inc(S("pool_in"), 16)

            pool.wait_ge(S("cd_over"), 1)
            for s in range(2):
                pool.dma_start(gw[:, s], a["wge"][s]).then_inc(S(f"gw_in{s}"), 16)

            def gates_out(i, more):
                for s in range(2):
                    for part in range(3):
                        m = 3 * s + part
                        pool.wait_ge(S("gate_out"), i * 6 + (m + 1))
                        pool.dma_start(gates[ds(i * 2 + s, 1), :, part * PART:part * PART + PART].rearrange(
                            "o p t -> (o p) t"), gstage[:, m % 2]).then_inc(S(f"gate_stored{m % 2}"), 16)
                    if more:
                        pool.dma_start(gw[:, s], a["wge"][ds(i * 2 + (s + 2), 1)].rearrange("o p k m -> (o p) k m"))\
                            .then_inc(S(f"gw_in{s}"), 16)
            rounds(pool, UNITS // 2 - 1, lambda i: gates_out(i, True))
            gates_out(UNITS // 2 - 1, False)

            def up_low(c, half):
                pool.wait_ge(S("u_hi"), c * 2 + (half + 1))
                nc.gpsimd.tensor_tensor(Ul[:, half], uraw[:, half], Uh[:, half].bitcast(F32), ALU.subtract)\
                    .then_inc(S("u_lo"), 1)

            def w_round(i, last=False):
                for half in range(2):
                    up_low(i * 2 + 1, half)
                if not last:
                    up_low(i * 2 + 2, 0)
                pool.wait_ge(S("d_hi"), i + 1)
                nc.gpsimd.tensor_tensor(Dl, draw, Dh.bitcast(F32), ALU.subtract).then_inc(S("d_lo"), 1)
                if not last:
                    up_low(i * 2 + 2, 1)
            for half in range(2):
                up_low(0, half)
            rounds(pool, 10, w_round)
            w_round(10, True)

            def y_round(i):
                for q in range(2):
                    pool.wait_ge(S("y_ready"), i * 2 + (q + 1))
                    dst = (o["y"][i * 2 + q] if isinstance(i, int) else
                           o["y"][ds(i * 2 + q, 1)].rearrange("o p t -> (o p) t"))
                    pool.dma_start(dst, yout[:, q]).then_inc(S(f"y_out{q}"), 16)
            rounds(pool, 4, y_round)


_OUTS = [("y", (KD, P, T)), ("k_cm", (P, 2, T)), ("v_p", (P, NCH, HW)), ("v_s", (NS, HW)),
         ("hgrn_p", (2, P, P)), ("hgrn_s", (2, P, DB, P)), ("h_p", (P, 2)), ("h_s", (P, 2, DB)),
         ("convc_p", (P, 2, 3)), ("convc_s", (2, P, DB, 3)), ("pool_p", (P, 2, HIST)), ("pool_s", (2, P, DB, HIST)),
         ("ffn_out", (P, NF, 2, 18))]


def constants():
    con = np.zeros((P, NCON), np.float32)

    def put(name, x):
        con[:x.shape[0], CON[name]:CON[name] + x.shape[1]] = x
    i = np.arange(P)
    head = i // HD
    put("ident", np.eye(P))
    put("mean", np.full((P, P), 1.0 / D))
    put("headmean", (head[:, None] == head[None]) / HD)
    put("bd", head[:, None] == head[None])
    put("strict", i[None] < i[:, None])
    put("notstrict", i[None] >= i[:, None])
    j = np.arange(NS)
    new = (i[:, None] // 16 == j[None] // DL) & (j[None] % DL < i[:, None] % DL)
    put("newkeys", new)
    put("notnewkeys", ~new)
    win = np.array([[2, 8], [4, 16]])[head]
    put("invw", 1.0 / win)
    t = np.arange(HIST)
    for k in range(2):
        con[:, CON["corr"] + k * HIST:CON["corr"] + (k + 1) * HIST] = \
            win[:, k:k + 1] / np.minimum(t[None] + 1, win[:, k:k + 1])
    put("batch", j[:, None] // DL == np.arange(DB)[None])
    masks = np.zeros((P, NL, P), np.int32)
    s, t = i[:, None], i[None]
    for n, m in enumerate(LEVELS):
        masks[:, n] = (s // (2 * m) == t // (2 * m)) & (s % (2 * m) < m) & (t % (2 * m) >= m)
    masks[:, NL - 1] = s == t
    return con, masks, np.ascontiguousarray(masks[:NS, 5:8, :NS])


def kernel(**inputs):
    import concourse.bacc as bacc
    from concourse.bass_utils import run_bass_kernel_spmd

    x = {k: np.asarray(v) for k, v in inputs.items()}

    def tokens(p, s):
        y = np.concatenate([p.reshape(SEQ, -1), s.reshape(NS, -1)], 0).T
        return y.reshape(-1, P, T)

    def weights(w):
        k, m = w.shape
        return w.reshape(k // P, P, m // P, P).transpose(2, 1, 0, 3)

    def cols(w):
        return w.reshape(-1, P).T

    w_in = x["w_in"][0]
    wz = np.concatenate([w_in[:, c:c + 256] for c in Z_COLS], 1)
    wg = w_in[:, 2560:].reshape(KD, P, 4, 4, 2, P).transpose(3, 1, 4, 2, 0, 5).reshape(4, P, 8, KD, P)
    wb = x["w_branch"][0].reshape(4, 2, P, KD, P).transpose(3, 2, 0, 1, 4)
    wvi = np.concatenate([w_in[:, 512:768], w_in[:, 1280:1536]], 1).reshape(KD, P, 512).transpose(1, 0, 2)

    def blockdiag(w):
        y = np.zeros((P, 2, P), w.dtype)
        for h in range(4):
            r = (h % 2) * HD
            y[r:r + HD, h // 2, r:r + HD] = w[h]
        return y

    wrg = np.stack([blockdiag(x["w_rg_a"][0]), blockdiag(x["w_rg_x"][0])], 2)
    par = np.zeros((P, NPAR), np.float32)

    def put(name, v):
        par[:, PAR[name]:PAR[name] + v.shape[1]] = v
    for name in ("norm_mix", "norm_ffn", "norm_ple", "conv_c_b", "b_rg_a", "b_rg_x", "lam", "pool_scale"):
        put(name, cols(x[name][0]))
    put("conv_c_w", cols(x["conv_c_w"][0]))
    for name in ("q_norm", "k_norm", "hgrn_norm"):
        put(name, np.tile(x[name][0], 2)[:, None])
    put("sb_head", np.broadcast_to(x["sb_bias"][0], (P, NH)))
    put("sb_row", x["sb_bias"][0][(np.arange(P) % 16) // 4][:, None])
    cw = x["conv_f_w"][0].reshape(3, 2, NF, P)
    fpar = np.concatenate([cw, x["conv_f_b"][0].reshape(1, 2, NF, P)], 0).transpose(3, 2, 1, 0).reshape(P, NF, 8)
    fhist = x["state_ffn_conv"][0].reshape(DB, 2, 2, NF, P).transpose(4, 3, 2, 0, 1)
    s0 = np.zeros((P, 2, DB, P), np.float32)
    for h in range(4):
        r = (h % 2) * HD
        s0[r:r + HD, h // 2, :, r:r + HD] = x["state_hgrn"][0][:, h].transpose(1, 0, 2)
    con, masks, smasks = constants()
    arrays = {
        "x": tokens(x["x_prompt"], x["x_sample"]),
        "wz": weights(wz), "wge": wg[:, :, 0:EARLY].transpose(0, 2, 1, 3, 4).reshape(UNITS, P, KD, P),
        "wgl": wg[:, :, EARLY:], "wb": wb, "wvi": wvi, "wrg": wrg, "wpool": blockdiag(x["w_pool"][0]),
        "wo": weights(x["w_out"][0]),
        "wu": x["w_up"][0].reshape(KD, P, 2, NF, P).transpose(3, 1, 2, 0, 4),
        "wd": x["w_down"][0].reshape(NF // 2, 2, P, KD, P).transpose(0, 2, 1, 3, 4),
        "wpg": weights(x["w_ple_gate"][0]), "wpl": weights(x["w_ple"][0]),
        "pe": tokens(x["p_prompt"][0], x["p_sample"][0]),
        "par": par, "fpar": fpar, "fhist": fhist, "con": con, "masks": masks, "smasks": smasks,
        "chist": x["state_rglru_conv"][0].reshape(DB, 3, 2, P).transpose(3, 2, 0, 1),
        "ch0": x["state_rglru_h"][0].reshape(DB, 2, P).transpose(2, 1, 0),
        "phist": x["state_pool"][0].reshape(DB, HIST, 2, P).transpose(2, 3, 0, 1),
        "s0": s0,
        "ck": x["cache_k"][0].reshape(-1, P, 2, P).transpose(0, 3, 2, 1),
        "cv": x["cache_v"][0].reshape(-1, P, HW),
        "pt": x["page_table"],
    }
    nc = bacc.Bacc("TRN2", target_bir_lowering=False, num_devices=1)
    arrays = {f"in_{k}": np.ascontiguousarray(v) for k, v in arrays.items()}
    ins = {k[3:]: nc.dram_tensor(k, v.shape, mybir.dt.from_np(v.dtype), kind="ExternalInput").ap()
           for k, v in arrays.items()}
    outs = {n: nc.dram_tensor(f"out_{n}", s, F32, kind="ExternalOutput").ap() for n, s in _OUTS}
    program(nc, ins, outs)
    got = run_bass_kernel_spmd(nc, [arrays], core_ids=[0]).results[0]
    g = {n: np.asarray(got[f"out_{n}"]) for n, _ in _OUTS}

    y = g["y"].reshape(D, T).T
    k = g["k_cm"].transpose(2, 1, 0).reshape(T, NH, HD)

    def heads(s):
        return [s[h // 2][(h % 2) * HD:(h % 2) * HD + HD, ..., (h % 2) * HD:(h % 2) * HD + HD] for h in range(4)]

    fo = g["ffn_out"].transpose(3, 2, 1, 0).reshape(18, 2 * FF)
    c = np.ascontiguousarray
    return (c(y[:SEQ].reshape(1, SEQ, D)), c(y[SEQ:].reshape(DB, DL, D)),
            c(k[:SEQ].reshape(1, 1, SEQ, NH, HD)),
            c(g["v_p"].transpose(1, 0, 2).reshape(1, 1, SEQ, NH, HD)),
            c(k[SEQ:].reshape(1, DB, DL, NH, HD)), c(g["v_s"].reshape(1, DB, DL, NH, HD)),
            c(np.stack(heads(g["hgrn_p"]))[None, None]),
            c(np.stack(heads(g["hgrn_s"])).transpose(2, 0, 1, 3)[None]),
            c(g["h_p"].T.reshape(1, 1, HW)), c(g["h_s"].transpose(2, 1, 0).reshape(1, DB, HW)),
            c(g["convc_p"].transpose(2, 1, 0).reshape(1, 1, 3, HW)),
            c(g["convc_s"].transpose(2, 3, 0, 1).reshape(1, DB, 3, HW)),
            c(g["pool_p"].transpose(2, 1, 0).reshape(1, 1, HIST, HW)),
            c(g["pool_s"].transpose(2, 3, 0, 1).reshape(1, DB, HIST, HW)),
            c(fo[:2].reshape(1, 1, 2, 2 * FF)), c(fo[2:].reshape(1, DB, 2, 2 * FF)))
```

```python
from contextlib import ExitStack

import numpy as np

import concourse.bass as bass
from concourse import mybir

F32 = mybir.dt.float32
F32R = mybir.dt.float32r
I32 = mybir.dt.int32
ALU = mybir.AluOpType
ACT = mybir.ActivationFunctionType
ds = bass.ds

P = 128
D = 1024
SEQ = 1024
DB, DL = 8, 4
NS = DB * DL
T = SEQ + NS
KD = D // P
HW = D // 4
HD = 64
NH = 4
PAGES = 4
PAST = PAGES * P
FF = 2816
NF = FF // P
DPLE = 256
KP = DPLE // P
EPS = 1e-6
CH = 128
NCH = SEQ // CH
SPANS = ((0, 512), (512, 512), (1024, NS))
HIST = 15
EXT = HIST + SEQ + DB * (HIST + DL)
XC, FB, QB, KA, XD, GC, GB, QA = range(0, 16, 2)
Z_COLS = (1792, 1024, 768, 256, 2304, 2048, 1536, 0)
BRANCH_AT = (QA, GB, GC, XD)
X_SEMS = (0, 1, 2, 3, 4, 4, 5, 5)
X_COUNTS = (16, 16, 16, 16, 32, 32, 48, 48)
LEVELS = (64, 32, 16, 8, 4, 2, 1)
NL = len(LEVELS) + 1


def table(*entries):
    at, n = {}, 0
    for name, width in entries:
        at[name] = n
        n += width
    return at, n


PAR, NPAR = table(("norm_mix", KD), ("norm_ffn", KD), ("norm_ple", KD), ("conv_c_w", 8), ("conv_c_b", 2),
                  ("b_rg_a", 2), ("b_rg_x", 2), ("lam", 2), ("pool_scale", 2), ("q_norm", 1), ("k_norm", 1),
                  ("hgrn_norm", 1), ("sb_head", NH), ("sb_row", 1))
CON, NCON = table(("ident", P), ("mean", P), ("headmean", P), ("bd", P), ("strict", P), ("notstrict", P),
                  ("newkeys", NS), ("notnewkeys", NS), ("invw", 2), ("corr", 2 * HIST), ("batch", DB))
NR = 23500
EARLY = 3
LATE = 8 - EARLY
UP = KD // 2
PLE = UP + NF
DOWN_SLOTS = (0, 2, 0, 1, 0, 1, 0, 1)
ADDED = tuple(sum(3 if s == 2 else 1 for s in DOWN_SLOTS[:d + 1]) for d in range(KD))
PART = T // 3
UNITS = 4 * EARLY
PLACES = (("start0", 5), ("states0", 3), ("levels0", 3), ("start1", 2), ("states1", 3), ("levels1", 3),
          ("norms", 1), ("normed", 2), ("steps", 8), ("samples", 6))


def parts(place):
    first = 0
    for name, n in PLACES:
        if name == place:
            return range(first, first + n)
        first += n
    assert False, place


assert sum(n for _, n in PLACES) == 3 * UNITS


class Link:

    def __init__(self, eng, sem):
        self.eng, self.sem, self.base, self.n = eng, sem, 0, 0

    def __call__(self, *inss):
        for ins in inss:
            ins.then_inc(self.sem, 1)
            self.n += 1
        self.eng.wait_ge(self.sem, self.base + self.n)

    def rounds(self, times, body):
        first = self.n
        body(0)
        per = self.n - first
        with self.eng.Fori(1, times) as i:
            self.base, self.n = i * per, first
            body(i)
            assert self.n == first + per
        self.base, self.n = 0, first + times * per


def rounds(eng, times, body):
    body(0)
    with eng.Fori(1, times) as i:
        body(i)


def wait_prior(eng, sem, value):
    if not isinstance(value, int) or value > 0:
        eng.wait_ge(sem, value)


def program(nc, a, o):
    with ExitStack() as ctx:
        def sb(name, shape, dt=F32):
            return ctx.enter_context(nc.sbuf_tensor(name, shape, dt))

        sems = {}

        def S(name):
            if name not in sems:
                sems[name] = ctx.enter_context(nc.semaphore(name))
            return sems[name]

        par = sb("par", [P, NPAR])
        con = sb("con", [P, NCON])
        masks = sb("masks", [P, NL, P], I32)
        smasks = sb("smasks", [NS, 3, NS], I32)
        fpar = sb("fpar", [P, NF, 8])
        small = sb("small", [P, 96])
        arena_at = -(-nc.sbuf_base // 32) * 32
        H = sb("H", [P, KD, T])
        BIG = sb("BIG", [P, 16 * T + NR])
        assert nc.sbuf_base == arena_at + 4 * (24 * T + NR)
        FH = sb("FH", [P, NF, 2, DB, 2])
        FO = sb("FO", [P, NF, 2, 18])
        Z = BIG[:, 0:16 * T].rearrange("p (c t) -> p c t", c=16)
        R0 = 16 * T
        ps = [ctx.enter_context(nc.psum_tensor(f"ps{s}", [P, 1536], F32)) for s in range(2)]
        pst = [ctx.enter_context(nc.psum_tensor(f"pst{s}", [P, 512], F32)) for s in range(2)]
        gbank = ps[1][:, 1024:1024 + PART]
        gates = nc.dram_tensor("gates", (UNITS, P, T), F32, kind="Internal").ap()

        def rounded(name, word, *shape):
            at = arena_at + 4 * (8 * T + word)
            return nc.alloc_sbuf_tensor_at(name, [P, *shape], F32R, offset=at, align_bytes=32)[:]

        def pc(name, j=0, n=1):
            return par[:, PAR[name] + j:PAR[name] + j + n]

        def cc(name, n=P, j=0, p=P):
            return con[0:p, CON[name] + j:CON[name] + j + n]

        class Region:

            def __init__(self, at=0):
                self.at = R0 + at

            def take(self, *shape):
                n = 1
                for s in shape:
                    n *= s
                v = BIG[:, self.at:self.at + n]
                self.at += n
                assert self.at <= R0 + NR, self.at - R0
                names = "abcd"[:len(shape)]
                if len(shape) > 1:
                    v = v.rearrange(f"p ({' '.join(names)}) -> p {' '.join(names)}",
                                    **{x: s for x, s in zip(names, shape)})
                return v

        r = Region()
        VT = r.take(NCH + 1, 512)
        base = r.at - R0
        zw = r.take(2, KD, P)
        wvi = r.take(KD, 512)
        wrg = r.take(2, 2, P)
        wpool = r.take(2, P)
        chist = r.take(2, DB, 3)
        ch0 = r.take(2, DB)
        at = r.at - R0
        SS, RS, SQ = r.take(T), r.take(T), r.take(2, T)
        r = Region(at)
        cX, cR, cI = r.take(2, T), r.take(2, T), r.take(2, T)
        cA, cB = r.take(T), r.take(T)
        cext = r.take(DB, 7)
        dE, dF = r.take(EXT), r.take(EXT)
        xin = Z[:, 8:16, :]
        r = Region(base)
        bB = r.take(2, T)
        KF, QF = r.take(2, T), [r.take(2, T), r.take(2, T)]
        QE = r.take(T)
        kdt = Region(base + 2 * T).take(NCH + 1, P)
        att = r.take(NCH, 2, P)
        atts = r.take(2, NS)
        Sall = r.take(NCH + 1, P)
        S0 = r.take(2, DB, P)
        vbd = r.take(DB, P)
        bdec = r.take(16)
        assert r.at <= R0 + NR - 2 * KD * P - 2 * PART
        tA = Z[:, XC:XC + 2, :]
        bd_, bE = Z[:, XC, :], Z[:, XC + 1, :]
        rmask = QE
        r = Region(NR - 2 * KD * P - 2 * PART)
        gw = r.take(2, KD, P)
        gstage = r.take(2, PART)
        r = Region(base)
        keep, beta, Pp = r.take(2, SEQ), r.take(2, SEQ), r.take(2, SEQ + 8)
        wT = r.take(2, SEQ)
        QS = r.take(2, 1152)
        QSall = r.take(2, P)
        pages = r.take(5, PAST * 2)
        negb = r.take(8)
        assert r.at <= R0 + NR - 2 * KD * P - 2 * PART
        qm = Z[:, FB:FB + 4, :]
        kp = [x.rearrange("p (g i t) -> p g i t", g=PAGES, i=2) for x in
              (pages[:, 0], pages[:, 1], Z[:, XC, 0:PAST * 2], Z[:, XC + 1, 0:PAST * 2])]
        vp = [x.rearrange("p (g c) -> p g c", g=PAGES) for x in
              (*(pages[:, 2 + b] for b in range(3)), *(qm[:, h, 0:PAST * 2] for h in range(NH)), keep[:, 1])]
        r = Region()
        MIX = r.take(KD, T)
        Ht = rounded("Ht", R0 + base + 2 * SEQ, 2, T)
        at = max(r.at - R0, base + 2 * SEQ + 2 * T)
        r = Region(at)
        early = r.take(EARLY, T)
        SIG = r.take(2, T)
        mwb = r.take(2, 4, 2, P)
        uraw = r.take(2, KD, P)
        Uh = rounded("Uh", r.at, 2, KD, P)
        Ul = rounded("Ul", r.at + 2 * KD * P, 2, KD, P)
        ACC = Region(r.at - R0 + 4 * KD * P).take(T)
        Hh, Hl = rounded("Hh", -8 * T, KD, T), rounded("Hl", 0, KD, T)
        SPLIT = (0, 1, 6, 7, 2, 3, 4, 5)
        X = Z[:, 0:KD, :]
        r = Region(at)
        r.take(2, KD, P)
        nSQ, nSS, nRS, ntmp = r.take(T), r.take(T), r.take(T), r.take(2, T)
        Ml = rounded("Ml", R0, KD, T)
        Fl = rounded("Fl", 8 * T, KD, T)
        Gh, Gl = rounded("Gh", R0, 2, T), rounded("Gl", R0 + 2 * T, 2, T)
        Dh, Dl = rounded("Dh", R0 + 4 * T, 2, KD, P), rounded("Dl", R0 + 4 * T + 2 * KD * P, 2, KD, P)
        assert 4 * T + 4 * KD * P <= at
        draw = Region(at).take(2, KD, P)
        V = Region(at + 2 * KD * P).take(2, T)
        dSQ, dSS, dRS = ntmp[:, 0], ntmp[:, 1], nRS
        sigp, yout = V, Region(at + 2 * KD * P + 2 * T).take(2, T)

        def slot(s):
            if s == 2:
                return [pst[0][:, 0:512], pst[1][:, 0:512], ps[1][:, T:T + NS]]
            return [ps[s][:, t0:t0 + n] for t0, n in SPANS]

        def m_slot(u):
            return u % 2 if u < EARLY else 1

        block = ctx.enter_context(nc.Block())

        @block.sync
        def _(sp):
            sp.dma_start(zw[:, 0], a["wz"][0]).then_inc(S("zw_in0"), 16)
            sp.dma_start(par[:], a["par"]).then_inc(S("params_in"), 16)
            for k in range(KD):
                sp.dma_start(xin[:, k, :], a["x"][k]).then_inc(S(f"x_in{X_SEMS[k]}"), 16)
                if k == KD - 3:
                    sp.dma_start(con[:], a["con"]).then_inc(S(f"x_in{X_SEMS[-1]}"), 16)
                if k == 0:
                    sp.dma_start(zw[:, 1], a["wz"][1]).then_inc(S("zw_in1"), 16)
            sp.dma_start(wrg, a["wrg"]).then_inc(S("cd_in"), 16)
            sp.dma_start(wpool, a["wpool"]).then_inc(S("cd_in"), 16)
            sp.dma_start(chist, a["chist"]).then_inc(S("cd_in"), 16)
            sp.dma_start(ch0, a["ch0"]).then_inc(S("cd_in"), 16)
            sp.dma_start(wvi, a["wvi"]).then_inc(S("wvi_in"), 16)
            sp.dma_start(masks[:], a["masks"]).then_inc(S("tables_in"), 16)
            sp.dma_start(smasks[:], a["smasks"]).then_inc(S("tables_in"), 16)
            sp.dma_start(fpar[:], a["fpar"]).then_inc(S("tables_in"), 16)
            sp.dma_start(FH[:], a["fhist"]).then_inc(S("tables_in"), 16)

            with sp.Fori(1, 8) as i:
                for s in range(2):
                    sp.wait_ge(S(f"z_done{s}"), i)
                    sp.dma_start(zw[:, s], a["wz"][ds(i * 2 + s, 1)].rearrange("o p k m -> (o p) k m"))\
                        .then_inc(S(f"zw_in{s}"), 16)
            outs = 0

            def out(name, src, idx=None):
                nonlocal outs
                dst = o[name] if idx is None else o[name][idx]
                sp.dma_start(dst, src).then_inc(S("stored"), 16)
                outs += 16

            for s in range(2):
                sp.wait_ge(S(f"z_free{s}"), 8)
            out("convc_p", Z[:, XC:XC + 2, SEQ - 3:SEQ])
            for i in range(2):
                out("convc_s", Z[:, XC + i, SEQ:T].rearrange("p (b t) -> p b t", b=DB)[:, :, 1:4], i)
                sp.dma_start(o["pool_s"][i][:, :, HIST - DL:], Z[:, XD + i, SEQ:T].rearrange("p (b t) -> p b t", b=DB))\
                    .then_inc(S("stored"), 16)
                sp.dma_start(o["pool_s"][i][:, :, 0:HIST - DL], a["phist"][i][:, :, DL:]).then_inc(S("stored"), 16)
                outs += 32
            out("pool_p", Z[:, XD:XD + 2, SEQ - HIST:SEQ])
            sp.wait_ge(S("stored"), outs)
            sp.sem_inc(S("raw_stored"), 1)
            sp.wait_ge(S("vt_free"), NCH + 1)
            out("v_p", VT[:, 0:NCH, 0:HW])
            out("v_s", VT[0:NS, NCH, 0:HW])
            sp.wait_ge(S("c_scanned"), 2)
            sp.wait_ge(S("c_out"), 2)
            out("h_p", small[:, 40:42])
            out("h_s", small[:, 48:64].rearrange("p (i b) -> p i b", i=2))
            sp.wait_ge(S("cd_over"), 1)
            sp.dma_start(S0[:], a["s0"]).then_inc(S("s0_in"), 16)
            for i in range(2):
                sp.wait_ge(S("b_states"), i + 1)
                out("hgrn_p", Sall[:, NCH, :], i)
                out("hgrn_s", vbd, i)
                sp.wait_ge(S("stored"), outs)
                sp.sem_inc(S("states_stored"), 1)
            sp.wait_ge(S("a_normed"), 2)
            out("k_cm", Z[:, KA:KA + 2, :])
            sp.wait_ge(S("b_over"), 2)
            for b in range(DB):
                if b == 3:
                    sp.wait_ge(S("stored"), outs)
                    sp.wait_ge(S("a_sc"), 32)
                if b >= 4:
                    sp.wait_ge(S("kp_used"), b - 3)
                if b == 7:
                    sp.wait_ge(S("a_w"), 32)
                for g in range(PAGES):
                    page = sp.value_load(a["pt"][b:b + 1, g:g + 1], min_val=0, max_val=39)
                    sp.dma_start(kp[b % 4][:, g], a["ck"][ds(page, 1)].rearrange("o p i t -> (o p) i t"))\
                        .then_inc(S(f"pages_in{b % 4}"), 16)
                    sp.dma_start(vp[b][:, g], a["cv"][ds(page, 1)].rearrange("o p c -> (o p) c"))\
                        .then_inc(S(f"pages_in{b % 4}"), 16)

            def early_gates(i):
                for g, (n, m) in enumerate(((0, 1), (1, EARLY - 1))):
                    sp.dma_start(early[:, n:n + m], gates[ds(i * EARLY + n, m)].rearrange("n p t -> p n t"))\
                        .then_inc(S(f"early_in{g}"), 16)

            def late_weights(i, v):
                src = a["wgl"][i, v] if isinstance(i, int) else a["wgl"][ds(i, 1), v].rearrange("o p k m -> (o p) k m")
                sp.dma_start(uraw[:, v % 2], src).then_inc(S(f"mg_in{v % 2}"), 16)

            def branch_weights(i, q):
                src = a["wb"][q] if isinstance(i, int) else \
                    a["wb"][ds(i * 2 + q, 1)].rearrange("o p n k m -> (o p) n k m")
                sp.dma_start(mwb[:, q], src).then_inc(S(("mw_in", "mb_in")[q]), 16)
            sp.wait_ge(S("kp_used"), DB)
            sp.wait_ge(S("as_sc"), 1)
            branch_weights(0, 0)
            branch_weights(0, 1)
            late_weights(0, 0)
            sp.wait_ge(S("vp_used"), 1)
            late_weights(0, 1)
            sp.wait_ge(S("a_over"), 2)
            for s in range(2):
                sp.wait_ge(S(f"gate_stored{s}"), 16 * 3 * UNITS // 2)
            early_gates(0)
            for v in range(2, LATE):
                sp.wait_ge(S("m_lo"), v - 1)
                late_weights(0, v)
            with sp.Fori(1, 4) as i:
                sp.wait_ge(S("m_proj"), i * 8 - 4)
                branch_weights(i, 0)
                sp.wait_ge(S("m_sig"), i * 8 + (EARLY - 8))
                early_gates(i)
                for v in range(2):
                    sp.wait_ge(S("m_lo"), i * LATE)
                    late_weights(i, v)
                sp.wait_ge(S("m_proj"), i * 8)
                branch_weights(i, 1)
                for v in range(2, LATE):
                    sp.wait_ge(S("m_lo"), i * LATE + (v - 1))
                    late_weights(i, v)

            def tiles(r, src):
                for half in range(2):
                    if isinstance(r, int) and r == 0:
                        sp.wait_ge(S("m_lo"), 4 * LATE)
                    else:
                        sp.wait_ge(S("u_lo"), r * 2 + (half - 1))
                    sp.dma_start(uraw[:, half], src(half)).then_inc(S(f"uw_in{half}"), 16)

            def outer(name, i, half):
                x = a[name]
                return x[i * 2 + half] if isinstance(i, int) else x[ds(i * 2 + half, 1)].rearrange("o p k m -> (o p) k m")

            def up_weights(c):
                tiles(c + UP, lambda half: a["wu"][c, :, half] if isinstance(c, int) else
                      a["wu"][ds(c, 1), :, half].rearrange("o p k m -> (o p) k m"))

            tiles(0, lambda half: outer("wo", 0, half))
            sp.wait_ge(S("m_gate"), 4 * LATE)
            for q in range(2):
                sp.dma_start(X[:, q, :], a["x"][q]).then_inc(S(f"x_in{q}"), 16)
            with sp.Fori(1, 4) as i:
                tiles(i, lambda half: outer("wo", i, half))
                for q in range(2):
                    sp.wait_ge(S(f"x_in{q}"), i * 16 + 16)
                    sp.dma_start(X[:, ds(i * 2 + q, 1), :], a["x"][ds(i * 2 + q, 1)].rearrange("o p t -> p o t"))\
                        .then_inc(S(f"x_in{q}"), 16)
            up_weights(0)
            up_weights(1)
            sp.wait_ge(S("n2_h"), 8)
            sp.dma_start(draw, a["wd"][0]).then_inc(S("d_in"), 16)
            with sp.Fori(1, 11) as i:
                up_weights(i * 2)
                sp.wait_ge(S("d_lo"), i)
                sp.dma_start(draw, a["wd"][ds(i, 1)].rearrange("o p k d m -> (o p) k d m")).then_inc(S("d_in"), 16)
                up_weights(i * 2 + 1)

            def gate_weights(i):
                tiles(i + PLE, lambda half: outer("wpg", i, half))
            gate_weights(0)
            sp.wait_ge(S("d_lo"), NF // 2)
            sp.dma_start(draw, a["wpl"]).then_inc(S("d_in"), 16)
            sp.wait_ge(S("g_ready"), NF)
            sp.dma_start(V, a["pe"]).then_inc(S("pe_in"), 16)
            sp.wait_ge(S("d_added"), 11 * ADDED[-1])
            out("ffn_out", FO[:])
            with sp.Fori(1, 4) as i:
                gate_weights(i)
            sp.wait_ge(S("stored"), outs)
            sp.wait_ge(S("y_out0"), 64)
            sp.wait_ge(S("y_out1"), 64)

        @block.tensor
        def _(pe):
            def dense(out, w, rhs, kk, first=True, last=True):
                ins = None
                for k in range(kk):
                    for t0, n in SPANS:
                        ins = nc.tensor.matmul(out[:, t0:t0 + n], w[:, k], rhs[:, k, t0:t0 + n],
                                               start=first and k == 0, stop=last and k == kk - 1)
                return ins

            def whole(out, w, rhs, first=True, last=True):
                for t0, n in SPANS:
                    ins = nc.tensor.matmul(out[:, t0:t0 + n], w, rhs[:, t0:t0 + n], start=first, stop=last)
                return ins

            def gate(p, halves=(0, 1)):
                u, part = divmod(p, 3)
                if 0 in halves:
                    if part == 0:
                        pe.wait_ge(S(f"gw_in{u % 2}"), 16 * (u // 2 + 1))
                    if p:
                        pe.wait_ge(S("gate_out"), p)
                for k in range(4 * halves[0], 4 * halves[-1] + 4):
                    ins = nc.tensor.matmul(gbank, gw[:, u % 2, k], H[:, k, part * PART:part * PART + PART],
                                           start=(k == 0), stop=(k == KD - 1))
                if 1 in halves:
                    ins.then_inc(S("gate_done"), 1)

            def dense3(out, w, x, kk, ready=None):
                for k in range(kk):
                    if ready is not None:
                        pe.wait_ge(S(ready[0]), ready[1] + k + 1)
                    for wp, xp in ((0, 0), (0, 1), (1, 0)):
                        for (t0, n), dst in zip(SPANS, slot(out)):
                            ins = nc.tensor.matmul(dst, w[wp][:, k], x[xp][:, k, t0:t0 + n],
                                                   start=(k == 0 and wp == xp), stop=(k == kk - 1 and wp == 1))
                return ins

            for k in range(KD):
                if k == KD - 2:
                    ins.then_inc(S("n1_read"), 1)
                    pe.wait_ge(S(f"x_in{X_SEMS[-1]}"), X_COUNTS[-1])
                    pe.wait_ge(S("n1_ss"), 8)
                    for g, (t0, n) in enumerate(SPANS):
                        if g == 2:
                            pe.wait_ge(S("n1_ln"), 1)
                        nc.tensor.matmul(pst[g % 2][:, 0:n], cc("mean"), SS[:, t0:t0 + n], start=True, stop=True)\
                            .then_inc(S("norm_sum"), 1)
                pe.wait_ge(S("n1_x"), k + 1)
                for s in range(2):
                    if k == 0:
                        pe.wait_ge(S(f"zw_in{s}"), 16)
                    ins = dense(ps[s], zw[:, s, k:k + 1], H[:, k:k + 1], 1, k == 0, k == KD - 1)
                    if k == KD - 1:
                        ins.then_inc(S(f"z_done{s}"), 1)

            def z_round(i):
                for s in range(2):
                    pe.wait_ge(S(f"zw_in{s}"), i * 16 + 16)
                    wait_prior(pe, S(f"z_free{s}"), i)
                    for k in range(KD):
                        if isinstance(i, int) and s == 0:
                            pe.wait_ge(S("n1_h"), k + 1)
                        ins = dense(ps[s], zw[:, s, k:k + 1], H[:, k:k + 1], 1, k == 0, k == KD - 1)
                    ins.then_inc(S(f"z_done{s}"), 1)
            z_round(1)
            with pe.Fori(2, 8) as i:
                z_round(i)

            def unit(u, w, x, ready):
                pe.wait_ge(S("cd_ready"), ready)
                if 2 <= u < 4:
                    pe.wait_ge(S("cd_free"), u - 1)
                elif u >= 4:
                    pe.wait_ge(S("vt_free"), u - 3)
                whole(ps[u % 2], w, x).then_inc(S("cd_done"), 1)

            def tokens(t):
                n = P if t < NCH else NS
                if t < 4:
                    pe.wait_ge(S("cd_free"), t + 3)
                else:
                    pe.wait_ge(S("vt_free"), t - 1)
                for k in range(KD):
                    ins = nc.tensor.matmul(ps[t % 2][0:n, 0:512], H[:, k, t * P:t * P + n], wvi[:, k, :],
                                           start=(k == 0), stop=(k == KD - 1))
                ins.then_inc(S("vt_done"), 1)

            pe.wait_ge(S("cd_in"), 64)
            for s in range(2):
                pe.wait_ge(S(f"z_free{s}"), 8)
            for i in range(2):
                for g in range(2):
                    unit(2 * i + g, wrg[:, i, g], cX[:, i], i + 1)
            pe.wait_ge(S("wvi_in"), 16)
            tokens(0)
            tokens(1)
            for i in range(2):
                unit(4 + i, wpool[:, i], Z[:, XD + i], 3 + i)
            for t in range(2, NCH + 1):
                tokens(t)
            pe.wait_ge(S("vt_free"), NCH + 1)

            for i in range(2):
                for p in parts(f"start{i}"):
                    gate(p)
                pe.wait_ge(S("b_kd"), i + 1)
                for g in range(3):
                    n = 3 * i + g
                    if n >= 2:
                        pe.wait_ge(S("b_tfree"), n - 1)
                    for c in range(4 * g, min(4 * g + 4, NCH + 1)):
                        m = P if c < NCH else NS
                        ins = nc.tensor.transpose(pst[n % 2][0:m, (c % 4) * P:(c % 4) * P + P],
                                                  bE[:, c * P:c * P + m], cc("ident"))
                    ins.then_inc(S("b_tdone"), 1)
                pe.wait_ge(S("b_tfree"), 3 * i + 3)
                pe.wait_ge(S("b_vbd"), i + 1)
                if i:
                    pe.wait_ge(S("b_over"), 1)
                for c in range(NCH):
                    ins = nc.tensor.matmul(ps[0][:, c * P:c * P + P], kdt[:, c, :],
                                           VT[:, c, HW + i * P:HW + i * P + P], start=(c % 4 == 0), stop=True,
                                           skip_group_check=True)
                for b in range(2):
                    ins = nc.tensor.matmul(ps[1][:, b * 512:b * 512 + 512], kdt[0:NS, NCH, :],
                                           vbd[0:NS, 4 * b:4 * b + 4, :], start=True, stop=True)
                ins.then_inc(S("b_u"), 1)
                for p in parts(f"states{i}"):
                    gate(p)
                pe.wait_ge(S("b_ufree"), 2 * (i + 1))
                for l in range(NL):
                    n = NL * i + l
                    if 1 <= l <= 6:
                        gate(parts(f"levels{i}")[(l - 1) // 2], ((l - 1) % 2,))
                    pe.wait_ge(S("b_factors"), n + 1)
                    for g in range(4):
                        u = 4 * n + g
                        if g + 4 * l >= 4:
                            pe.wait_ge(S("b_afree"), u - 3)
                        bank = ps[g // 2][:, (g % 2) * 512:(g % 2) * 512 + 512]
                        for j in range(4):
                            c, hh = 2 * g + j // 2, j % 2
                            kf = KF[:, l % 2, c * P:c * P + P] if l < NL - 1 else Z[:, FB + i, c * P:c * P + P]
                            ins = nc.tensor.matmul(bank[:, j * P:j * P + P], kf, QF[hh][:, l % 2, c * P:c * P + P],
                                                   start=(j == 0), stop=True, skip_group_check=True)
                        ins.then_inc(S("b_adone"), 1)
                    if l >= 5:
                        m = 3 * i + l - 5
                        if m >= 1:
                            pe.wait_ge(S("b_sfree"), m)
                        for hh in range(2):
                            kf = KF[:, l % 2, SEQ:T] if l < NL - 1 else Z[:, FB + i, SEQ:T]
                            ins = nc.tensor.matmul(pst[0][0:NS, hh * NS:hh * NS + NS], kf,
                                                   QF[hh][:, l % 2, SEQ:T], start=(hh == 0), stop=True,
                                                   skip_group_check=True)
                        ins.then_inc(S("b_sdone"), 1)
                pe.wait_ge(S("b_afree"), 4 * NL * (i + 1))
                pe.wait_ge(S("b_sfree"), 3 * (i + 1))
                for g in range(4):
                    bank = ps[g // 2][:, (g % 2) * 512:(g % 2) * 512 + 512]
                    first = True
                    for hh in range(2):
                        for c in (2 * g, 2 * g + 1):
                            dst = bank[:, (2 * hh + c % 2) * P:(2 * hh + c % 2) * P + P]
                            if c:
                                nc.tensor.matmul(dst, Sall[:, c, :], QE[:, c * P:c * P + P], start=first,
                                                 stop=False, skip_group_check=True)
                                first = False
                            ins = nc.tensor.matmul(dst, VT[:, c, HW + i * P:HW + i * P + P], att[:, c, hh, :],
                                                   start=first, stop=True, skip_group_check=True)
                            first = False
                ins.then_inc(S("b_odone"), 1)
                pe.wait_ge(S("s0_in"), 16)
                first = True
                for hh in range(2):
                    for b in range(DB):
                        c0 = hh * NS + b * DL
                        nc.tensor.matmul(pst[1][:, c0:c0 + DL], S0[:, i, b, :], QE[:, SEQ + b * DL:SEQ + b * DL + DL],
                                         start=first, stop=False, skip_group_check=True)
                        first = False
                    ins = nc.tensor.matmul(pst[1][:, hh * NS:hh * NS + NS], VT[0:NS, NCH, HW + i * P:HW + i * P + P],
                                           atts[0:NS, hh, :], start=False, stop=True, skip_group_check=True)
                ins.then_inc(S("b_osdone"), 1)
                pe.wait_ge(S("b_osq"), i + 1)
                pe.wait_ge(S("b_ofree"), i + 1)
                whole(ps[0], cc("headmean"), bE).then_inc(S("b_ms"), 1)

            for p in parts("norms"):
                gate(p)
            for j in range(4):
                if j == 1:
                    pe.wait_ge(S("gate_out"), parts("norms")[-1] + 1)
                pe.wait_ge(S("a_sq"), j + 1)
                if j == 0:
                    pe.wait_ge(S("b_over"), 2)
                if j >= 2:
                    pe.wait_ge(S("a_rs"), j - 1)
                whole(ps[j % 2], cc("headmean"), (keep.rearrange("p a b -> p (a b)"), wT.rearrange("p a b -> p (a b)"))[j % 2])\
                    .then_inc(S("a_ms"), 1)
            pe.wait_ge(S("a_rs"), 4)
            for p in parts("normed"):
                gate(p)
            pe.wait_ge(S("a_qm"), 1)
            tgroups = [0]
            for n in range(32):
                tgroups.append(tgroups[-1] + (n // 4 + 4) // 4)

            def scores(n):
                i, h = n // 4, n % 4
                if n >= 2:
                    pe.wait_ge(S("a_scfree"), n - 1)
                w = (i + 1) * P
                for c0 in range(0, w, 512):
                    m = min(512, w - c0)
                    ins = nc.tensor.matmul(ps[n % 2][:, c0:c0 + m], qm[:, h, i * P:i * P + P],
                                           Z[:, KA + h // 2, c0:c0 + m], start=True, stop=True)
                ins.then_inc(S("a_sc"), 1)

            def transposes(n):
                i = n // 4
                pe.wait_ge(S("a_w"), n + 1)
                for g in range(tgroups[n], tgroups[n + 1]):
                    if g >= 2:
                        pe.wait_ge(S("a_tfree"), g - 1)
                    j0 = 4 * (g - tgroups[n])
                    for j in range(j0, min(j0 + 4, i + 1)):
                        ins = nc.tensor.transpose(pst[g % 2][:, (j - j0) * P:(j - j0) * P + P],
                                                  beta[:, n % 2, j * P:j * P + P], cc("ident"))
                    ins.then_inc(S("a_tdone"), 1)

            def values(n):
                i, h = n // 4, n % 4
                pe.wait_ge(S("a_tfree"), tgroups[n + 1])
                if h == 0 and i >= 1:
                    pe.wait_ge(S("a_ofree"), i)
                for j in range(i + 1):
                    ins = nc.tensor.matmul(ps[0][:, 1024 + h * P:1024 + h * P + P],
                                           VT[:, j, (h // 2) * P:(h // 2) * P + P], wT[:, n % 2, j * P:j * P + P],
                                           start=(h == 0 and j == 0), stop=(j == i), skip_group_check=True)
                ins.then_inc(S("a_pv"), 1)

            for n in range(34):
                if n < 32:
                    scores(n)
                    if n % 4 == 1:
                        gate(parts("steps")[n // 4])
                if 1 <= n <= 32:
                    transposes(n - 1)
                if n >= 2:
                    values(n - 2)
            pe.wait_ge(S("a_scfree"), 32)
            pe.wait_ge(S("a_qs"), 1)
            for b in range(DB):
                if b >= 2:
                    gate(parts("samples")[b - 2])
                pe.wait_ge(S(f"pages_in{b % 4}"), 32 * PAGES * (b // 4 + 1))
                for i in range(2):
                    ins = nc.tensor.matmul(ps[0][:, 0:PAST], QS[:, i, b * P:b * P + P], kp[b % 4][:, :, i, :],
                                           start=(b == 0 and i == 0), stop=(b == DB - 1 and i == 1))
                ins.then_inc(S("kp_used"), 1)
            for i in range(2):
                ins = nc.tensor.matmul(ps[0][:, PAST:PAST + NS], QSall[:, i, :], Z[:, KA + i, SEQ:T],
                                       start=(i == 0), stop=(i == 1))
            ins.then_inc(S("as_sc"), 1)
            pe.wait_ge(S("as_w"), 1)
            for j in range(PAGES):
                ins = nc.tensor.transpose(pst[0][:, j * P:j * P + P], beta[:, 0, j * P:j * P + P], cc("ident"))
            ins = nc.tensor.transpose(pst[1][0:NS, 0:P], beta[:, 0, PAST:PAST + NS], cc("ident"))
            ins.then_inc(S("a_tdone"), 1)
            pe.wait_ge(S("a_tfree"), tgroups[32] + 2)
            for i in range(2):
                nc.tensor.matmul(ps[1][:, i * P:i * P + P], VT[0:NS, NCH, i * P:i * P + P], wT[0:NS, 1, 0:P],
                                 start=(i == 0), stop=False, skip_group_check=True)
            for b in range(DB):
                for i in range(2):
                    for g in range(PAGES):
                        ins = nc.tensor.matmul(ps[1][:, i * P + 16 * b:i * P + 16 * b + 16],
                                               vp[b][:, g, i * P:i * P + P],
                                               wT[:, 0, g * P + 16 * b:g * P + 16 * b + 16],
                                               start=False, stop=(g == PAGES - 1), skip_group_check=True)
                ins.then_inc(S("vp_used"), 1)
            pe.wait_ge(S("a_over"), 2)

            def m_round(i):
                for u in range(8):
                    q, n = divmod(u, 4)
                    if u == 0:
                        pe.wait_ge(S("mw_in"), i * 16 + 16)
                    if u == 4:
                        pe.wait_ge(S("mb_in"), i * 16 + 16)
                    if u >= EARLY:
                        v = u - EARLY
                        pe.wait_ge(S("m_lo"), i * LATE + (v + 1))
                        if v == 0:
                            if isinstance(i, int):
                                pe.wait_ge(S("h_lo"), KD)
                                pe.wait_ge(S("h_hi"), KD)
                            pe.wait_ge(S("m_pfree"), i * 8 + EARLY)
                        else:
                            pe.wait_ge(S("m_sig"), i * 8 + u)
                        dense3(0, (Uh[:, v % 2], Ul[:, v % 2]), (Hh, Hl), KD).then_inc(S("m_gate"), 1)
                    elif u == 0:
                        wait_prior(pe, S("m_sig"), i * 8)
                    else:
                        wait_prior(pe, S("m_pfree"), i * 8 + (u - 1))
                    if u >= EARLY or u == 1:
                        wait_prior(pe, S("m_pfree"), i * 8 + (u if u > 1 else 0))
                    dense(ps[m_slot(u)], mwb[:, q, n], Z[:, BRANCH_AT[n]:BRANCH_AT[n] + 2, :], 2)\
                        .then_inc(S("m_proj"), 1)
            rounds(pe, 4, m_round)

            pe.wait_ge(S("m_sig"), 32)
            def o_round(i):
                for q in range(2):
                    pe.wait_ge(S("u_lo"), i * 2 + (q + 1))
                    if q or not isinstance(i, int):
                        wait_prior(pe, S("r_added"), i * 2 + (q - 1) if not isinstance(i, int) else 0)
                    dense3(q, (Uh[:, q], Ul[:, q]), (Hh, Ml), KD,
                           ("h_lo", KD) if q == 0 and isinstance(i, int) else None).then_inc(S(f"r_done{q}"), 1)
            rounds(pe, 4, o_round)
            pe.wait_ge(S("r_ss"), 8)
            whole(ps[0], cc("mean"), nSS).then_inc(S("norm_sum"), 1)
            pe.wait_ge(S("norm_rs"), 2)

            def down3(d, freed):
                for pieces in ((0, 1), (2,)):
                    if pieces == (2,):
                        pe.wait_ge(S("u_free1"), freed)
                    for k in range(2):
                        for w, x in ((Dh, Gh), (Dh, Gl), (Dl, Gh)):
                            for g in pieces:
                                t0, n = SPANS[g]
                                ins = nc.tensor.matmul(slot(2)[g], w[:, k, d], x[:, k, t0:t0 + n],
                                                       start=(k == 0 and w is Dh and x is Gh),
                                                       stop=(k == 1 and w is Dl))
                return ins

            def down(i):
                pe.wait_ge(S("d_lo"), i + 1)
                freed = (i * 2 + 3) if not isinstance(i, int) or i < 10 else 22
                for d, s in enumerate(DOWN_SLOTS):
                    before = [e for e in range(d) if DOWN_SLOTS[e] == s or (s, DOWN_SLOTS[e]) == (1, 2)]
                    if before:
                        pe.wait_ge(S("d_added"), i * ADDED[-1] + ADDED[before[-1]])
                    elif s == 0:
                        pe.wait_ge(S("u_free0"), freed)
                    ins = down3(d, freed) if s == 2 else dense3(s, (Dh[:, :, d], Dl[:, :, d]), (Gh, Gl), 2,
                                                                ("g_ready", i * 2) if d == 0 else None)
                    ins.then_inc(S("d_done"), 1)

            def u_round(i):
                first = isinstance(i, int) and i == 0
                for q in range(2):
                    for half in range(2):
                        pe.wait_ge(S("u_lo"), i * 4 + (2 * UP + 2 * q + half + 1))
                        if q == 0:
                            wait_prior(pe, S(f"u_free{half}"), i * 2)
                        elif first:
                            pe.wait_ge(S(f"u_free{half}"), 1)
                        else:
                            last = max(d for d in range(KD) if DOWN_SLOTS[d] == half)
                            pe.wait_ge(S("d_added"), i * ADDED[-1] + (ADDED[last] - ADDED[-1]))
                        dense3(half, (Uh[:, half], Ul[:, half]), (Hh, Fl), KD,
                               ("n2_h", 0) if first and q == half == 0 else None).then_inc(S(f"u_done{half}"), 1)
                    if q == 0 and not first:
                        down(i - 1)
            rounds(pe, 11, u_round)
            down(10)
            pe.wait_ge(S("r_ss"), 15)
            whole(ps[0], cc("mean"), dSS, last=False)
            pe.wait_ge(S("r_sq"), 16)
            whole(ps[0], cc("mean"), dSQ, first=False).then_inc(S("norm_sum"), 1)
            pe.wait_ge(S("norm_rs"), 3)

            pe.wait_ge(S("g_ready"), NF + 1)

            def embedding(i, q):
                pe.wait_ge(S("d_lo"), i * 2 + (NF // 2 + q + 1))
                if q or not isinstance(i, int):
                    pe.wait_ge(S("p_efree"), i * 2 + q)
                dense3(1, (Dh[:, :, q], Dl[:, :, q]), (Gh, Gl), KP).then_inc(S(f"p_done{q}"), 1)

            def p_round(i):
                first = isinstance(i, int)
                for q in range(2):
                    if first and q == 0:
                        embedding(i, q)
                    pe.wait_ge(S("u_lo"), i * 2 + (2 * PLE + q + 1))
                    if q or not first:
                        pe.wait_ge(S("p_gfree"), i * 2 + q)
                    dense3(0, (Uh[:, q], Ul[:, q]), (Hh, Fl), KD, ("n2_h", KD) if first and q == 0 else None)\
                        .then_inc(S("p_gate"), 1)
                    if q or not first:
                        embedding(i, q)
            rounds(pe, 4, p_round)

        @block.scalar
        def _(act):
            link = Link(act, S("act_chain"))

            def rstd(src, dst):
                link(nc.scalar.activation(dst, src, ACT.Ln, bias=epsc))
                return nc.scalar.activation(dst, dst, ACT.Exp, scale=-0.5)

            epsc = small[:, 90:91]
            act.wait_ge(S("consts"), 1)
            for k in range(KD):
                act.wait_ge(S(f"x_in{X_SEMS[k]}"), X_COUNTS[k])
                if k >= 2:
                    act.wait_ge(S("n1_ss"), k - 1)
                nc.scalar.activation(SQ[:, k % 2], xin[:, k, :], ACT.Square).then_inc(S("n1_sq"), 1)
            act.preload_act_table_set("natural_log_exp_and_others")
            for g, (t0, n) in enumerate(SPANS):
                act.wait_ge(S("norm_sum"), g + 1)
                nc.scalar.activation(RS[:, t0:t0 + n], pst[g % 2][:, 0:n], ACT.Ln, bias=epsc).then_inc(S("n1_ln"), 1)
            act.wait_ge(S("n1_ln"), 3)
            nc.scalar.activation(RS, RS, ACT.Exp, scale=-0.5).then_inc(S("norm_rs"), 1)

            act.wait_ge(S("c_abs"), 1)
            nc.scalar.activation(small[:, 4:6], small[:, 2:4], ACT.Exp, scale=-1.0).then_inc(S("c_exp"), 1)

            def z_round(i):
                for s in range(2):
                    act.wait_ge(S(f"z_done{s}"), i + 1)
                    ins = nc.scalar.activation(Z[:, ds(i * 2 + s, 1), :] if not isinstance(i, int) else Z[:, i * 2 + s:i * 2 + s + 1, :],
                                               ps[s][:, 0:T].rearrange("p (o t) -> p o t", o=1), ACT.Copy)
                    ins.then_inc(S(f"z_free{s}"), 1)
            with act.Fori(1, 8) as i:
                z_round(i)

            for i in range(2):
                act.wait_ge(S("cd_done"), 2 * i + 1)
                nc.scalar.activation(cR[:, i], ps[0][:, 0:T], ACT.Sigmoid, bias=pc("b_rg_a", i)).then_inc(S("cd_free"), 1)
                act.wait_ge(S("cd_done"), 2 * i + 2)
                ins = nc.scalar.activation(cI[:, i], ps[1][:, 0:T], ACT.Sigmoid, bias=pc("b_rg_x", i))
                ins.then_inc(S("cd_free"), 1)

            def tokens(t):
                n = P if t < NCH else NS
                act.wait_ge(S("vt_done"), t + 1)
                nc.scalar.activation(VT[0:n, t, :], ps[t % 2][0:n, 0:512], ACT.Copy).then_inc(S("vt_free"), 1)

            tokens(0)
            tokens(1)
            act.wait_ge(S("raw_stored"), 1)
            for i in range(2):
                act.wait_ge(S("cd_done"), 5 + i)
                nc.scalar.activation(Z[:, XD + i, :], ps[i][:, 0:T], ACT.Copy, scale=pc("pool_scale", i))\
                    .then_inc(S("cd_free"), 1)
            act.wait_ge(S("cd_free"), 4)
            act.wait_ge(S("c_lam"), 1)
            for i in range(2):
                if i:
                    act.wait_ge(S("c_scanned"), 1)
                link(nc.scalar.activation(cA, cR[:, i], ACT.Exp, scale=small[:, 20 + i:21 + i]))
                nc.scalar.activation(cB, cA, ACT.Square).then_inc(S("c_a"), 1)
                nc.scalar.activation(cR[:, i], cR[:, i], ACT.Tanh, scale=small[:, 22 + i:23 + i]).then_inc(S("c_a"), 1)
                tokens(2 + 2 * i)
                act.wait_ge(S("c_1ma2"), i + 1)
                nc.scalar.activation(cB, cB, ACT.Sqrt).then_inc(S("c_sqrt"), 1)
                nc.scalar.activation(Z[:, GC + i, :], Z[:, GC + i, :], ACT.Gelu_apprx_tanh).then_inc(S("c_gelu"), 1)
                tokens(3 + 2 * i)
            for t in range(6, NCH + 1):
                tokens(t)

            def gate_out(p):
                act.wait_ge(S("gate_done"), p + 1)
                if p >= 2:
                    act.wait_ge(S(f"gate_stored{p % 2}"), 16 * (p // 2))
                nc.scalar.activation(gstage[:, p % 2], gbank, ACT.Copy).then_inc(S("gate_out"), 1)

            f2, q2, g2 = Z[:, FB:FB + 2, :], Z[:, QB:QB + 2, :], Z[:, GB:GB + 2, :]
            act.wait_ge(S("cd_over"), 1)
            link(nc.scalar.activation(tA, f2, ACT.Abs))
            link(nc.scalar.activation(tA, tA, ACT.Exp, scale=-1.0))
            nc.scalar.activation(tA, tA, ACT.Ln, bias=1.0).then_inc(S("b_act_pre"), 1)
            gate_out(parts("start0")[0])
            act.wait_ge(S("b_dve_pre"), 1)
            nc.scalar.activation(f2, f2, ACT.Sigmoid, scale=-1.0).then_inc(S("b_act_pre"), 1)
            nc.scalar.activation(tA, q2, ACT.Sigmoid).then_inc(S("b_act_pre"), 1)
            gate_out(parts("start0")[1])
            act.wait_ge(S("b_dve_pre"), 2)
            nc.scalar.activation(tA, g2, ACT.Sigmoid).then_inc(S("b_act_pre"), 1)
            gate_out(parts("start0")[2])
            act.wait_ge(S("b_dve_pre"), 3)
            act.preload_act_table_set("natural_log_exp_and_others")
            for i in range(2):
                b = bB[:, i]
                if i == 0:
                    act.wait_ge(S("b_cum"), 2)
                if i:
                    act.wait_ge(S("b_over"), 1)
                nc.scalar.activation(bE, b, ACT.Exp).then_inc(S("b_eb"), 1)
                nc.scalar.activation(bdec[:, 0:8], b[:, CH - 1:SEQ:CH], ACT.Exp).then_inc(S("b_dec"), 1)
                nc.scalar.activation(bdec[:, 8:16], b[:, SEQ + DL - 1:T:DL], ACT.Exp).then_inc(S("b_dec"), 1)
                act.wait_ge(S("b_kdiff"), i + 1)
                nc.scalar.activation(bE, bd_, ACT.Exp, scale=-1.0).then_inc(S("b_kexp"), 1)
                gate_out(parts(f"start{i}")[-2 if i == 0 else 0])
                for g in range(3):
                    act.wait_ge(S("b_tdone"), 3 * i + g + 1)
                    w = min(4, NCH + 1 - 4 * g) * P
                    m = P if g < 2 else NS
                    nc.scalar.activation(kdt[0:m, 4 * g:4 * g + w // P, :].rearrange("p c m -> p (c m)"),
                                         pst[(3 * i + g) % 2][0:m, 0:w], ACT.Copy).then_inc(S("b_tfree"), 1)
                gate_out(parts(f"start{i}")[-1])
                for p in parts(f"states{i}"):
                    gate_out(p)
                for l, m in enumerate(LEVELS):
                    n = len(LEVELS) * i + l
                    nt = T if m <= 2 else SEQ
                    act.wait_ge(S("b_diff"), n + 1)
                    if l == 0:
                        act.wait_ge(S("b_tdone"), 3 * i + 3)
                    dv = bd_[:, 0:nt].rearrange("p (n h m) -> p n h m", h=2, m=m)
                    kv = KF[:, l % 2, 0:nt].rearrange("p (n h m) -> p n h m", h=2, m=m)
                    ev = bE[:, 0:nt].rearrange("p (n h m) -> p n h m", h=2, m=m)
                    nc.scalar.activation(kv[:, :, 0, :], dv[:, :, 0, :], ACT.Exp, scale=-1.0).then_inc(S("b_exps"), 1)
                    nc.scalar.activation(ev[:, :, 1, :], dv[:, :, 1, :], ACT.Exp).then_inc(S("b_exps"), 1)
                    if l in (2, 4, 6):
                        gate_out(parts(f"levels{i}")[l // 2 - 1])
                act.wait_ge(S("b_ofree"), i + 1)
                nc.scalar.activation(bE, bd_, ACT.Square).then_inc(S("b_osq"), 1)
                act.wait_ge(S("b_ms"), i + 1)
                rstd(ps[0][:, 0:T], bE).then_inc(S("b_rs"), 1)

            def a_rs(j):
                act.wait_ge(S("a_ms"), j + 1)
                if j >= 2:
                    act.wait_ge(S("a_normed"), j - 1)
                rstd(ps[j % 2][:, 0:T], beta.rearrange("p a b -> p (a b)")[:, 0:T] if j % 2 == 0 else
                     Pp.rearrange("p a b -> p (a b)")[:, 0:T]).then_inc(S("a_rs"), 1)

            kf_, wf_ = keep.rearrange("p a b -> p (a b)"), wT.rearrange("p a b -> p (a b)")
            order = (KA, KA + 1, QA, QA + 1)
            act.wait_ge(S("b_over"), 2)
            for j in range(4):
                if j >= 2:
                    act.wait_ge(S("a_ms"), j - 1)
                nc.scalar.activation((kf_, wf_)[j % 2][:, 0:T], Z[:, order[j], :], ACT.Square).then_inc(S("a_sq"), 1)
                if j == 0:
                    for p in parts("norms"):
                        gate_out(p)
                if j >= 1:
                    a_rs(j - 1)
            a_rs(3)
            for p in parts("normed"):
                gate_out(p)
            act.wait_ge(S("a_qm"), 1)
            tg = [0]
            for n in range(32):
                tg.append(tg[-1] + (n // 4 + 4) // 4)

            def sticks(n):
                i, h = n // 4, n % 4
                w = (i + 1) * P
                act.wait_ge(S("a_sc"), n + 1)
                if n >= 2:
                    act.wait_ge(S("a_tdone"), tg[n - 1])
                nc.scalar.activation(keep[:, n % 2, 0:w], ps[n % 2][:, 0:w], ACT.Sigmoid,
                                     scale=-HD ** -0.5, bias=negb[:, h:h + 1]).then_inc(S("a_stick"), 1)
                nc.scalar.activation(beta[:, n % 2, 0:w], ps[n % 2][:, 0:w], ACT.Sigmoid,
                                     scale=HD ** -0.5, bias=pc("sb_head", h)).then_inc(S("a_scfree"), 1)

            def turned(n):
                i = n // 4
                for g in range(tg[n], tg[n + 1]):
                    j0 = 4 * (g - tg[n])
                    w = (min(j0 + 4, i + 1) - j0) * P
                    act.wait_ge(S("a_tdone"), g + 1)
                    if n >= 2:
                        act.wait_ge(S("a_pv"), n - 1)
                    nc.scalar.activation(wT[:, n % 2, j0 * P:j0 * P + w], pst[g % 2][:, 0:w], ACT.Copy)\
                        .then_inc(S("a_tfree"), 1)

            for n in range(33):
                if n < 32:
                    sticks(n)
                if n >= 1:
                    turned(n - 1)
                if n < 32 and n % 4 == 1:
                    gate_out(parts("steps")[n // 4])
            for p in parts("samples"):
                gate_out(p)
            act.wait_ge(S("as_sc"), 1)
            act.wait_ge(S("a_tdone"), tg[32])
            nc.scalar.activation(keep[:, 0, 0:PAST + NS], ps[0][:, 0:PAST + NS], ACT.Sigmoid,
                                 scale=-HD ** -0.5, bias=negb[:, 4:5]).then_inc(S("as_stick"), 1)
            nc.scalar.activation(beta[:, 0, 0:PAST + NS], ps[0][:, 0:PAST + NS], ACT.Sigmoid,
                                 scale=HD ** -0.5, bias=pc("sb_row")).then_inc(S("as_stick"), 1)

            def split_high(j):
                if j < KD:
                    if j >= 2:
                        act.wait_ge(S("h_lo"), j - 1)
                    nc.scalar.activation(Ht[:, j % 2], H[:, SPLIT[j]], ACT.Copy).then_inc(S("h_t"), 1)
                if j >= 1:
                    act.wait_ge(S("h_lo"), j)
                    nc.scalar.activation(Hh[:, SPLIT[j - 1]], H[:, SPLIT[j - 1]], ACT.Copy).then_inc(S("h_hi"), 1)
            act.wait_ge(S("a_tdone"), tg[32] + 1)
            act.wait_ge(S("a_pv"), 32)
            nc.scalar.activation(wT[:, 0, 0:PAST], pst[0][:, 0:PAST], ACT.Copy).then_inc(S("a_tfree"), 1)
            nc.scalar.activation(wT[0:NS, 1, 0:P], pst[1][0:NS, 0:P], ACT.Copy).then_inc(S("a_tfree"), 1)

            for j in range(KD + 1):
                split_high(j)

            def late_high(i, v):
                act.wait_ge(S(f"mg_in{v % 2}"), i * (16 * (3 - v % 2)) + 16 * (v // 2 + 1))
                nc.scalar.activation(Uh[:, v % 2], uraw[:, v % 2], ACT.Copy).then_inc(S("m_hi"), 1)

            def m_round(i, last=False):
                for u in range(8):
                    if u < EARLY:
                        act.wait_ge(S(f"early_in{min(u, 1)}"), i * 16 + 16)
                    else:
                        act.wait_ge(S("m_gate"), i * LATE + (u - EARLY + 1))
                    if u >= 2 or not isinstance(i, int) or i:
                        act.wait_ge(S("m_added"), i * 8 + (u - 1))
                    nc.scalar.activation(SIG[:, u % 2], early[:, u] if u < EARLY else ps[0][:, 0:T], ACT.Sigmoid)\
                        .then_inc(S("m_sig"), 1)
                    if EARLY <= u < 6:
                        late_high(i, u - EARLY + 2)
                if not last:
                    for v in range(2):
                        late_high(i + 1, v)
            act.wait_ge(S("a_over"), 2)
            for v in range(2):
                late_high(0, v)
            rounds(act, 3, m_round)
            m_round(3, True)

            def tile_high(r, half):
                act.wait_ge(S(f"uw_in{half}"), r * 16 + 16)
                nc.scalar.activation(Uh[:, half], uraw[:, half], ACT.Copy).then_inc(S("u_hi"), 1)

            tile_high(0, 0)
            for k in range(KD):
                if k == 2:
                    tile_high(0, 1)
                act.wait_ge(S("mix_ready"), k + 1)
                nc.scalar.activation(Hh[:, k], MIX[:, k], ACT.Copy).then_inc(S("h_hi"), 1)

            def o_squares(i):
                for q in range(2):
                    act.wait_ge(S(f"r_done{q}"), i + 1)
                    tile_high(i + 1, q)
                    act.wait_ge(S("r_added"), i * 2 + (q + 1))
                    src = X[:, i * 2 + q:i * 2 + q + 1, :] if isinstance(i, int) else X[:, ds(i * 2 + q, 1), :]
                    wait_prior(act, S("r_ss"), i * 2 + q)
                    nc.scalar.activation(nSQ.rearrange("p (o t) -> p o t", o=1), src, ACT.Square)\
                        .then_inc(S("r_sq"), 1)
            rounds(act, 4, o_squares)
            act.preload_act_table_set("natural_log_exp_and_others")
            act.wait_ge(S("norm_sum"), 4)
            rstd(ps[0][:, 0:T], nRS).then_inc(S("norm_rs"), 1)
            for k in range(KD):
                act.wait_ge(S("split_raw"), k + 1)
                nc.scalar.activation(Hh[:, k], ntmp[:, k % 2], ACT.Copy).then_inc(S("split_hi"), 1)

            act.wait_ge(S("tables_in"), 64)

            def u_round(i, last=False):
                def at(x, q):
                    c = i * 2 + q
                    return x[:, c:c + 1] if isinstance(i, int) else x[:, ds(c, 1)]

                for q in range(2):
                    for half in range(2):
                        act.wait_ge(S(f"u_done{half}"), i * 2 + (q + 1))
                        if half == 0:
                            if q or not isinstance(i, int) or i:
                                act.wait_ge(S("g_ready"), i * 2 + q)
                            fp = small[:, 64:72]
                            link(nc.scalar.activation(fp.rearrange("p (o e) -> p o e", o=1), at(fpar, q), ACT.Copy))
                        src = ps[half][:, 0:T]
                        nc.scalar.activation(V[:, half], src, ACT.Identity, scale=fp[:, 4 * half + 2:4 * half + 3],
                                             bias=fp[:, 4 * half + 3:4 * half + 4]).then_inc(S("u_tap"), 1)
                        fo = at(FO, q)[:, :, half, :]
                        nc.scalar.activation(fo[:, :, 0:2], src[:, SEQ - 2:SEQ].rearrange("p (o e) -> p o e", o=1),
                                             ACT.Copy).then_inc(S(f"u_read{half}"), 1)
                        nc.scalar.activation(
                            fo[:, :, 2:18].rearrange("p o (b e) -> p (o b) e", b=DB),
                            src[:, SEQ:T].rearrange("p (b t) -> p b t", b=DB)[:, :, 2:4], ACT.Copy)\
                            .then_inc(S(f"u_read{half}"), 1)
                        if not (last and q):
                            tile_high(i * 2 + (UP + q + 1), half)
                        if q == 1 and half == 0:
                            act.wait_ge(S("d_in"), i * 16 + 16)
                            wait_prior(act, S("d_done"), i * 8)
                            nc.scalar.activation(Dh, draw, ACT.Copy).then_inc(S("d_hi"), 1)
                    act.wait_ge(S("u_free0"), i * 2 + (q + 1))
                    nc.scalar.activation(V[:, 0], V[:, 0], ACT.Gelu_apprx_tanh).then_inc(S("u_gelu"), 1)
                    act.wait_ge(S("split_raw"), i * 2 + (KD + q + 1))
                    nc.scalar.activation(Gh[:, q], V[:, 0], ACT.Copy).then_inc(S("split_hi"), 1)
            link.rounds(10, u_round)
            u_round(10, True)

            act.preload_act_table_set("natural_log_exp_and_others")
            for q in range(2):
                tile_high(PLE, q)
            for d in range(KD):
                act.wait_ge(S("d_added"), 10 * ADDED[-1] + ADDED[d])
                if d:
                    act.wait_ge(S("r_ss"), 8 + d)
                nc.scalar.activation(dSQ, X[:, d, :], ACT.Square).then_inc(S("r_sq"), 1)
            act.wait_ge(S("d_in"), 16 * (NF // 2 + 1))
            act.wait_ge(S("d_done"), 88)
            for q in range(2):
                nc.scalar.activation(Dh[:, :, q:q + 1], draw[:, :, q:q + 1], ACT.Copy).then_inc(S("d_hi"), 1)
            act.wait_ge(S("pe_in"), 16)
            nc.scalar.activation(Gh, V, ACT.Copy).then_inc(S("h_hi"), 1)
            act.wait_ge(S("norm_sum"), 5)
            rstd(ps[0][:, 0:T], dRS).then_inc(S("norm_rs"), 1)
            for k in range(KD):
                act.wait_ge(S("split_raw"), NF + KD + k + 1)
                nc.scalar.activation(Hh[:, k], ntmp[:, k % 2], ACT.Copy).then_inc(S("split_hi"), 1)

            def p_round(i, last=False):
                for q in range(2):
                    act.wait_ge(S("p_gate"), i * 2 + (q + 1))
                    if not isinstance(i, int) or i:
                        act.wait_ge(S("y_ready"), i * 2 + (q - 1))
                    nc.scalar.activation(sigp[:, q], ps[0][:, 0:T], ACT.Sigmoid).then_inc(S("p_gfree"), 1)
                    if not last:
                        act.wait_ge(S(f"uw_in{q}"), i * 16 + 16 * (PLE + 2))
                        nc.scalar.activation(Uh[:, q], uraw[:, q], ACT.Copy).then_inc(S("u_hi"), 1)
                        act.wait_ge(S(f"p_done{q}"), i + 1)
                        src = draw[:, :, q + 2:q + 3] if isinstance(i, int) else draw[:, :, ds(i * 2 + (q + 2), 1)]
                        nc.scalar.activation(Dh[:, :, q:q + 1], src, ACT.Copy).then_inc(S("d_hi"), 1)
            rounds(act, 3, p_round)
            p_round(3, True)

        @block.vector
        def _(dve):
            v = nc.vector
            link = Link(dve, S("dve_chain"))
            v.memset(small[:, 90:91], EPS).then_inc(S("consts"), 1)
            dve.wait_ge(S("params_in"), 16)
            for k in range(KD):
                dve.wait_ge(S(f"x_in{X_SEMS[k]}"), X_COUNTS[k])
                v.tensor_scalar(H[:, k, :], xin[:, k, :], pc("norm_mix", k), None, ALU.mult).then_inc(S("n1_x"), 1)
                dve.wait_ge(S("n1_sq"), k + 1)
                if k == 0:
                    v.tensor_copy(SS, SQ[:, 0]).then_inc(S("n1_ss"), 1)
                else:
                    dve.wait_ge(S("n1_ss"), k)
                    v.tensor_tensor(SS, SS, SQ[:, k % 2], ALU.add).then_inc(S("n1_ss"), 1)
            link(v.tensor_scalar(small[:, 0:2], pc("lam", 0, 2), -1.0, 0.0, ALU.mult, ALU.max))
            v.scalar_tensor_tensor(small[:, 2:4], small[:, 0:2], 2.0, pc("lam", 0, 2), ALU.mult, ALU.add)\
                .then_inc(S("c_abs"), 1)
            dve.wait_ge(S("norm_rs"), 1)
            dve.wait_ge(S("n1_read"), 1)
            for k in range(KD):
                if k == 3:
                    for s in range(2):
                        dve.wait_ge(S(f"z_done{s}"), 1)
                        v.tensor_tensor(Z[:, s, :], ps[s][:, 0:T], RS, ALU.mult).then_inc(S(f"z_free{s}"), 1)
                v.tensor_tensor(H[:, k, :], H[:, k, :], RS, ALU.mult).then_inc(S("n1_h"), 1)
            dve.wait_ge(S("c_exp"), 1)
            e_, s_, s2, p_ = small[:, 4:6], small[:, 6:8], small[:, 8:10], small[:, 10:12]
            link(v.tensor_scalar(p_, e_, 2.0, None, ALU.add))
            link(v.reciprocal(p_, p_))
            link(v.tensor_tensor(s_, e_, p_, ALU.mult))
            link(v.tensor_tensor(s2, s_, s_, ALU.mult))
            link(v.tensor_scalar(p_, s2, 1.0 / 17, None, ALU.mult))
            for n in range(7, 0, -1):
                link(v.scalar_tensor_tensor(p_, p_, 1.0 / (2 * n + 1), s2, ALU.add, ALU.mult))
            link(v.tensor_scalar(p_, p_, 1.0, 2.0, ALU.add, ALU.mult))
            link(v.tensor_tensor(p_, p_, s_, ALU.mult))
            link(v.tensor_tensor(p_, p_, small[:, 0:2], ALU.add))
            link(v.tensor_scalar(small[:, 20:22], p_, -8.0, None, ALU.mult),
                 v.tensor_scalar(small[:, 22:24], p_, 8.0, None, ALU.mult))
            dve.sem_inc(S("c_lam"), 1)

            dve.wait_ge(S("cd_in"), 64)
            for i in range(2):
                dve.wait_ge(S(f"z_free{i}"), 1)
                x, y = Z[:, XC + i, :], cX[:, i]
                w = [pc("conv_c_w", 2 * j + i) for j in range(4)]
                link(v.tensor_copy(cext[:, :, 0:3], chist[:, i]),
                     v.tensor_copy(cext[:, :, 3:7], x[:, SEQ:T].rearrange("p (b t) -> p b t", b=DB)))
                ys = y[:, SEQ:T].rearrange("p (b t) -> p b t", b=DB)
                link(v.tensor_scalar(y[:, 0:SEQ], x[:, 0:SEQ], w[3], pc("conv_c_b", i), ALU.mult, ALU.add),
                     v.tensor_scalar(ys, cext[:, :, 3:7], w[3], pc("conv_c_b", i), ALU.mult, ALU.add))
                for j in (2, 1, 0):
                    d = 3 - j
                    link(v.scalar_tensor_tensor(y[:, d:SEQ], x[:, 0:SEQ - d], w[j], y[:, d:SEQ], ALU.mult, ALU.add),
                         v.scalar_tensor_tensor(ys, cext[:, :, j:j + 4], w[j], ys, ALU.mult, ALU.add))
                dve.sem_inc(S("cd_ready"), 1)

            for i in range(2):
                dve.wait_ge(S(f"z_free{i}"), XD // 2 + 1)
                x = Z[:, XD + i, :]
                dEs = dE[:, HIST + SEQ:EXT].rearrange("p (b t) -> p b t", b=DB)
                if i == 0:
                    link(v.memset(dE[:, 0:HIST], 0.0))
                dve.wait_ge(S("pool_in"), 16 * (i + 1))
                link(v.tensor_copy(dE[:, HIST:HIST + SEQ], x[:, 0:SEQ]),
                     v.tensor_copy(dEs[:, :, HIST:], x[:, SEQ:T].rearrange("p (b t) -> p b t", b=DB)))
                src, dst = dE, dF
                for w in ((1, 2), (1, 2, 4, 8))[i]:
                    top = w == (2, 8)[i]
                    if top:
                        link(v.tensor_tensor(dst[HD:P, 2 * w - 1:EXT], src[HD:P, 2 * w - 1:EXT],
                                             src[HD:P, w - 1:EXT - w], ALU.add),
                             v.tensor_copy(dst[0:HD, HIST:EXT], src[0:HD, HIST:EXT]))
                    else:
                        link(v.tensor_tensor(dst[:, 2 * w - 1:EXT], src[:, 2 * w - 1:EXT], src[:, w - 1:EXT - w],
                                             ALU.add))
                    src, dst = dst, src
                link(v.tensor_tensor(src[:, HIST:2 * HIST], src[:, HIST:2 * HIST], cc("corr", HIST, i * HIST),
                                     ALU.mult))
                dve.wait_ge(S("raw_stored"), 1)
                ss = src[:, HIST + SEQ:EXT].rearrange("p (b t) -> p b t", b=DB)[:, :, HIST:]
                xs = x[:, SEQ:T].rearrange("p (b t) -> p b t", b=DB)
                link(v.scalar_tensor_tensor(x[:, 0:SEQ], src[:, HIST:HIST + SEQ], cc("invw", 1, i), x[:, 0:SEQ],
                                            ALU.mult, ALU.subtract),
                     v.scalar_tensor_tensor(xs, ss, cc("invw", 1, i), xs, ALU.mult, ALU.subtract))
                dve.sem_inc(S("cd_ready"), 1)

            for i in range(2):
                dve.wait_ge(S("c_a"), 2 * i + 2)
                v.scalar_tensor_tensor(cB, cB, 1.0, cR[:, i], ALU.add, ALU.mult).then_inc(S("c_1ma2"), 1)
                link(v.tensor_tensor(cI[:, i], cI[:, i], cX[:, i], ALU.mult))
                dve.wait_ge(S("c_sqrt"), i + 1)
                link(v.tensor_tensor(cI[:, i], cI[:, i], cB, ALU.mult))
                a0, u0 = cA[:, SEQ:T:DL], cI[:, i, SEQ:T:DL]
                link(v.tensor_tensor(small[:, 24:32], a0, ch0[:, i], ALU.mult))
                link(v.tensor_tensor(u0, u0, small[:, 24:32], ALU.add), v.memset(a0, 0.0))
                link(v.tensor_tensor_scan(cX[:, i], cA, cI[:, i], 0.0, ALU.mult, ALU.add))
                link(v.tensor_copy(small[:, 40 + i:41 + i], cX[:, i, SEQ - 1:SEQ]),
                     v.tensor_copy(small[:, 48 + 8 * i:56 + 8 * i], cX[:, i, SEQ + DL - 1:T:DL]))
                dve.sem_inc(S("c_scanned"), 1)
                dve.wait_ge(S("c_gelu"), i + 1)
                v.tensor_tensor(Z[:, GC + i, :], Z[:, GC + i, :], cX[:, i], ALU.mult).then_inc(S("c_out"), 1)
            dve.wait_ge(S("c_out"), 2)
            dve.wait_ge(S("cd_free"), 6)
            dve.wait_ge(S("vt_free"), NCH + 1)
            dve.sem_inc(S("cd_over"), 1)

            f2, q2, g2 = Z[:, FB:FB + 2, :], Z[:, QB:QB + 2, :], Z[:, GB:GB + 2, :]
            link(v.memset(rmask, 1.0))
            link(v.memset(rmask[:, 0:SEQ:CH], 0.0), v.memset(rmask[:, SEQ:T:DL], 0.0))
            for buf in (KF, QF[0], QF[1], att, atts[0:NS]):
                link(v.memset(buf, 0.0))
            dve.wait_ge(S("b_act_pre"), 1)
            link(v.scalar_tensor_tensor(bB, f2, 0.0, tA, ALU.min, ALU.subtract))
            dve.sem_inc(S("b_dve_pre"), 1)
            for i in range(2):
                v.tensor_tensor_scan(bB[:, i], rmask, bB[:, i], 0.0, ALU.mult, ALU.add).then_inc(S("b_cum"), 1)
            dve.wait_ge(S("b_act_pre"), 3)
            v.tensor_tensor(q2, q2, tA, ALU.mult).then_inc(S("b_dve_pre"), 1)
            dve.wait_ge(S("b_act_pre"), 4)
            v.tensor_tensor(g2, g2, tA, ALU.mult).then_inc(S("b_dve_pre"), 1)
            dve.wait_ge(S("b_dve_pre"), 2)
            dve.wait_ge(S("b_dve_pre"), 3)
            dve.wait_ge(S("b_cum"), 2)
            dve.wait_ge(S("tables_in"), 64)
            dve.wait_ge(S("b_act_pre"), 2)
            for i in range(2):
                b, kk, qq, gg = bB[:, i], Z[:, FB + i, :], Z[:, QB + i, :], Z[:, GB + i, :]
                bp, bs = b[:, 0:SEQ].rearrange("p (c t) -> p c t", c=NCH), b[:, SEQ:T].rearrange("p (c t) -> p c t", c=DB)
                dp = bd_[:, 0:SEQ].rearrange("p (c t) -> p c t", c=NCH)
                dss = bd_[:, SEQ:T].rearrange("p (c t) -> p c t", c=DB)
                dve.wait_ge(S("b_eb"), i + 1)
                link(v.tensor_tensor(QE, qq, bE, ALU.mult))
                link(v.tensor_tensor(dp, bp, bp[:, :, CH - 1:CH].to_broadcast([P, NCH, CH]), ALU.subtract),
                     v.tensor_tensor(dss, bs, bs[:, :, DL - 1:DL].to_broadcast([P, DB, DL]), ALU.subtract))
                dve.sem_inc(S("b_kdiff"), 1)
                if i:
                    dve.wait_ge(S("states_stored"), 1)
                for bb in range(DB):
                    ins = v.tensor_scalar(vbd[0:NS, bb, :], VT[0:NS, NCH, HW + i * P:HW + i * P + P],
                                          cc("batch", 1, bb, NS), None, ALU.mult)
                    link(ins)
                dve.sem_inc(S("b_vbd"), 1)
                dve.wait_ge(S("b_kexp"), i + 1)
                v.tensor_tensor(bE, bE, kk, ALU.mult).then_inc(S("b_kd"), 1)
                dve.wait_ge(S("b_u"), i + 1)
                dve.wait_ge(S("b_dec"), 2 * i + 2)
                UBp = bd_[:, 0:NCH * P].rearrange("p (c m) -> p c m", c=NCH)
                bdb = cc("bd").rearrange("p (o m) -> p o m", o=1).to_broadcast([P, NCH, P])
                up = ps[0][:, 0:SEQ].rearrange("p (c m) -> p c m", c=NCH)
                us_ = ps[1][:, 0:SEQ].rearrange("p (c m) -> p c m", c=NCH)
                v.tensor_tensor(UBp, up, bdb, ALU.mult).then_inc(S("b_ufree"), 1)
                dve.wait_ge(S("b_ufree"), 2 * i + 1)
                link(v.tensor_copy(Sall[:, 1, :], UBp[:, 0, :]))
                for c in range(1, NCH):
                    link(v.scalar_tensor_tensor(Sall[:, c + 1, :], Sall[:, c, :], bdec[:, c:c + 1], UBp[:, c, :],
                                                ALU.mult, ALU.add))
                v.tensor_tensor(UBp, us_, bdb, ALU.mult).then_inc(S("b_ufree"), 1)
                dve.wait_ge(S("b_ufree"), 2 * i + 2)
                dve.wait_ge(S("s0_in"), 16)
                for bb in range(DB):
                    link(v.scalar_tensor_tensor(vbd[:, bb, :], S0[:, i, bb, :], bdec[:, 8 + bb:9 + bb],
                                                UBp[:, bb, :], ALU.mult, ALU.add))
                dve.sem_inc(S("b_states"), 1)

                def differences(l, m):
                    if l:
                        dve.wait_ge(S("b_exps"), 2 * (len(LEVELS) * i + l))
                    nt = T if m <= 2 else SEQ
                    bv = b[:, 0:nt].rearrange("p (n w) -> p n w", w=2 * m)
                    dv = bd_[:, 0:nt].rearrange("p (n w) -> p n w", w=2 * m)
                    if l >= 2:
                        dve.wait_ge(S("b_adone"), 4 * (NL * i + l - 1))
                    if l >= 7:
                        dve.wait_ge(S("b_sdone"), 3 * i + l - 6)
                    v.tensor_tensor(dv, bv, bv[:, :, m - 1:m].to_broadcast([P, nt // (2 * m), 2 * m]), ALU.subtract)\
                        .then_inc(S("b_diff"), 1)

                def factors(l, m):
                    nt = T if m <= 2 else SEQ
                    dve.wait_ge(S("b_exps"), 2 * (len(LEVELS) * i + l + 1))

                    def halves(x):
                        return x[:, 0:nt].rearrange("p (n h m) -> p n h m", h=2, m=m)
                    kv = halves(KF[:, l % 2])[:, :, 0, :]
                    link(v.tensor_tensor(kv, kv, halves(kk)[:, :, 0, :], ALU.mult),
                         *[v.tensor_tensor(halves(QF[hh][hh * HD:hh * HD + HD, l % 2])[:, :, 1, :],
                                           halves(qq[hh * HD:hh * HD + HD])[:, :, 1, :],
                                           halves(bE[hh * HD:hh * HD + HD])[:, :, 1, :], ALU.mult) for hh in range(2)])
                    dve.sem_inc(S("b_factors"), 1)

                def select(l):
                    n = NL * i + l
                    for g in range(4):
                        dve.wait_ge(S("b_adone"), 4 * n + g + 1)
                        bank = ps[g // 2][:, (g % 2) * 512:(g % 2) * 512 + 512].rearrange("p (a m) -> p a m", a=4)
                        v.copy_predicated(att[:, 2 * g:2 * g + 2].rearrange("p c h m -> p (c h) m"),
                                          masks[:, l:l + 1, :].to_broadcast([P, 4, P]), bank).then_inc(S("b_afree"), 1)
                    if l >= 5:
                        dve.wait_ge(S("b_sdone"), 3 * i + l - 4)
                        v.copy_predicated(atts[0:NS], smasks[:, l - 5:l - 4, :].to_broadcast([NS, 2, NS]),
                                          pst[0][0:NS, 0:2 * NS].rearrange("p (h t) -> p h t", h=2))\
                            .then_inc(S("b_sfree"), 1)

                for l in range(NL + 1):
                    if l < NL - 1:
                        differences(l, LEVELS[l])
                    if l >= 1:
                        select(l - 1)
                    if l < NL - 1:
                        factors(l, LEVELS[l])
                    elif l == NL - 1:
                        dve.wait_ge(S("b_adone"), 4 * (NL * i + l - 1))
                        dve.wait_ge(S("b_sdone"), 3 * i + 1)
                        link(*[v.tensor_copy(QF[hh][hh * HD:hh * HD + HD, l % 2], qq[hh * HD:hh * HD + HD])
                               for hh in range(2)])
                        dve.sem_inc(S("b_factors"), 1)
                dve.wait_ge(S("b_odone"), i + 1)
                dve.wait_ge(S("b_exps"), 2 * len(LEVELS) * (i + 1))
                head_rows = [slice(hh * HD, hh * HD + HD) for hh in range(2)]
                link(*[v.tensor_copy(bd_[head_rows[hh], g * 256:g * 256 + 256],
                                     ps[g // 2][head_rows[hh], (g % 2) * 512 + hh * 256:(g % 2) * 512 + hh * 256 + 256])
                       for hh in range(2) for g in range(4)])
                dve.wait_ge(S("b_osdone"), i + 1)
                link(*[v.tensor_copy(bd_[head_rows[hh], SEQ:T], pst[1][head_rows[hh], hh * NS:hh * NS + NS])
                       for hh in range(2)])
                dve.sem_inc(S("b_ofree"), 1)
                link(v.tensor_tensor(gg, gg, bd_, ALU.mult))
                dve.wait_ge(S("b_rs"), i + 1)
                dve.wait_ge(S("states_stored"), i + 1)
                link(v.scalar_tensor_tensor(gg, gg, pc("hgrn_norm"), bE, ALU.mult, ALU.mult))
                dve.sem_inc(S("b_over"), 1)

            link(v.tensor_scalar(negb[:, 0:NH + 1], par[:, PAR["sb_head"]:PAR["sb_head"] + NH + 1], -1.0, None,
                                 ALU.mult), v.memset(QS, 0.0), v.memset(qm, 0.0))
            rs = (beta.rearrange("p a b -> p (a b)")[:, 0:T], Pp.rearrange("p a b -> p (a b)")[:, 0:T])
            for j in range(4):
                dve.wait_ge(S("a_rs"), j + 1)
                if j < 2:
                    link(v.scalar_tensor_tensor(Z[:, KA + j, :], Z[:, KA + j, :], pc("k_norm"), rs[j % 2], ALU.mult,
                                                ALU.mult))
                else:
                    for hh in range(2):
                        rows = slice(hh * HD, hh * HD + HD)
                        link(v.scalar_tensor_tensor(qm[rows, 2 * (j - 2) + hh, :], Z[rows, QA + j - 2, :],
                                                    pc("q_norm")[rows], rs[j % 2][rows], ALU.mult, ALU.mult))
                dve.sem_inc(S("a_normed"), 1)
            for h in range(NH):
                rows = slice((h % 2) * HD, (h % 2) * HD + HD)
                src = qm[rows, h, SEQ:T].rearrange("p (b t) -> p b t", b=DB)
                link(v.tensor_copy(QS[rows, h // 2, :].rearrange("p (b c) -> p b c", c=144)[:, :, 4 * h:4 * h + 4],
                                   src))
            for i in range(2):
                link(v.memset(QSall[:, i], 0.0))
                for hh in range(2):
                    h = 2 * i + hh
                    rows = slice(hh * HD, hh * HD + HD)
                    link(v.tensor_copy(QSall[rows, i, :].rearrange("p (b c) -> p b c", c=16)[:, :, 4 * h:4 * h + 4],
                                       qm[rows, h, SEQ:T].rearrange("p (b t) -> p b t", b=DB)))
            dve.sem_inc(S("a_qs"), 1)
            for s in range(2):
                link(v.memset(Pp[:, s, :], 1.0))
            dve.sem_inc(S("a_qm"), 1)

            def broken(s, w, d0, dn, yes, no):
                link(v.tensor_tensor(beta[:, s, d0:d0 + dn], beta[:, s, d0:d0 + dn], yes, ALU.mult),
                     v.tensor_tensor(keep[:, s, d0:d0 + dn], keep[:, s, d0:d0 + dn], no, ALU.max))
                if w < SEQ:
                    link(v.memset(Pp[:, s, w:w + 1], 1.0))
                link(v.tensor_tensor_scan(Pp[:, s, 0:w][:, ::-1], keep[:, s, 0:w][:, ::-1], keep[:, s, 0:w][:, ::-1],
                                          1.0, ALU.mult, ALU.bypass))
                return v.tensor_tensor(beta[:, s, 0:w], beta[:, s, 0:w], Pp[:, s, 1:w + 1], ALU.mult)

            def heads_out(i):
                dve.wait_ge(S("a_pv"), 4 * i + 4)
                link(*[v.tensor_copy(Z[(h % 2) * HD:(h % 2) * HD + HD, QA + h // 2, i * P:i * P + P],
                                     ps[0][(h % 2) * HD:(h % 2) * HD + HD, 1024 + h * P:1024 + h * P + P])
                       for h in range(NH)])
                dve.sem_inc(S("a_ofree"), 1)

            for n in range(32):
                i = n // 4
                dve.wait_ge(S("a_stick"), n + 1)
                dve.wait_ge(S("a_scfree"), n + 1)
                if n:
                    dve.wait_ge(S("a_w"), n)
                broken(n % 2, (i + 1) * P, i * P, P, cc("strict"), cc("notstrict")).then_inc(S("a_w"), 1)
                if n % 4 == 1 and i >= 1:
                    heads_out(i - 1)
            heads_out(7)
            dve.wait_ge(S("as_stick"), 2)
            broken(0, PAST + NS, PAST, NS, cc("newkeys", NS), cc("notnewkeys", NS)).then_inc(S("as_w"), 1)

            def split_low(j):
                dve.wait_ge(S("h_t"), j + 1)
                v.tensor_tensor(Hl[:, SPLIT[j]], H[:, SPLIT[j]], Ht[:, j % 2].bitcast(F32), ALU.subtract)\
                    .then_inc(S("h_lo"), 1)
            for j in range(KD):
                if j >= 4:
                    dve.wait_ge(S("vp_used"), SPLIT[j] + 2)
                split_low(j)
            dve.wait_ge(S("vp_used"), DB)
            for h in range(NH):
                rows = slice((h % 2) * HD, (h % 2) * HD + HD)
                link(v.tensor_copy(Z[rows, QA + h // 2, SEQ:T].rearrange("p (b t) -> p b t", b=DB),
                                   ps[1][rows, (h // 2) * P:(h // 2) * P + P].rearrange(
                                       "p (b c) -> p b c", c=16)[:, :, 4 * h:4 * h + 4]))
            dve.sem_inc(S("a_over"), 2)

            def mixed_low(k):
                dve.wait_ge(S("h_hi"), KD + k + 1)
                v.tensor_tensor(Ml[:, k], MIX[:, k], Hh[:, k].bitcast(F32), ALU.subtract).then_inc(S("h_lo"), 1)

            def m_round(i, last=False):
                for q in range(2):
                    for n in range(4):
                        u = 4 * q + n
                        if last and u == 7:
                            for k in range(2):
                                mixed_low(k)
                        dve.wait_ge(S("m_sig"), i * 8 + (u + 1))
                        dve.wait_ge(S("m_proj"), i * 8 + (u + 1))
                        sig = SIG[:, u % 2]
                        v.tensor_tensor(ACC if n == 0 else sig, sig, ps[m_slot(u)][:, 0:T], ALU.mult)\
                            .then_inc(S("m_pfree"), 1)
                        dve.wait_ge(S("m_pfree"), i * 8 + (u + 1))
                        if n == 0:
                            dve.sem_inc(S("m_added"), 1)
                        elif n < 3:
                            v.tensor_tensor(ACC, ACC, sig, ALU.add).then_inc(S("m_added"), 1)
                            dve.wait_ge(S("m_added"), i * 8 + (u + 1))
                        else:
                            c = i * 2 + q
                            dst = MIX[:, c:c + 1, :] if isinstance(i, int) else MIX[:, ds(c, 1), :]
                            v.tensor_tensor(dst, ACC.rearrange("p (o t) -> p o t", o=1),
                                            sig.rearrange("p (o t) -> p o t", o=1), ALU.add)\
                                .then_inc(S("m_added"), 1)
                            dve.wait_ge(S("m_added"), i * 8 + (u + 1))
                            dve.sem_inc(S("mix_ready"), 1)
            rounds(dve, 3, m_round)
            m_round(3, True)

            for k in range(2, KD):
                mixed_low(k)

            link(v.memset(nSS, 0.0))

            def o_round(i):
                for q in range(2):
                    c = i * 2 + q
                    x = X[:, c:c + 1, :] if isinstance(i, int) else X[:, ds(c, 1), :]
                    dve.wait_ge(S(f"x_in{q}"), i * 16 + 32)
                    dve.wait_ge(S(f"r_done{q}"), i + 1)
                    v.tensor_tensor(x, x, ps[q][:, 0:T].rearrange("p (o t) -> p o t", o=1), ALU.add)\
                        .then_inc(S("r_added"), 1)
                    dve.wait_ge(S("r_sq"), i * 2 + (q + 1))
                    v.tensor_tensor(nSS, nSS, nSQ, ALU.add).then_inc(S("r_ss"), 1)
                    dve.wait_ge(S("r_ss"), i * 2 + (q + 1))
            rounds(dve, 4, o_round)
            dve.wait_ge(S("norm_rs"), 2)

            def normed(scale, rs, chunks, splits):
                def raw(k):
                    if k >= 2:
                        dve.wait_ge(S("n2_h"), chunks + k - 1)
                    v.scalar_tensor_tensor(ntmp[:, k % 2], X[:, k, :], pc(scale, k), rs, ALU.mult, ALU.mult)\
                        .then_inc(S("split_raw"), 1)

                raw(0)
                for k in range(KD):
                    if k < KD - 1:
                        raw(k + 1)
                    dve.wait_ge(S("split_hi"), splits + k + 1)
                    v.tensor_tensor(Fl[:, k], ntmp[:, k % 2], Hh[:, k].bitcast(F32), ALU.subtract)\
                        .then_inc(S("n2_h"), 1)

            normed("norm_ffn", nRS, 0, 0)

            def add_down(d):
                s = DOWN_SLOTS[d]
                pieces = zip(SPANS, slot(s)) if s == 2 else [((0, T), ps[s][:, 0:T])]
                for (t0, n), src in pieces:
                    v.tensor_tensor(X[:, d, t0:t0 + n], X[:, d, t0:t0 + n], src, ALU.add).then_inc(S("d_added"), 1)

            dve.wait_ge(S("tables_in"), 64)

            def u_round(i):
                for q in range(2):
                    c = i * 2 + q
                    fp = small[:, 64:72]
                    for half in range(2):
                        dve.wait_ge(S("u_tap"), i * 4 + (2 * q + half + 1))
                        dve.wait_ge(S(f"u_read{half}"), i * 4 + (2 * q + 2))
                        y, x = V[:, half], ps[half][:, 0:T]
                        w0, w1 = fp[:, 4 * half:4 * half + 1], fp[:, 4 * half + 1:4 * half + 2]
                        ys = y[:, SEQ:T].rearrange("p (b t) -> p b t", b=DB)
                        xs = x[:, SEQ:T].rearrange("p (b t) -> p b t", b=DB)
                        fh = (FH[:, c, half] if isinstance(i, int) else
                              FH[:, ds(c, 1), half].rearrange("p o b t -> p (o b) t"))
                        link(v.scalar_tensor_tensor(y[:, 1:SEQ], x[:, 0:SEQ - 1], w1, y[:, 1:SEQ], ALU.mult, ALU.add),
                             v.scalar_tensor_tensor(ys[:, :, 1:], xs[:, :, 0:3], w1, ys[:, :, 1:], ALU.mult, ALU.add),
                             v.scalar_tensor_tensor(ys[:, :, 0:1], fh[:, :, 1:2], w1, ys[:, :, 0:1], ALU.mult,
                                                    ALU.add))
                        link(v.scalar_tensor_tensor(y[:, 2:SEQ], x[:, 0:SEQ - 2], w0, y[:, 2:SEQ], ALU.mult, ALU.add),
                             v.scalar_tensor_tensor(ys[:, :, 2:], xs[:, :, 0:2], w0, ys[:, :, 2:], ALU.mult, ALU.add),
                             v.scalar_tensor_tensor(ys[:, :, 0:2], fh, w0, ys[:, :, 0:2], ALU.mult, ALU.add))
                        dve.sem_inc(S(f"u_free{half}"), 1)
                    if q == 0 and not isinstance(i, int):
                        for d in range(KD):
                            dve.wait_ge(S("d_done"), i * 8 + (d - 7))
                            add_down(d)
                    dve.wait_ge(S("u_gelu"), i * 2 + (q + 1))
                    v.tensor_tensor(V[:, 0], V[:, 0], V[:, 1], ALU.mult).then_inc(S("split_raw"), 1)
                    dve.wait_ge(S("split_hi"), i * 2 + (KD + q + 1))
                    v.tensor_tensor(Gl[:, q], V[:, 0], Gh[:, q].bitcast(F32), ALU.subtract)\
                        .then_inc(S("g_ready"), 1)
            link.rounds(11, u_round)

            link(v.memset(dSS, 0.0))
            for d in range(KD):
                dve.wait_ge(S("d_done"), 80 + d + 1)
                add_down(d)
                if d < KD - 1:
                    dve.wait_ge(S("r_sq"), 8 + d + 1)
                    if d:
                        dve.wait_ge(S("r_ss"), 8 + d)
                    v.tensor_tensor(dSS, dSS, dSQ, ALU.add).then_inc(S("r_ss"), 1)
            dve.wait_ge(S("norm_rs"), 3)
            normed("norm_ple", dRS, KD, NF + KD)

            def p_round(i):
                for q in range(2):
                    c = i * 2 + q
                    dve.wait_ge(S("p_gfree"), i * 2 + (q + 1))
                    dve.wait_ge(S(f"p_done{q}"), i + 1)
                    v.tensor_tensor(sigp[:, q], sigp[:, q], ps[1][:, 0:T], ALU.mult).then_inc(S("p_efree"), 1)
                    dve.wait_ge(S("p_efree"), i * 2 + (q + 1))
                    wait_prior(dve, S(f"y_out{q}"), i * 16)
                    x = X[:, c:c + 1, :] if isinstance(i, int) else X[:, ds(c, 1), :]
                    v.tensor_tensor(yout[:, q:q + 1, :], x, sigp[:, q:q + 1, :], ALU.add).then_inc(S("y_ready"), 1)
            rounds(dve, 4, p_round)

        @block.gpsimd
        def _(pool):
            for i in range(2):
                if i:
                    pool.wait_ge(S("cd_ready"), 3)
                pool.dma_start(dE[:, HIST + SEQ:EXT].rearrange("p (b t) -> p b t", b=DB)[:, :, 0:HIST],
                                   a["phist"][i]).then_inc(S("pool_in"), 16)

            pool.wait_ge(S("cd_ready"), 4)
            for s in range(2):
                pool.dma_start(gw[:, s], a["wge"][s]).then_inc(S(f"gw_in{s}"), 16)

            def gates_out(i, more):
                for s in range(2):
                    for part in range(3):
                        m = 3 * s + part
                        pool.wait_ge(S("gate_out"), i * 6 + (m + 1))
                        pool.dma_start(gates[ds(i * 2 + s, 1), :, part * PART:part * PART + PART].rearrange(
                            "o p t -> (o p) t"), gstage[:, m % 2]).then_inc(S(f"gate_stored{m % 2}"), 16)
                    if more:
                        pool.dma_start(gw[:, s], a["wge"][ds(i * 2 + (s + 2), 1)].rearrange("o p k m -> (o p) k m"))\
                            .then_inc(S(f"gw_in{s}"), 16)
            rounds(pool, UNITS // 2 - 1, lambda i: gates_out(i, True))
            gates_out(UNITS // 2 - 1, False)

            def late_low(n, v):
                pool.wait_ge(S("m_hi"), n)
                nc.gpsimd.tensor_tensor(Ul[:, v % 2], uraw[:, v % 2], Uh[:, v % 2].bitcast(F32), ALU.subtract)\
                    .then_inc(S("m_lo"), 1)

            def late_round(i):
                for v in range(LATE):
                    late_low(i * LATE + (v + 1), v)
            rounds(pool, 4, late_round)

            def tile_low(r, half):
                pool.wait_ge(S("u_hi"), r * 2 + (half + 1))
                nc.gpsimd.tensor_tensor(Ul[:, half], uraw[:, half], Uh[:, half].bitcast(F32), ALU.subtract)\
                    .then_inc(S("u_lo"), 1)

            def o_low(i):
                for half in range(2):
                    tile_low(i, half)
            rounds(pool, UP + 1, o_low)

            def w_round(i, last=False):
                for half in range(2):
                    tile_low(i * 2 + (UP + 1), half)
                if not last:
                    tile_low(i * 2 + (UP + 2), 0)
                pool.wait_ge(S("d_hi"), i + 1)
                nc.gpsimd.tensor_tensor(Dl, draw, Dh.bitcast(F32), ALU.subtract).then_inc(S("d_lo"), 1)
                if not last:
                    tile_low(i * 2 + (UP + 2), 1)
            rounds(pool, 10, w_round)
            w_round(10, True)

            def p_low(i):
                for q in range(2):
                    tile_low(i + PLE, q)
                    pool.wait_ge(S("d_hi"), i * 2 + (NF // 2 + q + 1))
                    src = draw[:, :, q:q + 1] if isinstance(i, int) else draw[:, :, ds(i * 2 + q, 1)]
                    nc.gpsimd.tensor_tensor(Dl[:, :, q:q + 1], src, Dh[:, :, q:q + 1].bitcast(F32), ALU.subtract)\
                        .then_inc(S("d_lo"), 1)
                if isinstance(i, int):
                    pool.wait_ge(S("h_hi"), 2 * KD + 1)
                    nc.gpsimd.tensor_tensor(Gl, V, Gh.bitcast(F32), ALU.subtract).then_inc(S("g_ready"), 1)

            def y_round(i):
                for q in range(2):
                    pool.wait_ge(S("y_ready"), i * 2 + (q + 1))
                    dst = (o["y"][i * 2 + q] if isinstance(i, int) else
                           o["y"][ds(i * 2 + q, 1)].rearrange("o p t -> (o p) t"))
                    pool.dma_start(dst, yout[:, q]).then_inc(S(f"y_out{q}"), 16)
            p_low(0)
            with pool.Fori(1, 4) as i:
                p_low(i)
                y_round(i - 1)
            y_round(3)


_OUTS = [("y", (KD, P, T)), ("k_cm", (P, 2, T)), ("v_p", (P, NCH, HW)), ("v_s", (NS, HW)),
         ("hgrn_p", (2, P, P)), ("hgrn_s", (2, P, DB, P)), ("h_p", (P, 2)), ("h_s", (P, 2, DB)),
         ("convc_p", (P, 2, 3)), ("convc_s", (2, P, DB, 3)), ("pool_p", (P, 2, HIST)), ("pool_s", (2, P, DB, HIST)),
         ("ffn_out", (P, NF, 2, 18))]


def constants():
    con = np.zeros((P, NCON), np.float32)

    def put(name, x):
        con[:x.shape[0], CON[name]:CON[name] + x.shape[1]] = x
    i = np.arange(P)
    head = i // HD
    put("ident", np.eye(P))
    put("mean", np.full((P, P), 1.0 / D))
    put("headmean", (head[:, None] == head[None]) / HD)
    put("bd", head[:, None] == head[None])
    put("strict", i[None] < i[:, None])
    put("notstrict", i[None] >= i[:, None])
    j = np.arange(NS)
    new = (i[:, None] // 16 == j[None] // DL) & (j[None] % DL < i[:, None] % DL)
    put("newkeys", new)
    put("notnewkeys", ~new)
    win = np.array([[2, 8], [4, 16]])[head]
    put("invw", 1.0 / win)
    t = np.arange(HIST)
    for k in range(2):
        con[:, CON["corr"] + k * HIST:CON["corr"] + (k + 1) * HIST] = \
            win[:, k:k + 1] / np.minimum(t[None] + 1, win[:, k:k + 1])
    put("batch", j[:, None] // DL == np.arange(DB)[None])
    masks = np.zeros((P, NL, P), np.int32)
    s, t = i[:, None], i[None]
    for n, m in enumerate(LEVELS):
        masks[:, n] = (s // (2 * m) == t // (2 * m)) & (s % (2 * m) < m) & (t % (2 * m) >= m)
    masks[:, NL - 1] = s == t
    return con, masks, np.ascontiguousarray(masks[:NS, 5:8, :NS])


def kernel(**inputs):
    import concourse.bacc as bacc
    from concourse.bass_utils import run_bass_kernel_spmd

    x = {k: np.asarray(v) for k, v in inputs.items()}

    def tokens(p, s):
        y = np.concatenate([p.reshape(SEQ, -1), s.reshape(NS, -1)], 0).T
        return y.reshape(-1, P, T)

    def weights(w):
        k, m = w.shape
        return w.reshape(k // P, P, m // P, P).transpose(2, 1, 0, 3)

    def cols(w):
        return w.reshape(-1, P).T

    w_in = x["w_in"][0]
    wz = np.concatenate([w_in[:, c:c + 256] for c in Z_COLS], 1)
    wg = w_in[:, 2560:].reshape(KD, P, 4, 4, 2, P).transpose(3, 1, 4, 2, 0, 5).reshape(4, P, 8, KD, P)
    wb = x["w_branch"][0].reshape(4, 2, P, KD, P).transpose(3, 2, 0, 1, 4)
    wvi = np.concatenate([w_in[:, 512:768], w_in[:, 1280:1536]], 1).reshape(KD, P, 512).transpose(1, 0, 2)

    def blockdiag(w):
        y = np.zeros((P, 2, P), w.dtype)
        for h in range(4):
            r = (h % 2) * HD
            y[r:r + HD, h // 2, r:r + HD] = w[h]
        return y

    wrg = np.stack([blockdiag(x["w_rg_a"][0]), blockdiag(x["w_rg_x"][0])], 2)
    par = np.zeros((P, NPAR), np.float32)

    def put(name, v):
        par[:, PAR[name]:PAR[name] + v.shape[1]] = v
    for name in ("norm_mix", "norm_ffn", "norm_ple", "conv_c_b", "b_rg_a", "b_rg_x", "lam", "pool_scale"):
        put(name, cols(x[name][0]))
    put("conv_c_w", cols(x["conv_c_w"][0]))
    for name in ("q_norm", "k_norm", "hgrn_norm"):
        put(name, np.tile(x[name][0], 2)[:, None])
    put("sb_head", np.broadcast_to(x["sb_bias"][0], (P, NH)))
    put("sb_row", x["sb_bias"][0][(np.arange(P) % 16) // 4][:, None])
    cw = x["conv_f_w"][0].reshape(3, 2, NF, P)
    fpar = np.concatenate([cw, x["conv_f_b"][0].reshape(1, 2, NF, P)], 0).transpose(3, 2, 1, 0).reshape(P, NF, 8)
    fhist = x["state_ffn_conv"][0].reshape(DB, 2, 2, NF, P).transpose(4, 3, 2, 0, 1)
    s0 = np.zeros((P, 2, DB, P), np.float32)
    for h in range(4):
        r = (h % 2) * HD
        s0[r:r + HD, h // 2, :, r:r + HD] = x["state_hgrn"][0][:, h].transpose(1, 0, 2)
    con, masks, smasks = constants()
    arrays = {
        "x": tokens(x["x_prompt"], x["x_sample"]),
        "wz": weights(wz), "wge": wg[:, :, 0:EARLY].transpose(0, 2, 1, 3, 4).reshape(UNITS, P, KD, P),
        "wgl": wg[:, :, EARLY:].transpose(0, 2, 1, 3, 4), "wb": wb, "wvi": wvi, "wrg": wrg, "wpool": blockdiag(x["w_pool"][0]),
        "wo": weights(x["w_out"][0]),
        "wu": x["w_up"][0].reshape(KD, P, 2, NF, P).transpose(3, 1, 2, 0, 4),
        "wd": x["w_down"][0].reshape(NF // 2, 2, P, KD, P).transpose(0, 2, 1, 3, 4),
        "wpg": weights(x["w_ple_gate"][0]), "wpl": x["w_ple"][0].reshape(KP, P, KD, P).transpose(1, 0, 2, 3),
        "pe": tokens(x["p_prompt"][0], x["p_sample"][0]).transpose(1, 0, 2),
        "par": par, "fpar": fpar, "fhist": fhist, "con": con, "masks": masks, "smasks": smasks,
        "chist": x["state_rglru_conv"][0].reshape(DB, 3, 2, P).transpose(3, 2, 0, 1),
        "ch0": x["state_rglru_h"][0].reshape(DB, 2, P).transpose(2, 1, 0),
        "phist": x["state_pool"][0].reshape(DB, HIST, 2, P).transpose(2, 3, 0, 1),
        "s0": s0,
        "ck": x["cache_k"][0].reshape(-1, P, 2, P).transpose(0, 3, 2, 1),
        "cv": x["cache_v"][0].reshape(-1, P, HW),
        "pt": x["page_table"],
    }
    nc = bacc.Bacc("TRN2", target_bir_lowering=False, num_devices=1)
    arrays = {f"in_{k}": np.ascontiguousarray(v) for k, v in arrays.items()}
    ins = {k[3:]: nc.dram_tensor(k, v.shape, mybir.dt.from_np(v.dtype), kind="ExternalInput").ap()
           for k, v in arrays.items()}
    outs = {n: nc.dram_tensor(f"out_{n}", s, F32, kind="ExternalOutput").ap() for n, s in _OUTS}
    program(nc, ins, outs)
    got = run_bass_kernel_spmd(nc, [arrays], core_ids=[0]).results[0]
    g = {n: np.asarray(got[f"out_{n}"]) for n, _ in _OUTS}

    y = g["y"].reshape(D, T).T
    k = g["k_cm"].transpose(2, 1, 0).reshape(T, NH, HD)

    def heads(s):
        return [s[h // 2][(h % 2) * HD:(h % 2) * HD + HD, ..., (h % 2) * HD:(h % 2) * HD + HD] for h in range(4)]

    fo = g["ffn_out"].transpose(3, 2, 1, 0).reshape(18, 2 * FF)
    c = np.ascontiguousarray
    return (c(y[:SEQ].reshape(1, SEQ, D)), c(y[SEQ:].reshape(DB, DL, D)),
            c(k[:SEQ].reshape(1, 1, SEQ, NH, HD)),
            c(g["v_p"].transpose(1, 0, 2).reshape(1, 1, SEQ, NH, HD)),
            c(k[SEQ:].reshape(1, DB, DL, NH, HD)), c(g["v_s"].reshape(1, DB, DL, NH, HD)),
            c(np.stack(heads(g["hgrn_p"]))[None, None]),
            c(np.stack(heads(g["hgrn_s"])).transpose(2, 0, 1, 3)[None]),
            c(g["h_p"].T.reshape(1, 1, HW)), c(g["h_s"].transpose(2, 1, 0).reshape(1, DB, HW)),
            c(g["convc_p"].transpose(2, 1, 0).reshape(1, 1, 3, HW)),
            c(g["convc_s"].transpose(2, 3, 0, 1).reshape(1, DB, 3, HW)),
            c(g["pool_p"].transpose(2, 1, 0).reshape(1, 1, HIST, HW)),
            c(g["pool_s"].transpose(2, 3, 0, 1).reshape(1, DB, HIST, HW)),
            c(fo[:2].reshape(1, 1, 2, 2 * FF)), c(fo[2:].reshape(1, DB, 2, 2 * FF)))
```
